# Optimizing a Trainium2 kernel written in Bass

```python
import math
import jax, jax.numpy as jnp
from jax import lax
import numpy as np

D_MODEL = 1024
BATCH = 1
SEQ = 256
DEPTH = 1
DEC_BATCH = 8
DEC_SEQ = 4
PAST_LEN = 2048
PAGE_SIZE = 128

GLA_HEADS = 4
GLA_DK = D_MODEL // 8
GLA_DV = D_MODEL // 4
GLA_QK = GLA_HEADS * GLA_DK
GLA_VW = GLA_HEADS * GLA_DV
GLA_GATE_RANK = 16
GLA_TAU = 16.0
GLA_CHUNK = 64
GDN_HEADS = 8
GDN_DK = D_MODEL // 8
GDN_DV = D_MODEL // 8
GDN_QK = GDN_HEADS * GDN_DK
GDN_VW = GDN_HEADS * GDN_DV
GDN_CONV = 4
GDN_CONV_DIM = 2 * GDN_QK + GDN_VW
GDN_CHUNK = 64
IN_SPLITS = (GLA_QK, GLA_QK, GLA_VW, GLA_VW, GLA_GATE_RANK,
             GDN_CONV_DIM, GDN_VW, GDN_HEADS, GDN_HEADS, D_MODEL, D_MODEL)
D_IN = 2 * GLA_QK + 2 * GLA_VW + GLA_GATE_RANK + GDN_CONV_DIM + GDN_VW + 2 * GDN_HEADS + 2 * D_MODEL
N_GROUPS = 4
EXPERTS_PER_GROUP = 4
D_EXPERT = D_MODEL // 2
TOP_K = 2
N_MOD = 6
NORM_EPS = 1e-6
L2_EPS = 1e-6

kernel_name = 'hybrid_gla_gdn_hmoe_adaln_step'

def _rms_norm(x, w):
    xf = x.astype(jnp.float32)
    y = xf * lax.rsqrt(jnp.mean(xf * xf, axis=-1, keepdims=True) + NORM_EPS)
    return (y * w.astype(jnp.float32)).astype(x.dtype)

def _l2norm(x):
    return x * lax.rsqrt(jnp.sum(x * x, axis=-1, keepdims=True) + L2_EPS)

def _split(x, sizes):
    out, off = [], 0
    for s in sizes:
        out.append(x[..., off:off + s])
        off += s
    return out

def _to_chunks(x, C):
    B, T, H = x.shape[:3]
    x = x.reshape((B, T // C, C, H) + x.shape[3:])
    return x.transpose((1, 0, 3, 2) + tuple(range(4, x.ndim)))

def _from_chunks(o):
    N, B, H, C, d = o.shape
    return o.transpose(1, 0, 3, 2, 4).reshape(B, N * C, H, d)

def _gla_chunked(q, k, v, log_a, S0):
    C = math.gcd(q.shape[1], GLA_CHUNK)
    causal = jnp.tril(jnp.ones((C, C), dtype=bool))

    def step(S, inp):
        qc, kc, vc, gc = inp
        b = jnp.cumsum(gc, axis=2)
        diff = b[:, :, :, None, :] - b[:, :, None, :, :]
        dec = jnp.exp(jnp.where(causal[:, :, None], diff, -jnp.inf))
        A = jnp.einsum('bhtd,bhsd,bhtsd->bhts', qc, kc, dec)
        o = (jnp.einsum('bhtd,bhdv->bhtv', qc * jnp.exp(b), S)
             + jnp.einsum('bhts,bhsv->bhtv', A, vc))
        b_last = b[:, :, -1:, :]
        S = (jnp.exp(b_last[:, :, 0, :, None]) * S
             + jnp.einsum('bhsd,bhsv->bhdv', kc * jnp.exp(b_last - b), vc))
        return S, o

    S, o = lax.scan(step, S0, (_to_chunks(q, C), _to_chunks(k, C), _to_chunks(v, C), _to_chunks(log_a, C)))
    return _from_chunks(o), S

def _gdn_chunked(q, k, v, log_g, beta, S0):
    C = math.gcd(q.shape[1], GDN_CHUNK)
    dv = v.shape[-1]
    incl = jnp.tril(jnp.ones((C, C), dtype=bool))
    strict = jnp.tril(jnp.ones((C, C), dtype=bool), k=-1)

    def step(S, inp):
        qc, kc, vc, gc, bc = inp
        b = jnp.cumsum(gc, axis=-1)
        diff = b[..., :, None] - b[..., None, :]
        dec = jnp.exp(jnp.where(incl, diff, -jnp.inf))
        kb = kc * bc[..., None]
        L = jnp.where(strict, jnp.einsum('bhtd,bhsd->bhts', kb, kc) * dec, 0.0)
        rhs = jnp.concatenate([vc * bc[..., None], kb * jnp.exp(b)[..., None]], axis=-1)
        X = lax.linalg.triangular_solve(L, rhs, left_side=True, lower=True, unit_diagonal=True)
        u, w = X[..., :dv], X[..., dv:]
        v_new = u - jnp.einsum('bhtd,bhdv->bhtv', w, S)
        attn = jnp.einsum('bhtd,bhsd->bhts', qc, kc) * dec
        o = (jnp.einsum('bhtd,bhdv->bhtv', qc * jnp.exp(b)[..., None], S)
             + jnp.einsum('bhts,bhsv->bhtv', attn, v_new))
        b_last = b[..., -1:]
        S = (jnp.exp(b_last)[..., None] * S
             + jnp.einsum('bhsd,bhsv->bhdv', kc * jnp.exp(b_last - b)[..., None], v_new))
        return S, o

    S, o = lax.scan(step, S0, (_to_chunks(q, C), _to_chunks(k, C), _to_chunks(v, C),
                               _to_chunks(log_g, C), _to_chunks(beta, C)))
    return _from_chunks(o), S

def _causal_conv(x, buf, w):
    T = x.shape[1]
    xp = jnp.concatenate([buf.astype(x.dtype), x], axis=1)
    y = xp[:, 0:T] * w[0]
    for j in range(1, GDN_CONV):
        y = y + xp[:, j:j + T] * w[j]
    return jax.nn.silu(y), xp[:, -(GDN_CONV - 1):]

def _mixer(h, S_gla, S_gdn, conv_buf, w_in, w_gla_a2, b_gla_a, gla_norm_w, w_conv,
           gdn_A_log, gdn_dt_bias, gdn_norm_w, w_out):
    f32 = jnp.float32
    B, T, _ = h.shape
    proj = h @ w_in
    qa, ka, va, ga, ra, qkv_b, zb, beta_raw, a_raw, gate_a, gate_b = _split(proj, IN_SPLITS)
    q = qa.reshape(B, T, GLA_HEADS, GLA_DK).astype(f32) * GLA_DK ** -0.5
    k = ka.reshape(B, T, GLA_HEADS, GLA_DK).astype(f32)
    v = va.reshape(B, T, GLA_HEADS, GLA_DV).astype(f32)
    log_a = jax.nn.log_sigmoid((ra @ w_gla_a2 + b_gla_a).astype(f32)) / GLA_TAU
    log_a = log_a.reshape(B, T, GLA_HEADS, GLA_DK)
    o, S_gla = _gla_chunked(q, k, v, log_a, S_gla.astype(f32))
    o_a = _rms_norm(o, gla_norm_w).reshape(B, T, GLA_VW) * jax.nn.silu(ga.astype(f32))
    qkv, conv_buf = _causal_conv(qkv_b, conv_buf, w_conv)
    qb, kb, vb = _split(qkv, (GDN_QK, GDN_QK, GDN_VW))
    q = _l2norm(qb.reshape(B, T, GDN_HEADS, GDN_DK).astype(f32)) * GDN_DK ** -0.5
    k = _l2norm(kb.reshape(B, T, GDN_HEADS, GDN_DK).astype(f32))
    v = vb.reshape(B, T, GDN_HEADS, GDN_DV).astype(f32)
    beta = jax.nn.sigmoid(beta_raw.astype(f32))
    log_g = -jnp.exp(gdn_A_log.astype(f32)) * jax.nn.softplus(a_raw.astype(f32) + gdn_dt_bias.astype(f32))
    o, S_gdn = _gdn_chunked(q, k, v, log_g, beta, S_gdn.astype(f32))
    o_b = _rms_norm(o, gdn_norm_w).reshape(B, T, GDN_VW) * jax.nn.silu(zb.astype(f32))
    merged = jax.nn.sigmoid(gate_a.astype(f32)) * o_a + jax.nn.sigmoid(gate_b.astype(f32)) * o_b
    return merged.astype(h.dtype) @ w_out, S_gla, S_gdn, conv_buf

def _moe(h, w_gr, b_gr, w_er, b_er, w_g, w_u, w_d):
    f32 = jnp.float32
    B, T, D = h.shape
    M = B * T
    hf = h.reshape(M, D)
    gp = jax.nn.softmax((hf @ w_gr).astype(f32) + b_gr.astype(f32), axis=-1)
    g_w, g_idx = lax.top_k(gp, 1)
    el = ((hf @ w_er).astype(f32) + b_er.astype(f32)).reshape(M, N_GROUPS, EXPERTS_PER_GROUP)
    el = jnp.take_along_axis(el, g_idx[:, :, None], axis=1)[:, 0]
    e_w, e_idx = lax.top_k(jax.nn.softmax(el, axis=-1), TOP_K)
    e_w = e_w / jnp.sum(e_w, axis=-1, keepdims=True)
    within = jnp.einsum('mk,mke->me', e_w, jax.nn.one_hot(e_idx, EXPERTS_PER_GROUP, dtype=f32))
    comb = ((jax.nn.one_hot(g_idx[:, 0], N_GROUPS, dtype=f32) * g_w)[:, :, None]
            * within[:, None, :]).astype(h.dtype)
    out = jnp.zeros_like(hf)
    for g in range(N_GROUPS):
        a = jnp.einsum('md,edf->mef', hf, w_g[g])
        u = jnp.einsum('md,edf->mef', hf, w_u[g])
        hid = jax.nn.silu(a) * u * comb[:, g, :, None]
        out = out + jnp.einsum('mef,efd->md', hid, w_d[g])
    return out.reshape(B, T, D)

def _trunk(x, c, st_gla, st_gdn, st_conv, params):
    (w_ada, b_ada, norm1_w, w_in, w_gla_a2, b_gla_a, gla_norm_w, w_conv, gdn_A_log, gdn_dt_bias,
     gdn_norm_w, w_out, norm2_w, w_group_router, b_group_router, w_expert_router, b_expert_router,
     w_exp_gate, w_exp_up, w_exp_down, final_norm_w) = params
    new_gla, new_gdn, new_conv = [], [], []
    cs = jax.nn.silu(c)
    for l in range(DEPTH):
        mod = (cs @ w_ada[l] + b_ada[l]).reshape(c.shape[0], N_MOD, D_MODEL)[:, :, None, :]
        shift1, scale1, gate1, shift2, scale2, gate2 = [mod[:, i] for i in range(N_MOD)]
        h = _rms_norm(x, norm1_w[l]) * (1 + scale1) + shift1
        y, sg, sd, cb = _mixer(h, st_gla[l], st_gdn[l], st_conv[l], w_in[l], w_gla_a2[l], b_gla_a[l],
                               gla_norm_w[l], w_conv[l], gdn_A_log[l], gdn_dt_bias[l], gdn_norm_w[l], w_out[l])
        x = x + gate1 * y
        h = _rms_norm(x, norm2_w[l]) * (1 + scale2) + shift2
        x = x + gate2 * _moe(h, w_group_router[l], b_group_router[l], w_expert_router[l],
                             b_expert_router[l], w_exp_gate[l], w_exp_up[l], w_exp_down[l])
        new_gla.append(sg)
        new_gdn.append(sd)
        new_conv.append(cb)
    return _rms_norm(x, final_norm_w), jnp.stack(new_gla), jnp.stack(new_gdn), jnp.stack(new_conv)

def setup_inputs(seed: int = 0) -> dict:
    key = jax.random.key(seed)
    ks = jax.random.split(key, 32)
    f32 = jnp.float32

    def nrm(k, shape, scale):
        return jax.random.normal(k, shape, f32) * scale

    L, D, G, E, F = DEPTH, D_MODEL, N_GROUPS, EXPERTS_PER_GROUP, D_EXPERT
    dt = jnp.exp(jax.random.uniform(ks[10], (L, GDN_HEADS), f32) * (math.log(0.1) - math.log(0.001)) + math.log(0.001))
    return {
        'x_prompt': nrm(ks[0], (BATCH, SEQ, D), 1.0),
        'x_sample': nrm(ks[1], (DEC_BATCH, DEC_SEQ, D), 1.0),
        'c_prompt': nrm(ks[2], (BATCH, D), 1.0),
        'c_sample': nrm(ks[3], (DEC_BATCH, D), 1.0),
        'state_gla': nrm(ks[4], (L, DEC_BATCH, GLA_HEADS, GLA_DK, GLA_DV), 0.5),
        'state_gdn': nrm(ks[5], (L, DEC_BATCH, GDN_HEADS, GDN_DK, GDN_DV), 0.1),
        'state_conv': nrm(ks[6], (L, DEC_BATCH, GDN_CONV - 1, GDN_CONV_DIM), 1.0),
        'w_ada': nrm(ks[7], (L, D, N_MOD * D), 0.5 * D ** -0.5),
        'b_ada': nrm(ks[8], (L, N_MOD * D), 0.02),
        'norm1_w': 1.0 + nrm(ks[9], (L, D), 0.02),
        'w_in': nrm(ks[11], (L, D, D_IN), D ** -0.5),
        'w_gla_a2': nrm(ks[12], (L, GLA_GATE_RANK, GLA_QK), GLA_GATE_RANK ** -0.5),
        'b_gla_a': nrm(ks[13], (L, GLA_QK), 0.1),
        'gla_norm_w': 1.0 + nrm(ks[14], (L, GLA_DV), 0.02),
        'w_conv': nrm(ks[15], (L, GDN_CONV, GDN_CONV_DIM), GDN_CONV ** -0.5),
        'gdn_A_log': jnp.log(jax.random.uniform(ks[16], (L, GDN_HEADS), f32, 1.0, 16.0)),
        'gdn_dt_bias': dt + jnp.log(-jnp.expm1(-dt)),
        'gdn_norm_w': 1.0 + nrm(ks[17], (L, GDN_DV), 0.02),
        'w_out': nrm(ks[18], (L, D, D), D ** -0.5),
        'norm2_w': 1.0 + nrm(ks[19], (L, D), 0.02),
        'w_group_router': nrm(ks[20], (L, D, G), D ** -0.5),
        'b_group_router': nrm(ks[21], (L, G), 0.01),
        'w_expert_router': nrm(ks[22], (L, D, G * E), D ** -0.5),
        'b_expert_router': nrm(ks[23], (L, G * E), 0.01),
        'w_exp_gate': nrm(ks[24], (L, G, E, D, F), D ** -0.5),
        'w_exp_up': nrm(ks[25], (L, G, E, D, F), D ** -0.5),
        'w_exp_down': nrm(ks[26], (L, G, E, F, D), F ** -0.5),
        'final_norm_w': 1.0 + nrm(ks[27], (D,), 0.02),
    }

def reference(x_prompt, x_sample, c_prompt, c_sample, state_gla, state_gdn, state_conv,
              w_ada, b_ada, norm1_w, w_in, w_gla_a2, b_gla_a, gla_norm_w, w_conv, gdn_A_log,
              gdn_dt_bias, gdn_norm_w, w_out, norm2_w, w_group_router, b_group_router,
              w_expert_router, b_expert_router, w_exp_gate, w_exp_up, w_exp_down, final_norm_w):
    params = (w_ada, b_ada, norm1_w, w_in, w_gla_a2, b_gla_a, gla_norm_w, w_conv, gdn_A_log,
              gdn_dt_bias, gdn_norm_w, w_out, norm2_w, w_group_router, b_group_router,
              w_expert_router, b_expert_router, w_exp_gate, w_exp_up, w_exp_down, final_norm_w)
    Bp = x_prompt.shape[0]
    zero_gla = jnp.zeros((DEPTH, Bp, GLA_HEADS, GLA_DK, GLA_DV), jnp.float32)
    zero_gdn = jnp.zeros((DEPTH, Bp, GDN_HEADS, GDN_DK, GDN_DV), jnp.float32)
    zero_conv = jnp.zeros((DEPTH, Bp, GDN_CONV - 1, GDN_CONV_DIM), x_prompt.dtype)
    y_prompt, gla_p, gdn_p, conv_p = _trunk(x_prompt, c_prompt, zero_gla, zero_gdn, zero_conv, params)
    y_sample, gla_s, gdn_s, conv_s = _trunk(x_sample, c_sample, state_gla, state_gdn, state_conv, params)
    return (y_prompt, y_sample,
            gla_p.astype(state_gla.dtype), gdn_p.astype(state_gdn.dtype), conv_p.astype(state_conv.dtype),
            gla_s.astype(state_gla.dtype), gdn_s.astype(state_gdn.dtype), conv_s.astype(state_conv.dtype))


_drawn_inputs = setup_inputs


def setup_inputs(seed=0):
    import zlib

    import numpy as np

    out = dict(_drawn_inputs(seed))
    spreads = {}
    factors = {'gla_norm_w': 8.0,
     'gdn_norm_w': 5.889,
     'norm2_w': 5.565,
     'b_group_router': 8.0,
     'b_expert_router': 41.023,
     'final_norm_w': 9.549}
    for name, (base, spread) in spreads.items():
        noise = np.random.default_rng([zlib.crc32(name.encode()), seed]).standard_normal(out[name].shape)
        drawn = base * np.exp(spread * noise) if base else spread * noise
        out[name] = __import__('jax').numpy.asarray(drawn.astype(out[name].dtype))
    for name, factor in factors.items():
        out[name] = (out[name] * factor).astype(out[name].dtype)
    return out
```

```python
from contextlib import ExitStack

import numpy as np

import concourse.bass as bass
import concourse.mybir as mybir

F32 = mybir.dt.float32
ALU = mybir.AluOpType
ACT = mybir.ActivationFunctionType
AX = mybir.AxisListType.X

P = 128
D = 1024
KD = D // P
SEQ, NSEQ, DT = 256, 8, 4
TOK = SEQ + NSEQ * DT
NC9 = 1 + NSEQ
TILES = ((0, 128), (128, 128), (256, 32))
HA, DKA, DVA = 4, 128, 256
HB, DKB, DVB = 8, 128, 128
RANK = 16
TAU = 16.0
TAPS = 4
NG, EPG = 4, 4
NE = NG * EPG
DE = 512
EPS = 1e-6
CONV0 = 3088
CT = 24
XPW = 3 + SEQ + NSEQ * (3 + DT)
YW = XPW - 3
SAMP0 = 3 + SEQ
LEVELS = 7

PROJ = ([("qa", i, 128 * i) for i in range(4)] + [("ka", i, 512 + 128 * i) for i in range(4)]
        + [("va", i, 1024 + 128 * i) for i in range(8)]
        + [("cv", i, CONV0 + 128 * i) for i in range(CT)]
        + [("ga", i, 2048 + 128 * i) for i in range(8)]
        + [("gsa", i, 7200 + 128 * i) for i in range(8)]
        + [("zb", i, 6160 + 128 * i) for i in range(8)]
        + [("gsb", i, 8224 + 128 * i) for i in range(8)])
NPROJ = len(PROJ)
CW = 256
RING = 5

VEC = {"b_ada": (0, 48), "norm1": (48, 8), "norm2": (56, 8), "final": (64, 8), "gla_norm": (72, 2),
       "gdn_norm": (74, 1)}
NVEC = 75


def constants():
    p = np.arange(P)
    parts = {"ident": np.eye(P), "ones": np.ones((P, P)), "tri": (p[:, None] <= p[None, :]) * 1.0}
    for lv in range(LEVELS):
        b = 1 << lv
        s, t = p[:, None], p[None, :]
        parts[f"level{lv}"] = ((s // (2 * b) == t // (2 * b)) & (s % (2 * b) < b) & (t % (2 * b) >= b)) * 1.0
    q = np.arange(32)
    same = (q[:, None] // DT == q[None, :] // DT)
    pad = lambda a: np.concatenate([a, np.zeros((P - a.shape[0], a.shape[1]))])
    parts["tri_s"] = pad(same & (q[:, None] <= q[None, :]))
    parts["same_s"] = pad(same)
    parts["seq"] = pad(q[:, None] // DT == np.arange(NSEQ)[None, :])
    parts["eps"] = np.full((P, 1), EPS)
    parts["lnq"] = np.full((P, 1), np.log(DKB ** -0.5))
    parts["iota"] = np.tile(np.arange(4.0)[None, :], (P, 1))
    off, at = 0, {}
    for k, a in parts.items():
        at[k] = (off, a.shape[1])
        off += a.shape[1]
    return np.concatenate([np.asarray(a, np.float32) for a in parts.values()], axis=1), at


CONST, CONST_AT = constants()


class Signals:

    def __init__(self, nc, ctx, counts):
        self.nc, self.ctx, self.counts = nc, ctx, counts
        self.sems, self.value, self.marks = {}, {}, {}

    def sem(self, kind):
        if kind not in self.sems:
            self.sems[kind] = self.ctx.enter_context(self.nc.semaphore(kind))
            self.value[kind] = 0
        return self.sems[kind]

    def mark(self, kind, *events, by=1):
        sem = self.sem(kind)
        self.value[kind] += by
        for event in events:
            assert event not in self.marks, event
            self.marks[event] = (kind, self.value[kind])
        return sem

    def when(self, event):
        kind, value = ("first_building", 1) if self.counts is None else self.counts[event]
        return self.sem(kind), value



def program(nc, ins, outs, known=None):
    ctx = ExitStack()
    with ctx:
        return _program(nc, ctx, ins, outs, known)


def _program(nc, ctx, I, O, known):
    S = Signals(nc, ctx, known)
    mark, when = S.mark, S.when

    ARENA = 53200
    arena = ctx.enter_context(nc.sbuf_tensor("arena", [P, ARENA], F32))
    top = [0]

    def carve(*shape, at=None):
        n = int(np.prod(shape))
        o = top[0] if at is None else at
        if at is None:
            top[0] += n
        assert o + n <= ARENA, (o, n)
        v = arena[:, o:o + n]
        if len(shape) == 2:
            v = v.rearrange("p (a b) -> p a b", b=shape[1])
        elif len(shape) == 3:
            v = v.rearrange("p (a b c) -> p a b c", b=shape[1], c=shape[2])
        return v

    xT = carve(KD, TOK)
    hT = carve(KD, TOK)
    modT = carve(48, NC9)
    A1, A2 = carve(KD, NC9), carve(KD, NC9)
    csT = carve(KD, NC9)
    vecT = carve(NVEC)
    cst = carve(CONST.shape[1])
    rsB = carve(TOK)
    rtw = carve(KD, 20)
    rtb = carve(20)
    gs = carve(2, 32)
    persistent = top[0]

    def const(name):
        o, n = CONST_AT[name]
        return cst[:, o:o + n]

    ident, ones, tri = const("ident"), const("ones"), const("tri")
    TRI = (tri, tri, const("tri_s"))
    LAST = (ones, ones, const("same_s"))

    W = carve(RING, KD, CW)
    QKA = carve(KD, TOK)
    vA_at = top[0]
    vA = carve(3, D)
    qB, kB = carve(KD, TOK), carve(KD, TOK)
    vB_at = top[0]
    vB = carve(3, D)
    GA_at = top[0]
    GA = carve(KD, TOK)
    GB_at = top[0]
    GB = carve(KD, TOK)
    convT = carve(96)
    cbT = carve(CT, 24)
    ccT = carve(CT, 27)
    wsm = carve(KD, 32)
    raT = carve(TOK)
    wa2 = carve(512)
    ba = carve(3, 16)
    beta = carve(3, HB)
    gB = carve(3, HB)
    gt = carve(3, HB)
    adt = carve(2, HB)
    bcum = carve(3, HB)
    blast = carve(3, HB)
    ebB, elB, eSd = carve(3, HB), carve(3, HB), carve(3, HB)
    gseq = carve(NSEQ, HB)
    eSs = carve(NSEQ, HB)
    xp = carve(2, XPW)
    yb = carve(4, YW)
    sgm = carve(4, YW)
    sqb = carve(2, TOK)
    rsb = carve(2, TOK)
    SA = carve(HA, DVA)
    SB = carve(HB, DVB)
    ebl = carve(HA, NSEQ)
    ssum = carve(HB)
    srs = carve(HB)
    oSt = carve(KD, 32)
    oSt2 = carve(KD, 32)
    work = top[0]
    E = carve(HB, P)
    AT = carve(HB, P)
    LT = carve(HB, P)
    Lm = carve(HB, P)
    Y = carve(HB, P)
    X_at = top[0]
    X = carve(HB, 2, P)
    R = carve(HB, P)
    tg = carve(HB, P, at=X_at)
    kem2 = carve(2, D, at=X_at)
    ke = LT
    gA = carve(HA, P, at=work)
    Eb = carve(HA, P, at=work + 512)
    Ep = carve(HA, P, at=work + 1024)
    Em = carve(HA, P, at=work + 1536)
    El = carve(HA, P, at=work + 2048)
    ATa = carve(HA, P, at=work + 2560)
    keTa = carve(HA, P, at=work + 3072)
    oNa = carve(D, at=work + 3584)
    kem1 = carve(2, 512, at=work + 4608)
    oNb = Y.rearrange("p a b -> p (a b)")
    sqo = Lm
    xr = vB
    cbrow = carve(3072, at=vA_at)
    crow = carve(D, at=GB_at)
    csx = carve(2, D, at=GA_at)
    vrow = carve(P, at=GB_at + 1024)
    cvrow = carve(P, at=GB_at + 1152)
    newconv = carve(3072, at=vA_at)
    n0 = persistent
    EW = carve(8, 4096, at=n0)
    n1 = n0 + 8 * 4096
    acc = carve(KD, TOK, at=n1)
    hid = carve(4, TOK, at=n1 + KD * TOK)
    sg2 = carve(4, TOK, at=n1 + KD * TOK + 4 * TOK)
    combT = carve(TOK, at=n1 + KD * TOK + 8 * TOK)
    cmb = carve(2, TOK, at=n1 + KD * TOK + 9 * TOK)
    cmbB = carve(2, TOK, at=n1 + KD * TOK + 11 * TOK)
    r0 = n1 + KD * TOK + 13 * TOK
    rt = carve(3, 20, at=r0)
    rs_ = {}
    for i, n in enumerate(["gmax", "gden", "gw", "hit", "idx", "gsel", "el", "emax", "p1", "h1", "p2", "within",
                           "tmp", "i1", "w1", "w2", "dd", "hh"]):
        rs_[n] = carve(3, 4, at=r0 + 60 + 12 * i)
    el16 = carve(3, 16, at=r0 + 60 + 12 * 18)
    comb = carve(3, 16, at=r0 + 60 + 12 * 18 + 48)
    yrow = carve(3, D, at=persistent)

    pm = [ctx.enter_context(nc.psum_tensor(f"bank{i}", [P, 512], F32)) for i in range(8)]

    T, V, A, G = nc.tensor, nc.vector, nc.scalar, nc.gpsimd
    block = ctx.enter_context(nc.Block())

    def cols(w, c0, n=CW):
        return w[:, c0:c0 + n].rearrange("(k p) n -> p k n", p=P)

    chunks = []
    chunk_of = {}

    def add(name, src):
        chunk_of[name] = len(chunks)
        chunks.append((name, src))

    def slot(name):
        return W[:, chunk_of[name] % RING]

    def loaded(name):
        return f"chunk {chunk_of[name]}"

    def used(name):
        return f"used {chunk_of[name]}"

    GLA_AT = {23: 0, 29: 1, 37: 2}
    GDN_AT = {47: 0, 57: 1, 67: 2}
    schedule = [("head",)] + [("ada", c) for c in range(8)] + [("norm", 1), ("small",)]
    for s in range(NPROJ + 6):
        schedule.append(("step", s))
        if s in GLA_AT:
            schedule.append(("gla", GLA_AT[s]))
        if s in GDN_AT:
            schedule.append(("gdn", GDN_AT[s]))
    schedule += [("conv_out",)] + [("ada", c) for c in range(8, 24)]
    schedule += [("merge",), ("wout",), ("norm", 2), ("router",), ("experts",), ("final",)]

    for item in schedule:
        kind, c = item[0], item[-1]
        if kind == "ada":
            add(("ada", c), cols(I["w_ada"], CW * c))
        elif kind == "step" and c % 2 == 0 and c < NPROJ:
            add(("win", c), cols(I["w_in"], PROJ[c][2]))
        elif item == ("gla", 2):
            for i in range(4):
                add(("sgla", i), I["state_gla"][2 * i:2 * i + 2].rearrange("s h k v -> k (s h) v"))
        elif item == ("gdn", 2):
            for i in range(4):
                add(("sgdn", i), I["state_gdn"][2 * i:2 * i + 2].rearrange("s (h a) k v -> k (s h) a v", a=2))
        elif kind == "wout":
            for i in range(4):
                add(("wout", i), cols(I["w_out"], CW * i))

    ring_names = []

    def ring_bank(name):
        n = len(ring_names)
        if n >= 4:
            PE[0].wait_ge(*when(f"read {ring_names[n - 4]}"))
        ring_names.append(name)
        banks[name] = n % 4
        return pm[n % 4]

    banks = {} if known is None else known["#banks"]
    if known is None:
        S.marks["#banks"] = banks
    PE = [None]
    free = {}

    def take(b, reader):
        if b in free:
            PE[0].wait_ge(*when(free[b]))
        free[b] = reader
        return pm[b]

    def rb(name):
        return pm[banks.get(name, 0)]

    def mm(out, lhsT, rhs, start=True, stop=True):
        return T.matmul(out, lhsT, rhs, start=start, stop=stop)

    def tr(out, in_, n):
        return T.transpose(out, in_, ident[0:n, 0:n])

    def bc(ap, n):
        return ap.unsqueeze(2).to_broadcast([ap.shape[0], ap.shape[1], n])

    def mid(ap, n):
        return ap.unsqueeze(1).to_broadcast([ap.shape[0], n, ap.shape[1]])

    def y_free(s):
        kind = PROJ[s][0] if s >= 0 else None
        if kind in ("qa", "ka", None):
            return []
        return [f"tr{s} ready"] if kind == "va" else [f"act{s}", f"ln{s}"]

    def sg_free(s):
        kind = PROJ[s][0] if s >= 0 else None
        if kind in ("qa", "ka", "va", None):
            return []
        return [f"act{s}"] + ([f"tr{s} ready"] if kind == "cv" and PROJ[s][1] >= 16 else [])

    def run(fns):
        for item in schedule:
            f = fns.get(item[0])
            if f is not None:
                f(*item[1:])

    @block.tensor
    def _(pe):
        PE[0] = pe

        def head():
            pe.wait_ge(*when("consts"))
            pe.wait_ge(*when("vec rows"))
            b = ring_bank("vec")
            tr(b[:, 0:NVEC], vrow[0:NVEC, :], NVEC)
            tr(b[:, 128:224], cvrow[0:96, :], 96).then_inc(mark("head_transposed", "vec ready"), 1)
            pe.wait_ge(*when("x rows"))
            for d in range(KD):
                b = ring_bank(f"x{d}")
                for m, (o, n) in enumerate(TILES):
                    last = tr(b[:, o:o + n], xr[0:n, m, 128 * d:128 * d + 128], n)
                last.then_inc(mark("head_transposed", f"x{d} ready"), 1)
            pe.wait_ge(*when("cb rows"))
            for g in range(2):
                b = ring_bank(f"cb{g}")
                for j in range(12):
                    c = 12 * g + j
                    last = tr(b[:, 24 * j:24 * j + 24], cbrow[0:24, 128 * c:128 * c + 128], 24)
                last.then_inc(mark("head_transposed", f"cb{g} ready"), 1)
            b = ring_bank("c")
            for k in range(KD):
                last = tr(b[:, NC9 * k:NC9 * k + NC9], crow[0:NC9, 128 * k:128 * k + 128], NC9)
            last.then_inc(mark("head_transposed", "c ready"), 1)

        def ada(c):
            pe.wait_ge(*when(loaded(("ada", c))))
            pe.wait_ge(*when("read c"))
            w = slot(("ada", c))
            b = ring_bank(f"ada{c}")
            for j in range(2):
                for k in range(KD):
                    last = mm(b[:, NC9 * j:NC9 * j + NC9], w[:, k, 128 * j:128 * j + 128], csT[:, k, :],
                              k == 0, k == KD - 1)
            last.then_inc(mark("ada_products", f"ada{c} ready", used(("ada", c))), 1)

        def norm(i):
            b = ring_bank(f"norm{i}")
            for d in range(KD):
                pe.wait_ge(*when(f"square{i} {d}"))
                last = mm(b[:, 0:TOK], ones, hT[:, d, :], d == 0, d == KD - 1)
            last.then_inc(mark("norm_sums", f"norm{i} ready"), 1)

        def small():
            pe.wait_ge(*when("small weights"))
            for d in range(KD):
                pe.wait_ge(*when(f"h1 {d}"))
            b = ring_bank("ra")
            for k in range(KD):
                last = mm(b[0:RANK, 0:TOK], wsm[:, k, 0:RANK], hT[:, k, :], k == 0, k == KD - 1)
            last.then_inc(mark("small_products", "ra ready"), 1)
            b = ring_bank("ba")
            for m, (o, n) in enumerate(TILES):
                for k in range(KD):
                    last = mm(b[0:n, 16 * m:16 * m + 16], hT[:, k, o:o + n], wsm[:, k, 16:32], k == 0, k == KD - 1)
            last.then_inc(mark("small_products", "ba ready"), 1)
            pe.wait_ge(*when("g"))
            b = ring_bank("bcum")
            for m, (o, n) in enumerate(TILES):
                mm(b[0:n, 8 * m:8 * m + 8], TRI[m][0:n, 0:n], gB[0:n, m, :])
                mm(b[0:n, 32 + 8 * m:40 + 8 * m], LAST[m][0:n, 0:n], gB[0:n, m, :])
            last = mm(b[:, 64:64 + 64], ones[0:32, :], gseq[0:32].rearrange("p s h -> p (s h)"))
            last.then_inc(mark("small_products", "bcum ready"), 1)

        def step(s):
            if s < NPROJ:
                name = ("win", s - s % 2)
                pe.wait_ge(*when(loaded(name)))
                w = slot(name)
                j = s % 2
                b = ring_bank(f"proj{s}")
                for k in range(KD):
                    last = mm(b[:, 0:TOK], w[:, k, 128 * j:128 * j + 128], hT[:, k, :], k == 0, k == KD - 1)
                last.then_inc(mark("projected", f"proj{s} ready", *([used(name)] if j == 1 else [])), 1)
            s5 = s - 5
            if 0 <= s5 < NPROJ:
                kind, i, _ = PROJ[s5]
                if kind == "cv" and i < 16:
                    pe.wait_ge(*when(f"sq{s5}"))
                    b = ring_bank(f"ssq{s5}")
                    mm(b[:, 0:TOK], ones, sqb[:, s5 % 2, :]).then_inc(mark("norm_sums", f"ssq{s5} ready"), 1)
                if kind == "va" or (kind == "cv" and i >= 16):
                    pe.wait_ge(*when(f"y{s5}" if kind == "va" else f"act{s5}"))
                    b = ring_bank(f"tr{s5}")
                    src = yb[:, s5 % 4] if kind == "va" else sgm[:, s5 % 4]
                    for m, (o, n) in enumerate(TILES):
                        last = tr(b[0:n, 128 * m:128 * m + 128], src[:, o:o + n], 128)
                    last.then_inc(mark("transposed", f"tr{s5} ready"), 1)

        def gla(m):
            o, n = TILES[m]
            t = f"gla{m} "
            pe.wait_ge(*when("wa2"))
            b = take(4, t + "logits read")
            mm(b[0:n, :], raT[0:RANK + 1, o:o + n], wa2[0:RANK + 1, :]) \
                .then_inc(mark("gla_products", t + "logits"), 1)
            pe.wait_ge(*when(t + "log decay"))
            b = take(5, t + "cum read")
            for h in range(HA):
                last = mm(b[:, n * h:n * h + n], gA[0:n, h, :], TRI[m][0:n, 0:n])
            last.then_inc(mark("gla_products", t + "cum"), 1)
            pe.wait_ge(*when(t + "qq"))
            pe.wait_ge(*when(t + "kk"))
            b = take(6, t + "A read")
            for h in range(HA):
                last = mm(b[0:n, n * h:n * h + n], Em[:, h, 0:n], Ep[:, h, 0:n])
            last.then_inc(mark("gla_products", t + "A"), 1)
            pe.wait_ge(*when(t + "ke"))
            b = take(7, t + "keT")
            for h in range(HA):
                last = tr(b[0:n, 128 * h:128 * h + 128], El[:, h, 0:n], 128)
            last.then_inc(mark("gla_products", t + "ke transposed"), 1)
            if m == 2:
                pe.wait_ge(*when(t + "qb"))
                b = take(6, t + "oS")
                for c in range(4):
                    pe.wait_ge(*when(loaded(("sgla", c))))
                    w = slot(("sgla", c)).rearrange("p (s h) v -> p s h v", h=HA)
                    for s2 in range(2):
                        s = 2 * c + s2
                        for h in range(HA):
                            for half in range(2):
                                j = 32 * (2 * h + half) + DT * s
                                last = mm(b[:, j:j + DT], w[:, s2, h, 128 * half:128 * half + 128],
                                          Eb[:, h, DT * s:DT * s + DT])
                last.then_inc(mark("gla_products", t + "oS ready"), 1)
                pe.wait_ge(*when(t + "oS"))
            pe.wait_ge(*when(t + "AT"))
            for g in range(2):
                b = take(4 + g, t + f"o{g} read")
                for hh in range(2):
                    h = 2 * g + hh
                    out = b[0:n, 256 * hh:256 * hh + 256]
                    last = mm(out, ATa[0:n, h, 0:n], vA[0:n, m, 256 * h:256 * h + 256], True, m == 0)
                    if m == 1:
                        last = mm(out, Eb[:, h, 0:n], SA[:, h, :], False, True)
                    if m == 2:
                        for half in range(2):
                            last = mm(out[:, 128 * half:128 * half + 128], oSt[:, 2 * h + half, :], ident,
                                      False, half == 1)
                last.then_inc(mark("gla_products", t + f"o{g} ready"), 1)
            pe.wait_ge(*when(t + "keT"))
            if m < 2:
                for g in range(2):
                    b = take(6 + g, t + f"S{g} read")
                    for hh in range(2):
                        h = 2 * g + hh
                        last = mm(b[:, 256 * hh:256 * hh + 256], keTa[0:n, h, :], vA[0:n, m, 256 * h:256 * h + 256])
                    last.then_inc(mark("gla_products", t + f"S{g} ready"), 1)
            else:
                for s in range(NSEQ):
                    pe.wait_ge(*when(f"kem1 {s}"))
                    for g in range(2):
                        b = take(6 + g, f"gla state {s} {g}")
                        for hh in range(2):
                            h = 2 * g + hh
                            last = mm(b[:, 256 * hh:256 * hh + 256], kem1[0:32, s % 2, 128 * h:128 * h + 128],
                                      vA[0:32, 2, 256 * h:256 * h + 256])
                        last.then_inc(mark("gla_products", f"gla state product {s} {g}"), 1)
            for g in range(2):
                pe.wait_ge(*when(t + "oN"))
                b = take(4 + g, t + f"oT{g}")
                for j in range(4):
                    c = 4 * g + j
                    last = tr(b[:, 128 * j:128 * j + n], oNa[0:n, 128 * c:128 * c + 128], n)
                last.then_inc(mark("gla_products", t + f"oT{g} ready"), 1)

        def conv_out():
            for i in range(CT):
                pe.wait_ge(*when(f"cc{i}"))
            for g in range(6):
                b = ring_bank(f"cvo{g}")
                for j in range(4):
                    last = tr(b[0:27, 128 * j:128 * j + 128], ccT[:, 4 * g + j, :], 128)
                last.then_inc(mark("transposed", f"cvo{g} ready"), 1)

        def gdn(m):
            o, n = TILES[m]
            t = f"gdn{m} "
            HG = 4
            pe.wait_ge(*when(t + "tg"))
            for g in range(2):
                b = take(4 + g, t + f"D{g}")
                mm(b[0:n, 0:HG * n], ones[0:n, 0:n], tg[0:n, HG * g:HG * g + HG, 0:n]) \
                    .then_inc(mark("gdn_products", t + f"bc{g}"), 1)
            for g in range(2):
                b = take(6 + g, t + f"KK{g} read")
                for j in range(HG):
                    h = HG * g + j
                    last = mm(b[0:n, n * j:n * j + n], kB[:, h, o:o + n], kB[:, h, o:o + n])
                last.then_inc(mark("gdn_products", t + f"KK{g}"), 1)
            for g in range(2):
                b = take(4 + g, t + f"AT{g}")
                for j in range(HG):
                    h = HG * g + j
                    last = mm(b[0:n, n * j:n * j + n], kB[:, h, o:o + n], qB[:, h, o:o + n])
                last.then_inc(mark("gdn_products", t + f"QK{g}"), 1)
            levels = LEVELS if m < 2 else 2
            for lv in range(levels):
                for g in range(2):
                    pe.wait_ge(*when(t + f"Lm{lv} {g}"))
                    b = take(4 + g, t + f"Y{lv} {g}")
                    for j in range(HG):
                        h = HG * g + j
                        rhs = ident[0:n, 0:n] if lv == 0 else X[0:n, h, 1, 0:n]
                        last = mm(b[0:n, n * j:n * j + n], Lm[0:n, h, 0:n], rhs)
                    last.then_inc(mark("gdn_products", t + f"Y{lv} {g} ready"), 1)
                if lv == 0:
                    continue
                for g in range(2):
                    pe.wait_ge(*when(t + f"Y{lv} {g}"))
                    b = take(6 + g, t + f"XT{lv} {g}")
                    for j in range(HG):
                        h = HG * g + j
                        last = mm(b[0:n, n * j:n * j + n], Y[0:n, h, 0:n], X[0:n, h, 0, 0:n])
                    last.then_inc(mark("gdn_products", t + f"ZT{lv} {g}"), 1)
                    if lv < levels - 1:
                        b = take(4 + g, t + f"X{lv} {g}")
                        for j in range(HG):
                            h = HG * g + j
                            last = mm(b[0:n, n * j:n * j + n], X[0:n, h, 0, 0:n], Y[0:n, h, 0:n])
                        last.then_inc(mark("gdn_products", t + f"Z{lv} {g}"), 1)
            for g in range(2):
                b = take(4 + g, t + f"ke{g}")
                for j in range(HG):
                    last = tr(b[0:n, 128 * j:128 * j + 128], kB[:, HG * g + j, o:o + n], 128)
                last.then_inc(mark("gdn_products", t + f"kT{g}"), 1)
            if m == 1:
                for g in range(2):
                    b = take(6 + g, t + f"R{g}")
                    for j in range(HG):
                        h = HG * g + j
                        last = mm(b[:, 128 * j:128 * j + 128], kB[:, h, o:o + n], SB[:, h, :])
                    last.then_inc(mark("gdn_products", t + f"kS{g}"), 1)
            if m == 2:
                bk, bq = take(6, t + "kSs"), take(7, t + "qSs")
                for c in range(4):
                    pe.wait_ge(*when(loaded(("sgdn", c))))
                    w = slot(("sgdn", c)).rearrange("p k n -> p (k n)").rearrange("p (s h v) -> p s h v", h=HB, v=DVB)
                    for s2 in range(2):
                        s = 2 * c + s2
                        for h in range(HB):
                            j = 32 * h + DT * s
                            at = SEQ + DT * s
                            mm(bk[:, j:j + DT], w[:, s2, h, :], kB[:, h, at:at + DT])
                            last = mm(bq[:, j:j + DT], w[:, s2, h, :], qB[:, h, at:at + DT])
                last.then_inc(mark("gdn_products", t + "Ss"), 1)
                pe.wait_ge(*when(t + "kSs"))
                for g in range(2):
                    b = take(6 + g, t + f"R{g}")
                    for j in range(HG):
                        last = tr(b[0:n, 128 * j:128 * j + 128], oSt[:, HG * g + j, :], 128)
                    last.then_inc(mark("gdn_products", t + f"kS{g}"), 1)
            for g in range(2):
                pe.wait_ge(*when(t + f"XT{levels - 1} {g}"))
                if m:
                    pe.wait_ge(*when(t + f"R{g}"))
                else:
                    for c in range(8):
                        pe.wait_ge(*when(f"vbtok{c}"))
                b = take(4 + g, t + f"vn{g}")
                for j in range(HG):
                    h = HG * g + j
                    rhs = vB[0:n, m, 128 * h:128 * h + 128] if m == 0 else R[0:n, h, :]
                    last = mm(b[0:n, 128 * j:128 * j + 128], X[0:n, h, 0, 0:n], rhs)
                last.then_inc(mark("gdn_products", t + f"y{g}"), 1)
            for g in range(2):
                if m == 1:
                    b = take(6 + g, t + f"qS{g} read")
                    for j in range(HG):
                        h = HG * g + j
                        last = mm(b[:, 128 * j:128 * j + 128], qB[:, h, o:o + n], SB[:, h, :])
                    last.then_inc(mark("gdn_products", t + f"qS{g}"), 1)
                if m == 2:
                    b = take(6 + g, t + f"qS{g} read")
                    for j in range(HG):
                        last = tr(b[0:n, 128 * j:128 * j + 128], oSt2[:, HG * g + j, :], 128)
                    last.then_inc(mark("gdn_products", t + f"qS{g}"), 1)
            for g in range(2):
                pe.wait_ge(*when(t + f"vn{g}"))
                b = take(4 + g, t + f"o{g}")
                for j in range(HG):
                    h = HG * g + j
                    last = mm(b[0:n, 128 * j:128 * j + 128], AT[0:n, h, 0:n], R[0:n, h, :])
                last.then_inc(mark("gdn_products", t + f"o{g} ready"), 1)
            if m < 2:
                for g in range(2):
                    b = take(6 + g, t + f"state{g}")
                    for j in range(HG):
                        h = HG * g + j
                        last = mm(b[:, 128 * j:128 * j + 128], ke[0:n, h, :], R[0:n, h, :])
                    last.then_inc(mark("gdn_products", t + f"S{g} ready"), 1)
            else:
                for s in range(NSEQ):
                    pe.wait_ge(*when(f"kem2 {s}"))
                    for g in range(2):
                        b = take(6 + g, f"gdn state {s} {g}")
                        for j in range(HG):
                            h = HG * g + j
                            last = mm(b[:, 128 * j:128 * j + 128], kem2[0:32, s % 2, 128 * h:128 * h + 128],
                                      R[0:32, h, :])
                        last.then_inc(mark("gdn_products", f"gdn state product {s} {g}"), 1)
            for g in range(2):
                pe.wait_ge(*when(t + "oN"))
                b = take(4 + g, t + f"oT{g}")
                for j in range(4):
                    c = 4 * g + j
                    last = tr(b[:, 128 * j:128 * j + n], oNb[0:n, 128 * c:128 * c + 128], n)
                last.then_inc(mark("gdn_products", t + f"oT{g} ready"), 1)

        def wout():
            for c in range(4):
                pe.wait_ge(*when(loaded(("wout", c))))
                w = slot(("wout", c))
                for j in range(2):
                    d = 2 * c + j
                    if d == 0:
                        for k in range(KD):
                            pe.wait_ge(*when(f"merged {k}"))
                    b = ring_bank(f"wout{d}")
                    for k in range(KD):
                        last = mm(b[:, 0:TOK], w[:, k, 128 * j:128 * j + 128], GA[:, k, :], k == 0, k == KD - 1)
                    last \
                        .then_inc(mark("projected", f"wout{d} ready", *([used(("wout", c))] if j == 1 else [])), 1)

        def router():
            pe.wait_ge(*when("router weights"))
            for d in range(KD):
                pe.wait_ge(*when(f"h2 {d}"))
            b = ring_bank("router")
            for m, (o, n) in enumerate(TILES):
                for k in range(KD):
                    last = mm(b[0:n, 20 * m:20 * m + 20], hT[:, k, o:o + n], rtw[:, k, :], k == 0, k == KD - 1)
            last.then_inc(mark("router_products", "router ready"), 1)
            pe.wait_ge(*when("comb"))
            b = ring_bank("combT")
            for m, (o, n) in enumerate(TILES):
                last = tr(b[0:16, o:o + n], comb[0:n, m, :], n)
            last.then_inc(mark("router_products", "combT ready"), 1)

        def experts():
            for e in range(NE):
                b = ring_bank(f"cmb{e}")
                pe.wait_ge(*when(f"cmb {e}"))
                mm(b[:, 0:TOK], ones[0:16, :], cmb[0:16, e % 2, :]) \
                    .then_inc(mark("router_products", f"cmb{e} ready"), 1)
                for f in range(4):
                    for w_ in range(2):
                        pe.wait_ge(*when(f"ew{e} {w_}"))
                        w = EW[:, (3 * e + w_) % 8].rearrange("p (k n) -> p k n", k=KD)
                        b = ring_bank(f"gu{e} {f} {w_}")
                        for k in range(KD):
                            last = mm(b[:, 0:TOK], w[:, k, 128 * f:128 * f + 128], hT[:, k, :], k == 0, k == KD - 1)
                        ev = [f"gu{e} {f} {w_} ready"]
                        if f == 3:
                            ev.append(f"ewused{e} {w_}")
                        last.then_inc(mark("expert_products", *ev), 1)
                for d in range(KD):
                    pe.wait_ge(*when(f"ew{e} 2"))
                    w = EW[:, (3 * e + 2) % 8].rearrange("p (k n) -> p k n", k=4)
                    b = take(4 + d % 4, f"acc{e} {d}")
                    for k in range(4):
                        pe.wait_ge(*when(f"hid{e} {k}"))
                        last = mm(b[:, 0:TOK], w[:, k, 128 * d:128 * d + 128], hid[:, k, :], k == 0, k == 3)
                    ev = [f"down{e} {d}"]
                    if d == KD - 1:
                        ev.append(f"ewused{e} 2")
                    last.then_inc(mark("expert_products", *ev), 1)

        def final():
            b = ring_bank("norm3")
            for d in range(KD):
                pe.wait_ge(*when(f"square3 {d}"))
                last = mm(b[:, 0:TOK], ones, hT[:, d, :], d == 0, d == KD - 1)
            last.then_inc(mark("norm_sums", "norm3 ready"), 1)
            for g in range(2):
                for m, (o, n) in enumerate(TILES):
                    for j in range(4):
                        pe.wait_ge(*when(f"yf {4 * g + j}"))
                    b = ring_bank(f"y{g}{m}")
                    for j in range(4):
                        last = tr(b[0:n, 128 * j:128 * j + 128], hT[:, 4 * g + j, o:o + n], 128)
                    last.then_inc(mark("transposed", f"y{g}{m} ready"), 1)

        run(locals())

    @block.vector
    def _(dve):
        def head():
            dve.wait_ge(*when("c exp1"))
            dve.wait_ge(*when("c rows"))
            V.scalar_tensor_tensor(csx[0:NC9, 1, :], crow[0:NC9, :], 0.0, csx[0:NC9, 0, :], ALU.min, ALU.subtract) \
                .then_inc(mark("head_by_vector", "c ls"), 1)
            dve.wait_ge(*when("c sig"))
            V.tensor_tensor(crow[0:NC9, :], crow[0:NC9, :], csx[0:NC9, 1, :], ALU.mult) \
                .then_inc(mark("head_by_vector", "silu(c)"), 1)
            dve.wait_ge(*when("vec ready"))
            V.tensor_copy(vecT[:, 0:NVEC], rb("vec")[:, 0:NVEC])
            V.tensor_copy(convT[:, 0:96], rb("vec")[:, 128:224]).then_inc(mark("head_by_vector", "read vec"), 1)
            for d in range(KD):
                dve.wait_ge(*when(f"x{d} ready"))
                V.tensor_copy(xT[:, d, :], rb(f"x{d}")[:, 0:TOK]) \
                    .then_inc(mark("head_by_vector", f"read x{d}"), 1)
            for g in range(2):
                dve.wait_ge(*when(f"cb{g} ready"))
                V.tensor_copy(cbT[:, 12 * g:12 * g + 12, :],
                                   rb(f"cb{g}")[:, 0:288].rearrange("p (a b) -> p a b", b=24)) \
                    .then_inc(mark("head_by_vector", f"read cb{g}"), 1)
            dve.wait_ge(*when("c ready"))
            V.tensor_copy(csT, rb("c")[:, 0:KD * NC9].rearrange("p (a b) -> p a b", b=NC9)) \
                .then_inc(mark("head_by_vector", "read c"), 1)

        def ada(c):
            dve.wait_ge(*when(f"ada{c} ready"))
            dve.wait_ge(*when("read vec"))
            V.tensor_tensor(modT[:, 2 * c:2 * c + 2, :],
                                 rb(f"ada{c}")[:, 0:2 * NC9].rearrange("p (a b) -> p a b", b=NC9),
                                 bc(vecT[:, 2 * c:2 * c + 2], NC9), ALU.add) \
                .then_inc(mark("ada_by_vector", f"read ada{c}"), 1)

        def norm(i):
            base = 24 * (i - 1)
            dve.wait_ge(*when(f"read ada{(base + 15) // 2}"))
            AA = A1 if i == 1 else A2
            o, _ = VEC[f"norm{i}"]
            V.scalar_tensor_tensor(AA, modT[:, base + 8:base + 16, :], 1.0, bc(vecT[:, o:o + 8], NC9),
                                        ALU.add, ALU.mult) \
                .then_inc(mark("norm_by_vector", f"A{i}"), 1)
            dve.wait_ge(*when(f"rstd{i}"))
            dve.wait_ge(*when(f"A{i}"))
            dve.wait_ge(*when(f"norm{i} ready"))
            for d in range(KD):
                V.tensor_tensor(hT[:, d, :], xT[:, d, :], rsB, ALU.mult) \
                    .then_inc(mark("norm_by_vector", f"n{i} {d}"), 1)
            for d in range(KD):
                dve.wait_ge(*when(f"n{i} {d}"))
                V.tensor_scalar(hT[:, d, 0:SEQ], hT[:, d, 0:SEQ], AA[:, d, 0:1], modT[:, base + d, 0:1], ALU.mult,
                                ALU.add)
                hs = hT[:, d, SEQ:TOK].rearrange("p (s t) -> p s t", t=DT)
                V.tensor_tensor(hs, hs, bc(AA[:, d, 1:NC9], DT), ALU.mult) \
                    .then_inc(mark("norm_by_vector", f"m{i} {d}"), 1)
            for d in range(KD):
                dve.wait_ge(*when(f"m{i} {d}"))
                hs = hT[:, d, SEQ:TOK].rearrange("p (s t) -> p s t", t=DT)
                V.tensor_tensor(hs, hs, bc(modT[:, base + d, 1:NC9], DT), ALU.add) \
                    .then_inc(mark("norm_by_vector", f"h{i} {d}"), 1)

        def small():
            dve.wait_ge(*when("ra ready"))
            dve.wait_ge(*when("raT ones"))
            V.tensor_copy(raT[0:RANK, :], rb("ra")[0:RANK, 0:TOK]) \
                .then_inc(mark("small_by_vector", "read ra", "raT"), 1)
            dve.wait_ge(*when("ba ready"))
            dve.wait_ge(*when("adt"))
            V.tensor_copy(ba[:, 0:2, :], rb("ba")[:, 0:32].rearrange("p (a b) -> p a b", b=16))
            V.tensor_copy(ba[0:32, 2, :], rb("ba")[0:32, 32:48]).then_inc(mark("small_by_vector", "read ba"), 1)
            dve.wait_ge(*when("read ba"))
            V.tensor_tensor(ba[:, :, 8:16], ba[:, :, 8:16], mid(adt[:, 1, :], 3), ALU.add) \
                .then_inc(mark("small_by_vector", "a + dt"), 1)
            dve.wait_ge(*when("small ln"))
            V.scalar_tensor_tensor(beta, ba[:, :, 0:8], 0.0, bcum_tmp(0), ALU.min, ALU.subtract)
            V.scalar_tensor_tensor(gt, ba[:, :, 8:16], 0.0, bcum_tmp(1), ALU.max, ALU.add) \
                .then_inc(mark("small_by_vector", "softplus"), 1)
            dve.wait_ge(*when("softplus"))
            dve.wait_ge(*when("exp A"))
            V.scalar_tensor_tensor(gB, gt, -1.0, mid(adt[:, 0, :], 3), ALU.mult, ALU.mult) \
                .then_inc(mark("small_by_vector", "g main"), 1)
            dve.wait_ge(*when("g main"))
            V.tensor_tensor(gseq[0:32], mid(gB[0:32, 2, :], NSEQ), bc(const("seq")[0:32, :], HB), ALU.mult) \
                .then_inc(mark("small_by_vector", "g"), 1)
            dve.wait_ge(*when("bcum ready"))
            for m, (o, n) in enumerate(TILES):
                V.tensor_copy(bcum[0:n, m, :], rb("bcum")[0:n, 8 * m:8 * m + 8])
                V.tensor_copy(blast[0:n, m, :], rb("bcum")[0:n, 32 + 8 * m:40 + 8 * m]) \
                    .then_inc(mark("small_by_vector", f"b{m}"), 1)
            dve.wait_ge(*when("b2"))
            V.tensor_tensor(gt, blast, bcum, ALU.subtract).then_inc(mark("small_by_vector", "b rest"), 1)

        def bcum_tmp(i):
            return sgm[:, 0, 24 * i:24 * i + 24].rearrange("p (a b) -> p a b", b=8)

        def step(s):
            s6, s4, s3, s1 = s - 6, s - 4, s - 3, s - 1
            if 0 <= s6 < NPROJ:
                kind, i, _ = PROJ[s6]
                if kind == "cv" and i < 16:
                    q = (qB if i < 8 else kB)[:, i % 8, :]
                    dve.wait_ge(*when(f"rs{s6}"))
                    V.tensor_tensor(q, q, rsb[:, s6 % 2, :], ALU.mult) \
                        .then_inc(mark("proj_by_vector", f"qkn{s6}"), 1)
                if kind == "va" or (kind == "cv" and i >= 16):
                    dve.wait_ge(*when(f"tr{s6} ready"))
                    dst = vA if kind == "va" else vB
                    c = i if kind == "va" else i - 16
                    b = rb(f"tr{s6}")
                    V.tensor_copy(dst[:, 0:2, 128 * c:128 * c + 128], b[:, 0:256].rearrange("p (a b) -> p a b", b=128))
                    V.tensor_copy(dst[0:32, 2, 128 * c:128 * c + 128], b[0:32, 256:384]) \
                        .then_inc(mark("proj_by_vector", f"read tr{s6}", f"vtok{i}" if kind == "va" else f"vbtok{c}"), 1)
            if 0 <= s4 < NPROJ:
                kind, i, _ = PROJ[s4]
                sg, y = sgm[:, s4 % 4], yb[:, s4 % 4]
                if kind in ("cv", "ga", "zb", "gsa", "gsb"):
                    dve.wait_ge(*when(f"sig{s4}"))
                if kind == "cv":
                    if i < 16:
                        out = (qB if i < 8 else kB)[:, i % 8, :]
                        V.tensor_tensor(out[:, 0:SEQ], y[:, 0:SEQ], sg[:, 0:SEQ], ALU.mult)
                        V.tensor_tensor(out[:, SEQ:TOK].rearrange("p (s t) -> p s t", t=DT), sampled(y),
                                             sampled(sg), ALU.mult) \
                            .then_inc(mark("proj_by_vector", f"act{s4}"), 1)
                    else:
                        V.tensor_tensor(sg[:, 0:SEQ], y[:, 0:SEQ], sg[:, 0:SEQ], ALU.mult) \
                            .then_inc(mark("proj_by_vector", f"actp{s4}"), 1)
                        dve.wait_ge(*when(f"actp{s4}"))
                        V.tensor_tensor(y[:, 0:32].rearrange("p (s t) -> p s t", t=DT), sampled(y), sampled(sg),
                                             ALU.mult) \
                            .then_inc(mark("proj_by_vector", f"acty{s4}"), 1)
                        dve.wait_ge(*when(f"acty{s4}"))
                        V.tensor_copy(sg[:, SEQ:TOK], y[:, 0:32]) \
                            .then_inc(mark("proj_by_vector", f"act{s4}"), 1)
                if kind == "ga":
                    V.tensor_tensor(GA[:, i, :], y[:, 0:TOK], sg[:, 0:TOK], ALU.mult) \
                        .then_inc(mark("proj_by_vector", f"act{s4}"), 1)
                if kind == "zb":
                    V.tensor_tensor(GB[:, i, :], y[:, 0:TOK], sg[:, 0:TOK], ALU.mult) \
                        .then_inc(mark("proj_by_vector", f"act{s4}"), 1)
                if kind in ("gsa", "gsb"):
                    GG = GA if kind == "gsa" else GB
                    dve.wait_ge(*when(f"act{s4 - 8}"))
                    V.tensor_tensor(GG[:, i, :], GG[:, i, :], sg[:, 0:TOK], ALU.mult) \
                        .then_inc(mark("proj_by_vector", f"act{s4}"), 1)
            if 0 <= s3 < NPROJ:
                kind, i, _ = PROJ[s3]
                if kind in ("cv", "ga", "zb", "gsa", "gsb"):
                    n = YW if kind == "cv" else TOK
                    dve.wait_ge(*when(f"ln{s3}"))
                    sg, y = sgm[:, s3 % 4, 0:n], yb[:, s3 % 4, 0:n]
                    V.scalar_tensor_tensor(sg, y, 0.0, sg, ALU.min, ALU.subtract) \
                        .then_inc(mark("proj_by_vector", f"ls{s3}"), 1)
            if 0 <= s1 < NPROJ:
                kind, i, _ = PROJ[s1]
                if kind == "cv":
                    dve.wait_ge(*when(f"xp{s1}"))
                    x, y = xp[:, s1 % 2], yb[:, s1 % 4]
                    dve.wait_ge(*when("read c"))
                    for event in y_free(s1 - 4):
                        dve.wait_ge(*when(event))
                    wv = lambda j: convT[:, 24 * j + i:24 * j + i + 1]
                    V.tensor_scalar(y, x[:, 0:YW], wv(0), None, ALU.mult) \
                        .then_inc(mark("proj_by_vector", f"tap0 {s1}"), 1)
                    for j in range(1, TAPS):
                        dve.wait_ge(*when(f"tap{j - 1} {s1}"))
                        V.scalar_tensor_tensor(y, x[:, j:j + YW], wv(j), y, ALU.mult, ALU.add) \
                            .then_inc(mark("proj_by_vector", f"tap{j} {s1}"), 1)

        def sampled(a):
            return a[:, SEQ:SEQ + 7 * NSEQ].rearrange("p (s t) -> p s t", t=7)[:, :, 3:7]

        def gla(m):
            o, n = TILES[m]
            t = f"gla{m} "
            dve.wait_ge(*when(t + "ln"))
            V.scalar_tensor_tensor(gA[0:n].rearrange("p a b -> p (a b)"), pm[4][0:n, :], 0.0,
                                        gA[0:n].rearrange("p a b -> p (a b)"), ALU.min, ALU.subtract) \
                .then_inc(mark("gla_by_vector", t + "logits read", t + "log decay"), 1)
            dve.wait_ge(*when(t + "cum"))
            dve.wait_ge(*when(t + "eb"))
            cum = pm[5][:, 0:HA * n].rearrange("p (h t) -> p h t", t=n)
            if m < 2:
                V.tensor_copy(ebl[:, :, 0:1], Eb[:, :, n - 1:n])
                V.tensor_copy(ebl[:, :, 1:2], cum[:, :, n // 2 - 1:n // 2]) \
                    .then_inc(mark("gla_by_vector", t + "ref"), 1)
                V.tensor_copy(ebl[:, :, 2:3], cum[:, :, n - 1:n]).then_inc(mark("gla_by_vector", t + "ref2"), 1)
                dve.wait_ge(*when(t + "ref2"))
                V.tensor_tensor(Ep, cum, ebl[:, :, 1:2].to_broadcast([P, HA, n]), ALU.subtract)
                V.tensor_tensor(El, ebl[:, :, 2:3].to_broadcast([P, HA, n]), cum, ALU.subtract) \
                    .then_inc(mark("gla_by_vector", t + "cum read", t + "D"), 1)
            else:
                V.tensor_copy(Em[:, :, 0:n], cum).then_inc(mark("gla_by_vector", t + "cumc"), 1)
                dve.wait_ge(*when(t + "cumc"))
                V.tensor_copy(Ep[:, :, 0:n], Em[:, :, 0:n])
                for h in range(HA):
                    c4 = Em[:, h, 0:n].rearrange("p (s t) -> p s t", t=DT)
                    e4 = Eb[:, h, 0:n].rearrange("p (s t) -> p s t", t=DT)
                    V.tensor_copy(ebl[:, h, :].unsqueeze(2), e4[:, :, DT - 1:DT])
                    last = V.tensor_tensor(El[:, h, 0:n].rearrange("p (s t) -> p s t", t=DT),
                                           c4[:, :, DT - 1:DT].to_broadcast([P, NSEQ, DT]), c4, ALU.subtract)
                last.then_inc(mark("gla_by_vector", t + "cum read", t + "D"), 1)
            q, k = QKA[:, 0:HA, o:o + n], QKA[:, HA:2 * HA, o:o + n]
            dve.wait_ge(*when(t + "exps"))
            V.tensor_tensor(Ep[:, :, 0:n], q, Ep[:, :, 0:n], ALU.mult) \
                .then_inc(mark("gla_by_vector", t + "qq"), 1)
            V.tensor_tensor(Em[:, :, 0:n], k, Em[:, :, 0:n], ALU.mult) \
                .then_inc(mark("gla_by_vector", t + "kk"), 1)
            V.tensor_tensor(El[:, :, 0:n], k, El[:, :, 0:n], ALU.mult) \
                .then_inc(mark("gla_by_vector", t + "ke"), 1)
            V.tensor_tensor(Eb[:, :, 0:n], q, Eb[:, :, 0:n], ALU.mult) \
                .then_inc(mark("gla_by_vector", t + "qb"), 1)
            dve.wait_ge(*when(t + "A"))
            V.tensor_tensor(ATa[0:n, :, 0:n], pm[6][0:n, 0:HA * n].rearrange("p (h t) -> p h t", t=n),
                                 mid(TRI[m][0:n, 0:n], HA), ALU.mult) \
                .then_inc(mark("gla_by_vector", t + "A read", t + "AT"), 1)
            if m == 2:
                dve.wait_ge(*when(t + "oS ready"))
                V.tensor_copy(oSt, pm[6][:, 0:256].rearrange("p (a b) -> p a b", b=32)) \
                    .then_inc(mark("gla_by_vector", t + "oS"), 1)
            if m == 1:
                for g in range(2):
                    dve.wait_ge(*when(t + f"S{g} ready"))
                    dve.wait_ge(*when(t + f"o{g} ready"))
                    for hh in range(2):
                        h = 2 * g + hh
                        last = V.scalar_tensor_tensor(SA[:, h, :], SA[:, h, :], ebl[:, h, 0:1],
                                                      pm[6 + g][:, 256 * hh:256 * hh + 256], ALU.mult, ALU.add)
                    last.then_inc(mark("gla_by_vector", t + f"S{g} read", f"gla state prompt {g}"), 1)
            dve.wait_ge(*when(t + "rstd"))
            dve.wait_ge(*when(t + "o1 ready"))
            for g in range(2):
                last = V.tensor_tensor(oNa[0:n, 512 * g:512 * g + 512].rearrange("p (a b) -> p a b", b=256),
                                       pm[4 + g][0:n, :].rearrange("p (a b) -> p a b", b=256),
                                       bc(srs[0:n, 2 * g:2 * g + 2], 256), ALU.mult)
                last.then_inc(mark("gla_by_vector", t + f"o{g} read", *([t + "oN"] if g else [])), 1)
            if m == 2:
                for s in range(NSEQ):
                    w = slot(("sgla", s // 2)).rearrange("p (s h) v -> p s h v", h=HA)
                    for g in range(2):
                        dve.wait_ge(*when(f"gla state product {s} {g}"))
                        for hh in range(2):
                            h = 2 * g + hh
                            st = w[:, s % 2, h, :]
                            last = V.scalar_tensor_tensor(st, st, ebl[:, h, s:s + 1],
                                                          pm[6 + g][:, 256 * hh:256 * hh + 256], ALU.mult, ALU.add)
                        last.then_inc(mark("gla_by_vector", f"gla state {s} {g}"), 1)
            for g in range(2):
                dve.wait_ge(*when(t + f"oT{g} ready"))
                V.tensor_copy(QKA[:, 4 * g:4 * g + 4, o:o + n],
                                   pm[4 + g][:, 0:512].rearrange("p (a b) -> p a b", b=128)[:, :, 0:n]) \
                    .then_inc(mark("gla_by_vector", t + f"oT{g}"), 1)

        def conv_out():
            for g in range(6):
                dve.wait_ge(*when(f"cvo{g} ready"))
                V.tensor_copy(newconv[0:27, 512 * g:512 * g + 512], rb(f"cvo{g}")[0:27, :]) \
                    .then_inc(mark("proj_by_vector", f"read cvo{g}"), 1)

        def gdn(m):
            o, n = TILES[m]
            t = f"gdn{m} "
            HG = 4
            if m == 0:
                dve.wait_ge(*when("gla2 oT1"))
            else:
                pass
            V.tensor_tensor(tg[0:n, :, 0:n], mid(TRI[m][0:n, 0:n], HB), bc(gB[0:n, m, :], n), ALU.mult) \
                .then_inc(mark("gdn_by_vector", t + "tg"), 1)
            for g in range(2):
                dve.wait_ge(*when(t + f"bc{g}"))
                for j in range(HG):
                    h = HG * g + j
                    last = V.tensor_scalar(E[0:n, h, 0:n], pm[4 + g][0:n, n * j:n * j + n], bcum[0:n, m, h:h + 1],
                                           0.0, ALU.subtract, ALU.min)
                last.then_inc(mark("gdn_by_vector", t + f"D{g}"), 1)
            for g in range(2):
                dve.wait_ge(*when(t + f"E{g}"))
                ee = E[0:n, HG * g:HG * g + HG, 0:n]
                V.tensor_tensor(ee, ee, mid(TRI[m][0:n, 0:n], HG), ALU.mult) \
                    .then_inc(mark("gdn_by_vector", t + f"Em{g}"), 1)
            for g in range(2):
                dve.wait_ge(*when(t + f"KK{g}"))
                dve.wait_ge(*when(t + f"Em{g}"))
                dve.wait_ge(*when("beta"))
                for j in range(HG):
                    h = HG * g + j
                    last = V.scalar_tensor_tensor(LT[0:n, h, 0:n], pm[6 + g][0:n, n * j:n * j + n],
                                                  beta[0:n, m, h:h + 1], E[0:n, h, 0:n], ALU.mult, ALU.mult)
                last.then_inc(mark("gdn_by_vector", t + f"KK{g} read"), 1)
            for g in range(2):
                dve.wait_ge(*when(t + f"QK{g}"))
                V.tensor_tensor(AT[0:n, HG * g:HG * g + HG, 0:n],
                                     pm[4 + g][0:n, 0:HG * n].rearrange("p (h t) -> p h t", t=n),
                                     E[0:n, HG * g:HG * g + HG, 0:n], ALU.mult) \
                    .then_inc(mark("gdn_by_vector", t + f"AT{g}"), 1)
            levels = LEVELS if m < 2 else 2
            idm = mid(ident[0:n, 0:n], HG)
            for lv in range(levels):
                for g in range(2):
                    hs = slice(HG * g, HG * g + HG)
                    dve.wait_ge(*when(t + f"KK{g} read"))
                    if lv == 1:
                        dve.wait_ge(*when(t + f"XT0 {g}"))
                    V.tensor_tensor(Lm[0:n, hs, 0:n], LT[0:n, hs, 0:n],
                                         mid(const(f"level{lv}")[0:n, 0:n], HG), ALU.mult) \
                        .then_inc(mark("gdn_by_vector", t + f"Lm{lv} {g}"), 1)
                for g in range(2):
                    hs = slice(HG * g, HG * g + HG)
                    view = lambda b: pm[b][0:n, 0:HG * n].rearrange("p (h t) -> p h t", t=n)
                    if lv == 0:
                        dve.wait_ge(*when(t + f"Lm0 {g}"))
                        V.tensor_tensor(X[0:n, hs, 0, 0:n], idm, Lm[0:n, hs, 0:n], ALU.subtract) \
                            .then_inc(mark("gdn_by_vector", t + f"XT0 {g}"), 1)
                        dve.wait_ge(*when(t + f"Y0 {g} ready"))
                        V.tensor_tensor(X[0:n, hs, 1, 0:n], idm, view(4 + g), ALU.subtract) \
                            .then_inc(mark("gdn_by_vector", t + f"Y0 {g}", t + f"X0 {g}"), 1)
                    else:
                        dve.wait_ge(*when(t + f"ZT{lv} {g}"))
                        if lv < levels - 1:
                            dve.wait_ge(*when(t + f"Z{lv} {g}"))
                        V.tensor_tensor(X[0:n, hs, 0, 0:n], X[0:n, hs, 0, 0:n], view(6 + g), ALU.subtract) \
                            .then_inc(mark("gdn_by_vector", t + f"XT{lv} {g}"), 1)
                        if lv < levels - 1:
                            V.tensor_tensor(X[0:n, hs, 1, 0:n], X[0:n, hs, 1, 0:n], view(4 + g), ALU.subtract) \
                                .then_inc(mark("gdn_by_vector", t + f"X{lv} {g}"), 1)
            full = lambda b: pm[b][0:n, :].rearrange("p (h t) -> p h t", t=128)
            for g in range(2):
                hs = slice(HG * g, HG * g + HG)
                dve.wait_ge(*when(t + f"kT{g}"))
                dve.wait_ge(*when("exp b"))
                for x in range(2):
                    dve.wait_ge(*when(t + f"Lm{levels - 1} {x}"))
                V.tensor_tensor(ke[0:n, hs, :], full(4 + g), bc(elB[0:n, m, hs], 128), ALU.mult) \
                    .then_inc(mark("gdn_by_vector", t + f"ke{g}"), 1)
            if m == 2:
                dve.wait_ge(*when(t + "Ss"))
                V.tensor_copy(oSt, pm[6][:, 0:256].rearrange("p (a b) -> p a b", b=32)) \
                    .then_inc(mark("gdn_by_vector", t + "kSs"), 1)
                V.tensor_copy(oSt2, pm[7][:, 0:256].rearrange("p (a b) -> p a b", b=32)) \
                    .then_inc(mark("gdn_by_vector", t + "qSs"), 1)
            for g in range(2):
                hs = slice(HG * g, HG * g + HG)
                vtok = vB[0:n, m, 512 * g:512 * g + 512].rearrange("p (h v) -> p h v", v=128)
                if m == 0:
                    continue
                dve.wait_ge(*when(t + f"kS{g}"))
                V.tensor_tensor(R[0:n, hs, :], full(6 + g), bc(ebB[0:n, m, hs], 128), ALU.mult) \
                    .then_inc(mark("gdn_by_vector", t + f"ekS{g}"), 1)
                dve.wait_ge(*when(t + f"ekS{g}"))
                V.tensor_tensor(R[0:n, hs, :], vtok, R[0:n, hs, :], ALU.subtract) \
                    .then_inc(mark("gdn_by_vector", t + f"R{g}"), 1)
            for g in range(2):
                hs = slice(HG * g, HG * g + HG)
                dve.wait_ge(*when(t + f"y{g}"))
                V.tensor_tensor(R[0:n, hs, :], full(4 + g), bc(beta[0:n, m, hs], 128), ALU.mult) \
                    .then_inc(mark("gdn_by_vector", t + f"vn{g}"), 1)
            for g in range(2):
                hs = slice(HG * g, HG * g + HG)
                if m:
                    dve.wait_ge(*when(t + f"qS{g}"))
                    V.tensor_tensor(E[0:n, hs, :], full(6 + g), bc(ebB[0:n, m, hs], 128), ALU.mult) \
                        .then_inc(mark("gdn_by_vector", t + f"qS{g} read"), 1)
            for g in range(2):
                hs = slice(HG * g, HG * g + HG)
                dve.wait_ge(*when(t + f"o{g} ready"))
                if m:
                    dve.wait_ge(*when(t + f"qS{g} read"))
                    V.tensor_tensor(E[0:n, hs, :], E[0:n, hs, :], full(4 + g), ALU.add) \
                        .then_inc(mark("gdn_by_vector", t + f"o{g}"), 1)
                else:
                    V.tensor_copy(E[0:n, hs, :], full(4 + g)).then_inc(mark("gdn_by_vector", t + f"o{g}"), 1)
            if m < 2:
                for g in range(2):
                    hs = slice(HG * g, HG * g + HG)
                    dve.wait_ge(*when(t + f"S{g} ready"))
                    if m == 0:
                        last = V.tensor_copy(SB[:, hs, :], full(6 + g))
                    else:
                        for j in range(HG):
                            h = HG * g + j
                            last = V.scalar_tensor_tensor(SB[:, h, :], SB[:, h, :], eSd[:, m, h:h + 1],
                                                          pm[6 + g][:, 128 * j:128 * j + 128], ALU.mult, ALU.add)
                    last.then_inc(mark("gdn_by_vector", t + f"state{g}"), 1)
            dve.wait_ge(*when(t + "squares"))
            V.tensor_reduce(ssum[0:n, :], sqo[0:n], AX, ALU.add).then_inc(mark("gdn_by_vector", t + "ssum"), 1)
            dve.wait_ge(*when(t + "rstd"))
            V.tensor_tensor(Y[0:n], E[0:n], bc(srs[0:n, :], 128), ALU.mult) \
                .then_inc(mark("gdn_by_vector", t + "oN"), 1)
            if m == 2:
                for s in range(NSEQ):
                    w = slot(("sgdn", s // 2)).rearrange("p k n -> p (k n)").rearrange("p (s h v) -> p s h v", h=HB, v=DVB)
                    for g in range(2):
                        dve.wait_ge(*when(f"gdn state product {s} {g}"))
                        for j in range(HG):
                            h = HG * g + j
                            st = w[:, s % 2, h, :]
                            last = V.scalar_tensor_tensor(st, st, eSs[:, s, h:h + 1],
                                                          pm[6 + g][:, 128 * j:128 * j + 128], ALU.mult, ALU.add)
                        last.then_inc(mark("gdn_by_vector", f"gdn state {s} {g}"), 1)
            for g in range(2):
                dve.wait_ge(*when(t + f"oT{g} ready"))
                V.tensor_copy(qB[:, 4 * g:4 * g + 4, o:o + n],
                                   pm[4 + g][:, 0:512].rearrange("p (a b) -> p a b", b=128)[:, :, 0:n]) \
                    .then_inc(mark("gdn_by_vector", t + f"oT{g}"), 1)

        def merge():
            dve.wait_ge(*when("gdn2 oT1"))
            for s in range(NPROJ - 32, NPROJ):
                dve.wait_ge(*when(f"act{s}"))
            an, bn = VEC["gla_norm"][0], VEC["gdn_norm"][0]
            for d in range(KD):
                V.scalar_tensor_tensor(GA[:, d, :], QKA[:, d, :], vecT[:, an + d % 2:an + d % 2 + 1], GA[:, d, :],
                                            ALU.mult, ALU.mult) \
                    .then_inc(mark("merge_by_vector", f"ma {d}"), 1)
                V.scalar_tensor_tensor(GB[:, d, :], qB[:, d, :], vecT[:, bn:bn + 1], GB[:, d, :],
                                            ALU.mult, ALU.mult) \
                    .then_inc(mark("merge_by_vector", f"mb {d}"), 1)
            for d in range(KD):
                dve.wait_ge(*when(f"mb {d}"))
                V.tensor_tensor(GA[:, d, :], GA[:, d, :], GB[:, d, :], ALU.add) \
                    .then_inc(mark("merge_by_vector", f"merged {d}"), 1)

        def wout():
            dve.wait_ge(*when("read ada11"))
            for d in range(KD):
                dve.wait_ge(*when(f"wout{d} ready"))
                residual(d, rb(f"wout{d}")[:, 0:TOK], 16, f"read wout{d}", f"x2 {d}", "merge_by_vector")

        def residual(d, src, gate, read, new, kind):
            V.scalar_tensor_tensor(xT[:, d, 0:SEQ], src[:, 0:SEQ], modT[:, gate + d, 0:1], xT[:, d, 0:SEQ],
                                   ALU.mult, ALU.add)
            V.tensor_tensor(gs[:, d % 2, :].rearrange("p (s t) -> p s t", t=DT),
                                 src[:, SEQ:TOK].rearrange("p (s t) -> p s t", t=DT),
                                 bc(modT[:, gate + d, 1:NC9], DT), ALU.mult) \
                .then_inc(mark(kind, read), 1)
            dve.wait_ge(*when(read))
            V.tensor_tensor(xT[:, d, SEQ:TOK], xT[:, d, SEQ:TOK], gs[:, d % 2, :], ALU.add) \
                .then_inc(mark(kind, new), 1)

        def router():
            dve.wait_ge(*when("router ready"))
            dve.wait_ge(*when("router bias"))
            dve.wait_ge(*when("rt zero"))
            V.tensor_copy(rt[:, 0:2, :], rb("router")[:, 0:40].rearrange("p (a b) -> p a b", b=20))
            V.tensor_copy(rt[0:32, 2, :], rb("router")[0:32, 40:60]) \
                .then_inc(mark("router_by_vector", "read router"), 1)
            k = [0]

            def st(ins, *ev):
                k[0] += 1
                ins.then_inc(mark("router_by_vector", f"rstep{k[0]}", *ev), 1)
                dve.wait_ge(*when(f"rstep{k[0]}"))
            dve.wait_ge(*when("read router"))
            st(V.tensor_tensor(rt, rt, mid(rtb, 3), ALU.add))
            r = rs_
            iota = mid(const("iota"), 3)
            one = lambda n: r[n][:, :, 0:1]
            spread = lambda n: r[n][:, :, 0:1].to_broadcast([P, 3, 4])

            def first_max(vals, mx, sel, i):
                st(V.tensor_reduce(one(mx), vals, AX, ALU.max))
                st(V.tensor_tensor(r["hit"], vals, spread(mx), ALU.is_equal))
                st(V.scalar_tensor_tensor(r["idx"], iota, -4.0, r["hit"], ALU.add, ALU.mult))
                st(V.tensor_reduce(one("i1"), r["idx"], AX, ALU.min))
                st(V.tensor_scalar(one("tmp"), one("i1"), 4.0, None, ALU.add))
                st(V.tensor_tensor(r[sel], iota, spread("tmp"), ALU.is_equal))

            first_max(rt[:, :, 0:4], "gmax", "gsel", 0)
            st(V.tensor_tensor(r["dd"], rt[:, :, 0:4], spread("gmax"), ALU.subtract), "gd")
            dve.wait_ge(*when("gexp"))
            st(V.tensor_reduce(one("gden"), r["dd"], AX, ALU.add))
            st(V.reciprocal(one("gw"), one("gden")))
            e4 = el16.rearrange("p m (g e) -> p m g e", e=4)
            l4 = rt[:, :, 4:20].rearrange("p m (g e) -> p m g e", e=4)
            for m in range(3):
                st(V.tensor_tensor(e4[:, m], l4[:, m], bc(r["gsel"][:, m, :], 4), ALU.mult))
                st(V.tensor_reduce(r["el"][:, m, :], e4[:, m].rearrange("p g e -> p e g"), AX, ALU.add))
            first_max(r["el"], "emax", "h1", 1)
            st(V.tensor_tensor(r["p1"], r["el"], spread("emax"), ALU.subtract), "ed")
            dve.wait_ge(*when("eexp"))
            st(V.scalar_tensor_tensor(r["p2"], r["h1"], -4.0, r["p1"], ALU.mult, ALU.add))
            first_max(r["p2"], "w2", "hh", 2)
            st(V.tensor_scalar(one("w1"), one("w2"), 1.0, None, ALU.add))
            st(V.reciprocal(one("w1"), one("w1")))
            st(V.tensor_tensor(r["within"], r["hh"], spread("w2"), ALU.mult))
            st(V.tensor_tensor(r["within"], r["within"], r["h1"], ALU.add))
            st(V.tensor_tensor(one("w1"), one("w1"), one("gw"), ALU.mult))
            st(V.tensor_tensor(r["within"], r["within"], spread("w1"), ALU.mult))
            c4 = comb.rearrange("p m (g e) -> p m g e", e=4)
            for m in range(3):
                st(V.tensor_tensor(c4[:, m], bc(r["gsel"][:, m, :], 4), mid(r["within"][:, m, :], 4), ALU.mult),
                   *(["comb"] if m == 2 else []))
            dve.wait_ge(*when("combT ready"))
            V.tensor_copy(combT[0:16, :], rb("combT")[0:16, 0:TOK]) \
                .then_inc(mark("router_by_vector", "read combT"), 1)

        def experts():
            for e in range(NE):
                dve.wait_ge(*when("read combT"))
                V.tensor_scalar(cmb[0:16, e % 2, :], combT[0:16, :], ident[0:16, e:e + 1], None, ALU.mult) \
                    .then_inc(mark("expert_by_vector", f"cmb {e}"), 1)
                dve.wait_ge(*when(f"cmb{e} ready"))
                V.tensor_copy(cmbB[:, e % 2, :], rb(f"cmb{e}")[:, 0:TOK]) \
                    .then_inc(mark("expert_by_vector", f"read cmb{e}"), 1)
                for f in range(4):
                    i = 4 * e + f
                    a, s = rb(f"gu{e} {f} 0")[:, 0:TOK], sg2[:, f, :]
                    dve.wait_ge(*when(f"eln{e} {f}"))
                    V.scalar_tensor_tensor(s, a, 0.0, s, ALU.min, ALU.subtract) \
                        .then_inc(mark("expert_by_vector", f"els{e} {f}"), 1)
                    dve.wait_ge(*when(f"esig{e} {f}"))
                    V.tensor_tensor(s, a, s, ALU.mult) \
                        .then_inc(mark("expert_by_vector", f"read gu{e} {f} 0"), 1)
                    dve.wait_ge(*when(f"read gu{e} {f} 0"))
                    dve.wait_ge(*when(f"gu{e} {f} 1 ready"))
                    V.tensor_tensor(s, rb(f"gu{e} {f} 1")[:, 0:TOK], s, ALU.mult) \
                        .then_inc(mark("expert_by_vector", f"read gu{e} {f} 1"), 1)
                    dve.wait_ge(*when(f"read gu{e} {f} 1"))
                    V.tensor_tensor(hid[:, f, :], s, cmbB[:, e % 2, :], ALU.mult) \
                        .then_inc(mark("expert_by_vector", f"hid{e} {f}"), 1)
                for d in range(KD):
                    dve.wait_ge(*when(f"down{e} {d}"))
                    src = pm[4 + d % 4][:, 0:TOK]
                    if e == 0:
                        ins = V.tensor_copy(acc[:, d, :], src)
                    else:
                        ins = V.tensor_tensor(acc[:, d, :], acc[:, d, :], src, ALU.add)
                    ins.then_inc(mark("expert_by_vector", f"acc{e} {d}"), 1)

        def final():
            dve.wait_ge(*when("read ada23"))
            for d in range(KD):
                dve.wait_ge(*when(f"acc{NE - 1} {d}"))
                residual(d, acc[:, d, :], 40, f"moe {d}", f"x3 {d}", "final_by_vector")
            fo = VEC["final"][0]
            dve.wait_ge(*when("rstd3"))
            dve.wait_ge(*when("norm3 ready"))
            for d in range(KD):
                V.scalar_tensor_tensor(hT[:, d, :], xT[:, d, :], vecT[:, fo + d:fo + d + 1], rsB, ALU.mult,
                                            ALU.mult) \
                    .then_inc(mark("final_by_vector", f"yf {d}"), 1)
            for g in range(2):
                for m, (o, n) in enumerate(TILES):
                    dve.wait_ge(*when(f"y{g}{m} ready"))
                    V.tensor_copy(yrow[0:n, m, 512 * g:512 * g + 512], rb(f"y{g}{m}")[0:n, :]) \
                        .then_inc(mark("final_by_vector", f"read y{g}{m}"), 1)

        run(locals())

    @block.scalar
    def _(act):
        A.preload_act_table_set("natural_log_exp_and_others")
        one = ones[:, 0:1]

        def lnexp(dst, src, n=P, kind="", event=None):
            A.activation(dst, src, ACT.Abs).then_inc(mark(kind, event + " abs"), 1)
            act.wait_ge(*when(event + " abs"))
            A.activation(dst, dst, ACT.Exp, scale=-1.0).then_inc(mark(kind, event + " exp"), 1)
            act.wait_ge(*when(event + " exp"))
            A.activation(dst, dst, ACT.Ln, bias=one[0:n]).then_inc(mark(kind, event), 1)

        def rstd(dst, src, scale, kind, event, n=P, bias=None, mid_event=None):
            ev = [mid_event] if mid_event else []
            A.activation(dst, src, ACT.Ln, bias=const("eps")[0:n], scale=scale) \
                .then_inc(mark(kind, event + " ln", *ev), 1)
            act.wait_ge(*when(event + " ln"))
            if bias is None:
                ins = A.activation(dst, dst, ACT.Exp, scale=-0.5)
            else:
                ins = A.activation(dst, dst, ACT.Exp, scale=-0.5, bias=bias)
            ins.then_inc(mark(kind, event), 1)

        def head():
            act.wait_ge(*when("consts"))
            act.wait_ge(*when("c rows"))
            lnexp(csx[0:NC9, 0, :], crow[0:NC9, :], NC9, "head_by_scalar", "c exp1")
            act.wait_ge(*when("c ls"))
            A.activation(csx[0:NC9, 1, :], csx[0:NC9, 1, :], ACT.Exp) \
                .then_inc(mark("head_by_scalar", "c sig"), 1)
            for d in range(KD):
                act.wait_ge(*when(f"read x{d}"))
                A.activation(hT[:, d, :], xT[:, d, :], ACT.Square) \
                    .then_inc(mark("head_by_scalar", f"square1 {d}"), 1)

        def norm(i):
            if i == 2:
                for d in range(KD):
                    act.wait_ge(*when(f"x2 {d}"))
                    A.activation(hT[:, d, :], xT[:, d, :], ACT.Square) \
                        .then_inc(mark("norm_by_scalar", f"square2 {d}"), 1)
            act.wait_ge(*when(f"norm{i} ready"))
            if i == 2:
                act.wait_ge(*when("h1 7"))
            rstd(rsB, rb(f"norm{i}")[:, 0:TOK], 1.0 / D, "norm_by_scalar", f"rstd{i}", mid_event=f"read norm{i}")

        def small():
            act.wait_ge(*when("a + dt"))
            t0 = sgm[:, 0, 0:24].rearrange("p (a b) -> p a b", b=8)
            t1 = sgm[:, 0, 24:48].rearrange("p (a b) -> p a b", b=8)
            A.activation(t0, ba[:, :, 0:8], ACT.Abs)
            A.activation(t1, ba[:, :, 8:16], ACT.Abs).then_inc(mark("small_by_scalar", "small abs"), 1)
            act.wait_ge(*when("small abs"))
            tt = sgm[:, 0, 0:48]
            A.activation(tt, tt, ACT.Exp, scale=-1.0).then_inc(mark("small_by_scalar", "small exp"), 1)
            act.wait_ge(*when("small exp"))
            A.activation(tt, tt, ACT.Ln, bias=one).then_inc(mark("small_by_scalar", "small ln"), 1)
            A.activation(adt[:, 0, :], adt[:, 0, :], ACT.Exp).then_inc(mark("small_by_scalar", "exp A"), 1)
            act.wait_ge(*when("softplus"))
            A.activation(beta, beta, ACT.Exp).then_inc(mark("small_by_scalar", "beta"), 1)
            act.wait_ge(*when("b rest"))
            A.activation(eSs, rb("bcum")[:, 64:128].rearrange("p (s h) -> p s h", h=HB), ACT.Exp) \
                .then_inc(mark("small_by_scalar", "read bcum"), 1)
            A.activation(ebB, bcum, ACT.Exp)
            A.activation(eSd, blast, ACT.Exp)
            A.activation(elB, gt, ACT.Exp).then_inc(mark("small_by_scalar", "exp b"), 1)

        def step(s):
            s5, s4, s3, s2, s0 = s - 5, s - 4, s - 3, s - 2, s
            if 0 <= s5 < NPROJ:
                kind, i, _ = PROJ[s5]
                if kind == "cv" and i < 16:
                    act.wait_ge(*when(f"ssq{s5} ready"))
                    rstd(rsb[:, s5 % 2, :], rb(f"ssq{s5}")[:, 0:TOK], 1.0, "proj_by_scalar", f"rs{s5}",
                         bias=const("lnq") if i < 8 else None, mid_event=f"read ssq{s5}")
            if 0 <= s4 < NPROJ:
                kind, i, _ = PROJ[s4]
                if kind == "cv" and i < 16:
                    act.wait_ge(*when(f"act{s4}"))
                    q = (qB if i < 8 else kB)[:, i % 8, :]
                    A.activation(sqb[:, s4 % 2, :], q, ACT.Square) \
                        .then_inc(mark("proj_by_scalar", f"sq{s4}"), 1)
            if 0 <= s3 < NPROJ:
                kind, i, _ = PROJ[s3]
                if kind in ("cv", "ga", "zb", "gsa", "gsb"):
                    n = YW if kind == "cv" else TOK
                    act.wait_ge(*when(f"ls{s3}"))
                    sg = sgm[:, s3 % 4, 0:n]
                    A.activation(sg, sg, ACT.Exp).then_inc(mark("proj_by_scalar", f"sig{s3}"), 1)
            if 0 <= s2 < NPROJ:
                kind, i, _ = PROJ[s2]
                if kind in ("cv", "ga", "zb", "gsa", "gsb"):
                    n = YW if kind == "cv" else TOK
                    act.wait_ge(*when(f"tap3 {s2}" if kind == "cv" else f"y{s2}"))
                    for event in sg_free(s2 - 4):
                        act.wait_ge(*when(event))
                    lnexp(sgm[:, s2 % 4, 0:n], yb[:, s2 % 4, 0:n], P, "proj_by_scalar", f"ln{s2}")
            if s0 < NPROJ:
                kind, i, _ = PROJ[s0]
                act.wait_ge(*when(f"proj{s0} ready"))
                b = rb(f"proj{s0}")
                if kind == "qa":
                    A.activation(QKA[:, i, :], b[:, 0:TOK], ACT.Copy, scale=DKA ** -0.5) \
                        .then_inc(mark("proj_by_scalar", f"read proj{s0}"), 1)
                elif kind == "ka":
                    A.activation(QKA[:, 4 + i, :], b[:, 0:TOK], ACT.Copy) \
                        .then_inc(mark("proj_by_scalar", f"read proj{s0}"), 1)
                elif kind == "cv":
                    x = xp[:, s0 % 2]
                    act.wait_ge(*when("xp zero"))
                    act.wait_ge(*when("read cb1"))
                    if i >= 2:
                        act.wait_ge(*when(f"cc{i - 2}"))
                    A.activation(x[:, 3:3 + SEQ], b[:, 0:SEQ], ACT.Copy)
                    blk = x[:, SAMP0:XPW].rearrange("p (s t) -> p s t", t=7)
                    A.activation(blk[:, :, 0:3], cbT[:, i, :].rearrange("p (s t) -> p s t", t=3), ACT.Copy)
                    A.activation(blk[:, :, 3:7], b[:, SEQ:TOK].rearrange("p (s t) -> p s t", t=DT), ACT.Copy) \
                        .then_inc(mark("proj_by_scalar", f"read proj{s0}", f"xp{s0}"), 1)
                else:
                    for event in y_free(s0 - 4):
                        act.wait_ge(*when(event))
                    A.activation(yb[:, s0 % 4, 0:TOK], b[:, 0:TOK], ACT.Copy) \
                        .then_inc(mark("proj_by_scalar", f"read proj{s0}", f"y{s0}"), 1)

        def gla(m):
            o, n = TILES[m]
            t = f"gla{m} "
            act.wait_ge(*when(t + "logits"))
            lnexp(gA[0:n].rearrange("p a b -> p (a b)"), pm[4][0:n, :], n, "gla_by_scalar", t + "ln")
            act.wait_ge(*when(t + "cum"))
            sc = 1.0 / TAU
            cum = pm[5][:, 0:HA * n].rearrange("p (h t) -> p h t", t=n)
            A.activation(Eb[:, :, 0:n], cum, ACT.Exp, scale=sc).then_inc(mark("gla_by_scalar", t + "eb"), 1)
            act.wait_ge(*when(t + "D"))
            A.activation(Em[:, :, 0:n], Ep[:, :, 0:n], ACT.Exp, scale=-sc)
            A.activation(El[:, :, 0:n], El[:, :, 0:n], ACT.Exp, scale=sc) \
                .then_inc(mark("gla_by_scalar", t + "em"), 1)
            act.wait_ge(*when(t + "em"))
            A.activation(Ep[:, :, 0:n], Ep[:, :, 0:n], ACT.Exp, scale=sc) \
                .then_inc(mark("gla_by_scalar", t + "exps"), 1)
            act.wait_ge(*when(t + "ke transposed"))
            A.activation(keTa[0:n], pm[7][0:n, :].rearrange("p (h t) -> p h t", t=128), ACT.Copy) \
                .then_inc(mark("gla_by_scalar", t + "keT"), 1)
            if m == 0:
                for g in range(2):
                    act.wait_ge(*when(t + f"S{g} ready"))
                    A.activation(SA[:, 2 * g:2 * g + 2, :], pm[6 + g][:, :].rearrange("p (a b) -> p a b", b=256),
                                      ACT.Copy) \
                        .then_inc(mark("gla_by_scalar", t + f"S{g} read", *(["gla0 state"] if g else [])), 1)
            for g in range(2):
                act.wait_ge(*when(t + f"o{g} ready"))
                for hh in range(2):
                    h = 2 * g + hh
                    A.activation(oNa[0:n, 256 * h:256 * h + 256], pm[4 + g][0:n, 256 * hh:256 * hh + 256],
                                      ACT.Square, accum_out=ssum[0:n, h:h + 1]) \
                        .then_inc(mark("gla_by_scalar", *([t + "ss"] if h == HA - 1 else [])), 1)
            act.wait_ge(*when(t + "ss"))
            rstd(srs[0:n, 0:HA], ssum[0:n, 0:HA], 1.0 / DVA, "gla_by_scalar", t + "rstd", n=n)

        def gdn(m):
            o, n = TILES[m]
            t = f"gdn{m} "
            HG = 4
            for g in range(2):
                act.wait_ge(*when(t + f"D{g}"))
                ee = E[0:n, HG * g:HG * g + HG, 0:n]
                A.activation(ee, ee, ACT.Exp).then_inc(mark("gdn_by_scalar", t + f"E{g}"), 1)
            levels = LEVELS if m < 2 else 2
            for lv in range(1, levels):
                for g in range(2):
                    act.wait_ge(*when(t + f"Y{lv} {g} ready"))
                    A.activation(Y[0:n, HG * g:HG * g + HG, 0:n],
                                      pm[4 + g][0:n, 0:HG * n].rearrange("p (h t) -> p h t", t=n), ACT.Copy) \
                        .then_inc(mark("gdn_by_scalar", t + f"Y{lv} {g}"), 1)
            act.wait_ge(*when(t + "o0"))
            act.wait_ge(*when(t + "o1"))
            A.activation(sqo[0:n], E[0:n], ACT.Square).then_inc(mark("gdn_by_scalar", t + "squares"), 1)
            act.wait_ge(*when(t + "ssum"))
            rstd(srs[0:n, :], ssum[0:n, :], 1.0 / DVB, "gdn_by_scalar", t + "rstd", n=n)

        def router():
            act.wait_ge(*when("gd"))
            A.activation(rs_["dd"], rs_["dd"], ACT.Exp).then_inc(mark("router_by_scalar", "gexp"), 1)
            act.wait_ge(*when("ed"))
            A.activation(rs_["p1"], rs_["p1"], ACT.Exp).then_inc(mark("router_by_scalar", "eexp"), 1)

        def experts():
            for e in range(NE):
                for f in range(4):
                    act.wait_ge(*when(f"gu{e} {f} 0 ready"))
                    s = sg2[:, f, :]
                    lnexp(s, rb(f"gu{e} {f} 0")[:, 0:TOK], P, "expert_by_scalar", f"eln{e} {f}")
                    act.wait_ge(*when(f"els{e} {f}"))
                    A.activation(s, s, ACT.Exp).then_inc(mark("expert_by_scalar", f"esig{e} {f}"), 1)

        def final():
            for d in range(KD):
                act.wait_ge(*when(f"x3 {d}"))
                act.wait_ge(*when(f"gu{NE - 1} 3 1 ready"))
                A.activation(hT[:, d, :], xT[:, d, :], ACT.Square) \
                    .then_inc(mark("norm_by_scalar", f"square3 {d}"), 1)
            act.wait_ge(*when("norm3 ready"))
            act.wait_ge(*when("h2 7"))
            rstd(rsB, rb("norm3")[:, 0:TOK], 1.0 / D, "norm_by_scalar", "rstd3", mid_event="read norm3")

        run(locals())

    @block.gpsimd
    def _(pool):
        def head():
            pool.wait_ge(*when("x rows"))
            G.memset(ba, 0.0).then_inc(mark("cleared", "ba zero"), 1)
            G.memset(bcum, 0.0)
            G.memset(blast, 0.0).then_inc(mark("cleared", "bcum zero"), 1)
            G.memset(xp, 0.0).then_inc(mark("cleared", "xp zero"), 1)
            G.memset(raT[0:32, :], 1.0).then_inc(mark("cleared", "raT ones"), 1)

        def step(s):
            s1 = s - 1
            if 0 <= s1 < NPROJ and PROJ[s1][0] == "cv":
                i = PROJ[s1][1]
                pool.wait_ge(*when(f"xp{s1}"))
                x = xp[:, s1 % 2]
                G.tensor_copy(ccT[:, i, 0:3], x[:, SEQ:SEQ + 3])
                G.tensor_copy(ccT[:, i, 3:27].rearrange("p (s t) -> p s t", t=3),
                                   x[:, SAMP0:XPW].rearrange("p (s t) -> p s t", t=7)[:, :, 4:7]) \
                    .then_inc(mark("conv_tails", f"cc{i}"), 1)

        def gla(m):
            if m == 2:
                for s in range(NSEQ):
                    pool.wait_ge(*when("gla2 keT"))
                    if s >= 2:
                        pool.wait_ge(*when(f"gla state product {s - 2} 1"))
                    G.tensor_scalar(kem1[0:32, s % 2, :], keTa[0:32].rearrange("p a b -> p (a b)"),
                                         const("seq")[0:32, s:s + 1], None, ALU.mult) \
                        .then_inc(mark("masked_keys", f"kem1 {s}"), 1)

        def gdn(m):
            if m == 2:
                for s in range(NSEQ):
                    pool.wait_ge(*when("gdn2 ke0"))
                    pool.wait_ge(*when("gdn2 ke1"))
                    pool.wait_ge(*when("gdn2 y0"))
                    pool.wait_ge(*when("gdn2 y1"))
                    if s >= 2:
                        pool.wait_ge(*when(f"gdn state product {s - 2} 1"))
                    G.tensor_scalar(kem2[0:32, s % 2, :], ke[0:32].rearrange("p a b -> p (a b)"),
                                         const("seq")[0:32, s:s + 1], None, ALU.mult) \
                        .then_inc(mark("masked_keys", f"kem2 {s}"), 1)

        def router():
            pool.wait_ge(*when("merged 7"))
            pool.wait_ge(*when("wout7 ready"))
            G.memset(rt, 0.0).then_inc(mark("cleared", "rt zero"), 1)

        run(locals())

    @block.sync
    def _(sp):
        n = [0]

        def load(dst, src, event, kind=None):
            kind = kind or f"loaded_{event.replace(' ', '_')}"
            sp.dma_start(dst, src).then_inc(mark(kind, event, by=16), 16)

        load(cst, I["const"], "consts")
        load(crow[0:NC9, :], I["cc"], "c rows")
        for i, (k, (r, c)) in enumerate(VEC.items()):
            src = {"b_ada": I["b_ada"], "norm1": I["norm1_w"], "norm2": I["norm2_w"], "final": I["final_norm_w"],
                   "gla_norm": I["gla_norm_w"], "gdn_norm": I["gdn_norm_w"]}[k]
            sp.dma_start(vrow[r:r + c, :], src.rearrange("(n p) -> n p", p=P)) \
                .then_inc(mark("loaded_vectors", by=16), 16)
        sp.dma_start(cvrow[0:96, :], I["w_conv"].rearrange("t (n p) -> (t n) p", p=P)) \
            .then_inc(mark("loaded_vectors", "vec rows", by=16), 16)
        sp.dma_start(xr[:, 0:2, :], I["x_prompt"].rearrange("(m p) d -> p m d", p=P)) \
            .then_inc(mark("loaded_x", by=16), 16)
        sp.dma_start(xr[0:32, 2, :], I["x_sample"]).then_inc(mark("loaded_x", "x rows", by=16), 16)
        load(cbrow[0:24, :], I["state_conv"], "cb rows")
        sp.dma_start(wsm[:, :, 0:RANK], I["w_in"][:, 3072:3088].rearrange("(k p) n -> p k n", p=P)) \
            .then_inc(mark("loaded_small", by=16), 16)
        sp.dma_start(wsm[:, :, 16:32], I["w_in"][:, 7184:7200].rearrange("(k p) n -> p k n", p=P)) \
            .then_inc(mark("loaded_small", "small weights", by=16), 16)
        sp.dma_start(wa2[0:RANK, :], I["w_gla_a2"]).then_inc(mark("loaded_wa2", by=16), 16)
        sp.dma_start(wa2[RANK:RANK + 1, :], I["b_gla_a"].rearrange("(a n) -> a n", a=1)) \
            .then_inc(mark("loaded_wa2", "wa2", by=16), 16)
        sp.dma_start(adt[:, 0, :], I["gdn_A_log"].rearrange("(a n) -> a n", a=1).to_broadcast([P, HB])) \
            .then_inc(mark("loaded_adt", by=16), 16)
        sp.dma_start(adt[:, 1, :], I["gdn_dt_bias"].rearrange("(a n) -> a n", a=1).to_broadcast([P, HB])) \
            .then_inc(mark("loaded_adt", "adt", by=16), 16)
        sp.dma_start(rtw[:, :, 0:4], I["w_group_router"].rearrange("(k p) n -> p k n", p=P)) \
            .then_inc(mark("loaded_router", by=16), 16)
        sp.dma_start(rtw[:, :, 4:20], I["w_expert_router"].rearrange("(k p) n -> p k n", p=P)) \
            .then_inc(mark("loaded_router", "router weights", by=16), 16)
        sp.dma_start(rtb[:, 0:4], I["b_group_router"].rearrange("(a n) -> a n", a=1).to_broadcast([P, 4])) \
            .then_inc(mark("loaded_rtb", by=16), 16)
        sp.dma_start(rtb[:, 4:20], I["b_expert_router"].rearrange("(a n) -> a n", a=1).to_broadcast([P, 16])) \
            .then_inc(mark("loaded_rtb", "router bias", by=16), 16)
        outs = []
        for n, (name, src) in enumerate(chunks):
            if n >= RING:
                prev = chunks[n - RING][0]
                if prev[0] in ("sgla", "sgdn"):
                    c = prev[1]
                    for s in (2 * c, 2 * c + 1):
                        for g in range(2):
                            sp.wait_ge(*when(f"{'gla' if prev[0] == 'sgla' else 'gdn'} state {s} {g}"))
                    if prev[0] == "sgla":
                        dst = O["gla_s"][2 * c:2 * c + 2].rearrange("s h k v -> k (s h) v")
                    else:
                        dst = O["gdn_s"][2 * c:2 * c + 2].rearrange("s (h a) k v -> k (s h) a v", a=2)
                    s_ = slot(prev)
                    if prev[0] == "sgdn":
                        s_ = s_.rearrange("p k (a v) -> p k a v", a=2)
                    sp.dma_start(dst, s_) \
                        .then_inc(mark(f"stored_slot{(n - RING) % RING}", f"stored {n - RING}", by=16), 16)
                    sp.wait_ge(*when(f"stored {n - RING}"))
                else:
                    sp.wait_ge(*when(used(prev)))
            d_ = slot(name)
            if name[0] == "sgdn":
                d_ = d_.rearrange("p k (a v) -> p k a v", a=2)
            sp.dma_start(d_, src).then_inc(mark(f"loaded_slot{n % RING}", loaded(name), by=16), 16)
        for g in range(6):
            sp.wait_ge(*when(f"read cvo{g}"))
        sp.dma_start(O["conv_p"], newconv[0:3, :]).then_inc(mark("stored", by=16), 16)
        sp.dma_start(O["conv_s"], newconv[3:27, :]).then_inc(mark("stored", by=16), 16)
        sp.dma_start(O["gla_p"].rearrange("h k v -> k h v"), SA).then_inc(mark("stored", by=16), 16)
        sp.dma_start(O["gdn_p"].rearrange("h k v -> k h v"), SB) \
            .then_inc(mark("stored", "small outputs stored", by=16), 16)
        for e in range(NE):
            for w_ in range(3):
                c = 3 * e + w_
                if c == 0:
                    sp.wait_ge(*when("merged 7"))
                    sp.wait_ge(*when("wout7 ready"))
                    sp.wait_ge(*when("read wout7"))
                    sp.wait_ge(*when("x2 7"))
                    sp.wait_ge(*when("small outputs stored"))
                if c >= 8:
                    sp.wait_ge(*when(f"ewused{(c - 8) // 3} {(c - 8) % 3}"))
                g, x = e // EPG, e % EPG
                src = (I["w_exp_gate"][g, x], I["w_exp_up"][g, x], I["w_exp_down"][g, x])[w_]
                sp.dma_start(EW[:, c % 8].rearrange("p (k n) -> p k n", k=4 if w_ == 2 else KD),
                                  src.rearrange("(k p) n -> p k n", p=P)) \
                    .then_inc(mark(f"loaded_expert_slot{c % 8}", f"ew{e} {w_}", by=16), 16)
        for g in range(2):
            for m in range(3):
                sp.wait_ge(*when(f"read y{g}{m}"))
            cs = slice(512 * g, 512 * g + 512)
            sp.dma_start(O["y_p"].rearrange("(m p) d -> p m d", p=P)[:, :, cs], yrow[:, 0:2, cs]) \
                .then_inc(mark("stored", by=16), 16)
            sp.dma_start(O["y_s"][:, cs], yrow[0:32, 2, cs]) \
                .then_inc(mark("stored", f"all stored{g}", by=16), 16)
        sp.wait_ge(*when("all stored1"))

    return S.marks


_SHAPES = {
    "y_p": (SEQ, D), "y_s": (NSEQ * DT, D), "gla_p": (HA, DKA, DVA), "gdn_p": (HB, DKB, DVB), "conv_p": (3, 3072),
    "gla_s": (NSEQ, HA, DKA, DVA), "gdn_s": (NSEQ, HB, DKB, DVB), "conv_s": (NSEQ * 3, 3072),
}
_NAMES = ("w_ada", "b_ada", "norm1_w", "w_in", "w_gla_a2", "b_gla_a", "gla_norm_w", "w_conv", "gdn_A_log",
          "gdn_dt_bias", "gdn_norm_w", "w_out", "norm2_w", "w_group_router", "b_group_router", "w_expert_router",
          "b_expert_router", "w_exp_gate", "w_exp_up", "w_exp_down")


def lay_out(inputs):
    a = {k: np.ascontiguousarray(np.asarray(inputs[k])[0]) for k in _NAMES}
    a["final_norm_w"] = np.asarray(inputs["final_norm_w"])
    a["x_prompt"] = np.asarray(inputs["x_prompt"]).reshape(SEQ, D)
    a["x_sample"] = np.asarray(inputs["x_sample"]).reshape(NSEQ * DT, D)
    a["cc"] = np.concatenate([np.asarray(inputs["c_prompt"]), np.asarray(inputs["c_sample"])], axis=0)
    a["state_gla"] = np.asarray(inputs["state_gla"])[0]
    a["state_gdn"] = np.asarray(inputs["state_gdn"])[0]
    a["state_conv"] = np.asarray(inputs["state_conv"]).reshape(NSEQ * 3, 3072)
    a["const"] = CONST
    return {k: np.ascontiguousarray(v) for k, v in a.items()}


def kernel(**inputs):
    import concourse.bacc as bacc
    from concourse.bass_utils import run_bass_kernel_spmd

    arrays = lay_out(inputs)
    counts = None
    for _ in range(2):
        nc = bacc.Bacc("TRN2", target_bir_lowering=False, num_devices=1)
        ins = {k: nc.dram_tensor("in_" + k, v.shape, F32, kind="ExternalInput").ap() for k, v in arrays.items()}
        outs = {k: nc.dram_tensor("out_" + k, s, F32, kind="ExternalOutput").ap() for k, s in _SHAPES.items()}
        counts = program(nc, ins, outs, counts)
    r = run_bass_kernel_spmd(nc, [{"in_" + k: v for k, v in arrays.items()}], core_ids=[0]).results[0]
    o = {k: r["out_" + k] for k in _SHAPES}
    return (o["y_p"].reshape(1, SEQ, D), o["y_s"].reshape(NSEQ, DT, D),
            o["gla_p"].reshape(1, 1, HA, DKA, DVA), o["gdn_p"].reshape(1, 1, HB, DKB, DVB),
            o["conv_p"].reshape(1, 1, 3, 3072), o["gla_s"].reshape(1, NSEQ, HA, DKA, DVA),
            o["gdn_s"].reshape(1, NSEQ, HB, DKB, DVB), o["conv_s"].reshape(1, NSEQ, 3, 3072))
```

```python
from contextlib import ExitStack

import numpy as np

import concourse.bass as bass
import concourse.mybir as mybir

F32 = mybir.dt.float32
ALU = mybir.AluOpType
ACT = mybir.ActivationFunctionType
AX = mybir.AxisListType.X

P = 128
D = 1024
KD = D // P
SEQ, NSEQ, DT = 256, 8, 4
TOK = SEQ + NSEQ * DT
NC9 = 1 + NSEQ
TILES = ((0, 128), (128, 128), (256, 32))
HA, DKA, DVA = 4, 128, 256
HB, DKB, DVB = 8, 128, 128
RANK = 16
TAU = 16.0
TAPS = 4
NG, EPG = 4, 4
NE = NG * EPG
DE = 512
EPS = 1e-6
CONV0 = 3088
CT = 24
XPW = 3 + SEQ + NSEQ * (3 + DT)
YW = XPW - 3
SAMP0 = 3 + SEQ
LEVELS = 7

PROJ = ([("qa", i, 128 * i) for i in range(4)] + [("ka", i, 512 + 128 * i) for i in range(4)]
        + [("va", i, 1024 + 128 * i) for i in range(8)]
        + [("cv", i, CONV0 + 128 * i) for i in range(CT)]
        + [("ga", i, 2048 + 128 * i) for i in range(8)]
        + [("gsa", i, 7200 + 128 * i) for i in range(8)]
        + [("zb", i, 6160 + 128 * i) for i in range(8)]
        + [("gsb", i, 8224 + 128 * i) for i in range(8)])
NPROJ = len(PROJ)
NPROJ_CV = 32
SLOTS = 64
PAIR = 2 * SLOTS
MORE = -(-(TOK - SLOTS) // PAIR)
OVER = 2 * TOK // (SLOTS + 1)
CW = 256
RING = 5

VEC = {"b_ada": (0, 48), "norm1": (48, 8), "norm2": (56, 8), "final": (64, 8), "gla_norm": (72, 2),
       "gdn_norm": (74, 1)}
NVEC = 75


def constants():
    p = np.arange(P)
    parts = {"ident": np.eye(P), "ones": np.ones((P, P)), "tri": (p[:, None] <= p[None, :]) * 1.0}
    for lv in range(LEVELS):
        b = 1 << lv
        s, t = p[:, None], p[None, :]
        parts[f"level{lv}"] = ((s // (2 * b) == t // (2 * b)) & (s % (2 * b) < b) & (t % (2 * b) >= b)) * 1.0
    q = np.arange(32)
    same = (q[:, None] // DT == q[None, :] // DT)
    pad = lambda a: np.concatenate([a, np.zeros((P - a.shape[0], a.shape[1]))])
    parts["tri_s"] = pad(same & (q[:, None] <= q[None, :]))
    parts["same_s"] = pad(same)
    parts["seq"] = pad(q[:, None] // DT == np.arange(NSEQ)[None, :])
    parts["eps"] = np.full((P, 1), EPS)
    parts["lnq"] = np.full((P, 1), np.log(DKB ** -0.5))
    parts["iota"] = np.tile(np.arange(float(P))[None, :], (P, 1))
    r, e = np.arange(MORE * NE) // NE, np.arange(MORE * NE) % NE
    parts["over_at"] = pad((SLOTS + PAIR * r * 1.0)[:, None])
    parts["over_expert"] = pad(np.tile((1.0 * e)[:, None], (1, P)))
    parts["over_base"] = pad(np.tile((SLOTS + PAIR * r * 1.0)[:, None], (1, P)))
    off, at = 0, {}
    for k, a in parts.items():
        at[k] = (off, a.shape[1])
        off += a.shape[1]
    return np.concatenate([np.asarray(a, np.float32) for a in parts.values()], axis=1), at


CONST, CONST_AT = constants()


class Signals:

    def __init__(self, nc, ctx, counts):
        self.nc, self.ctx, self.counts = nc, ctx, counts
        self.sems, self.value, self.marks = {}, {}, {}

    def sem(self, kind):
        if kind not in self.sems:
            self.sems[kind] = self.ctx.enter_context(self.nc.semaphore(kind))
            self.value[kind] = 0
        return self.sems[kind]

    def mark(self, kind, *events, by=1):
        sem = self.sem(kind)
        self.value[kind] += by
        for event in events:
            assert event not in self.marks, event
            self.marks[event] = (kind, self.value[kind])
        return sem

    def when(self, event):
        kind, value = ("first_building", 1) if self.counts is None else self.counts[event]
        return self.sem(kind), value



def program(nc, ins, outs, known=None):
    ctx = ExitStack()
    with ctx:
        return _program(nc, ctx, ins, outs, known)


def _program(nc, ctx, I, O, known):
    S = Signals(nc, ctx, known)
    mark, when = S.mark, S.when

    ARENA = 53200
    arena = ctx.enter_context(nc.sbuf_tensor("arena", [P, ARENA], F32))
    top = [0]

    def carve(*shape, at=None):
        n = int(np.prod(shape))
        o = top[0] if at is None else at
        if at is None:
            top[0] += n
        assert o + n <= ARENA, (o, n)
        v = arena[:, o:o + n]
        if len(shape) == 2:
            v = v.rearrange("p (a b) -> p a b", b=shape[1])
        elif len(shape) == 3:
            v = v.rearrange("p (a b c) -> p a b c", b=shape[1], c=shape[2])
        return v

    xT = carve(KD, TOK)
    hT = carve(KD, TOK)
    modT = carve(48, NC9)
    A1, A2 = carve(KD, NC9), carve(KD, NC9)
    csT = carve(KD, NC9)
    vecT = carve(NVEC)
    cst = carve(CONST.shape[1])
    rsB = carve(TOK)
    rtw = carve(KD, 20)
    rtb = carve(20)
    gs = carve(2, 32)
    persistent = top[0]

    def const(name):
        o, n = CONST_AT[name]
        return cst[:, o:o + n]

    ident, ones, tri = const("ident"), const("ones"), const("tri")
    TRI = (tri, tri, const("tri_s"))
    LAST = (ones, ones, const("same_s"))

    W = carve(RING, KD, CW)
    GA = carve(KD, TOK)
    QKA = carve(KD, TOK)
    GB_at = top[0]
    GB = carve(KD, TOK)
    qB = carve(KD, TOK)
    mixer_only = top[0]
    kB = carve(KD, TOK)
    vA_at = top[0]
    vA = carve(3, D)
    vB = carve(3, D)
    convT = carve(96)
    cbT = carve(CT, 24)
    ccT = carve(CT, 27)
    wsm = carve(KD, 32)
    raT_at = top[0]
    raT = carve(TOK)
    wa2_at = top[0]
    wa2 = carve(512)
    ba = carve(3, 16)
    beta = carve(3, HB)
    gB = carve(3, HB)
    gt = carve(3, HB)
    adt = carve(2, HB)
    bcum = carve(3, HB)
    blast = carve(3, HB)
    ebB, elB, eSd = carve(3, HB), carve(3, HB), carve(3, HB)
    gseq = carve(NSEQ, HB)
    eSs = carve(NSEQ, HB)
    xp = carve(2, XPW)
    yb = carve(4, YW)
    sgm = carve(4, YW)
    sqb = carve(2, TOK)
    rsb = carve(2, TOK)
    SA = carve(HA, DVA)
    SB = carve(HB, DVB)
    ebl = carve(HA, NSEQ)
    ssum = carve(HB)
    srs = carve(HB)
    oSt = carve(KD, 32, at=raT_at)
    oSt2 = carve(KD, 32, at=wa2_at)
    work = top[0]
    E = carve(HB, P)
    AT = carve(HB, P)
    LT = carve(HB, P)
    Lm = carve(HB, P)
    Y = carve(HB, P)
    X_at = top[0]
    X = carve(HB, 2, P)
    R = carve(HB, P)
    tg = carve(HB, P, at=X_at)
    kem2 = carve(2, D, at=X_at)
    ke = LT
    gA = carve(HA, P, at=work)
    Eb = carve(HA, P, at=work + 512)
    Ep = carve(HA, P, at=work + 1024)
    Em = carve(HA, P, at=work + 1536)
    El = carve(HA, P, at=work + 2048)
    ATa = carve(HA, P, at=work + 2560)
    keTa = carve(HA, P, at=work + 3072)
    oNa = carve(D, at=work + 3584)
    kem1 = carve(2, 512, at=work + 4608)
    oNb = Y.rearrange("p a b -> p (a b)")
    sqo = Lm
    xr = vB
    cbrow = carve(3072, at=persistent + RING * KD * CW)
    crow = carve(D, at=GB_at)
    csx = carve(2, D, at=vA_at + 0)
    vrow = carve(P, at=GB_at + 1024)
    cvrow = carve(P, at=GB_at + 1152)
    newconv = carve(3072, at=vA_at)
    EW = carve(3, 2, 4096, at=mixer_only)
    yrow = carve(3, D, at=mixer_only)
    top[0] = persistent
    h2t = carve(3, D)
    acc = carve(KD, TOK)
    Dg, Dc = carve(3, 2, SLOTS), carve(3, 2, SLOTS)
    DT_ = carve(TOK)
    hg = carve(KD, PAIR)
    hid = carve(DE)
    sg2 = carve(DE)
    hidT = carve(4, PAIR)
    yt = carve(D)
    rt = carve(3, 20)
    rs_ = {}
    for n in ["gmax", "gden", "gw", "hit", "idx", "gsel", "el", "emax", "p1", "h1", "p2", "within", "tmp", "i1",
              "w1", "w2", "dd", "hh"]:
        rs_[n] = carve(3, 4)
    el16 = carve(3, 16)
    sel = carve(3, NE)
    comb, rank = carve(3, NE + 2), carve(3, NE + 2)
    sel4 = carve(3, MORE * NE)
    over = carve(40)
    oneh = carve(OVER)
    expB, rankO, combO = carve(OVER), carve(3, OVER), carve(3, OVER)
    rankJ, combJ = carve(3), carve(3)
    hitE = carve(NE)
    tabf = carve(2 * OVER + 2)
    tab = carve(2 * OVER + 2).bitcast(mybir.dt.int32)
    assert top[0] <= mixer_only

    pm = [ctx.enter_context(nc.psum_tensor(f"bank{i}", [P, 512], F32)) for i in range(8)]

    T, V, A, G = nc.tensor, nc.vector, nc.scalar, nc.gpsimd
    block = ctx.enter_context(nc.Block())

    def cols(w, c0, n=CW):
        return w[:, c0:c0 + n].rearrange("(k p) n -> p k n", p=P)

    chunks = []
    chunk_of = {}

    def add(name, src):
        chunk_of[name] = len(chunks)
        chunks.append((name, src))

    def slot(name):
        return W[:, chunk_of[name] % RING]

    def loaded(name):
        return f"chunk {chunk_of[name]}"

    def used(name):
        return f"used {chunk_of[name]}"

    GLA_AT = {23: 0, 29: 1, 37: 2}
    GDN_AT = {47: 0, 57: 1, 67: 2}
    schedule = [("head",)] + [("ada", c) for c in range(8)] + [("norm", 1), ("small",)]
    for s in range(NPROJ + 6):
        schedule.append(("step", s))
        if s in GLA_AT:
            schedule.append(("gla", GLA_AT[s]))
        if s == 46:
            schedule.append(("conv_out",))
        if s in GDN_AT:
            schedule.append(("gdn", GDN_AT[s]))
    schedule += [("ada", c) for c in range(8, 24)]
    schedule += [("merge",), ("wout",), ("norm", 2), ("router",), ("experts",), ("final",)]

    for item in schedule:
        kind, c = item[0], item[-1]
        if kind == "ada":
            add(("ada", c), cols(I["w_ada"], CW * c))
        elif kind == "step" and c % 2 == 0 and c < NPROJ:
            add(("win", c), cols(I["w_in"], PROJ[c][2]))
        elif item == ("gla", 2):
            for i in range(4):
                add(("sgla", i), I["state_gla"][2 * i:2 * i + 2].rearrange("s h k v -> k (s h) v"))
        elif item == ("gdn", 2):
            for i in range(4):
                add(("sgdn", i), I["state_gdn"][2 * i:2 * i + 2].rearrange("s (h a) k v -> k (s h) a v", a=2))
        elif kind == "wout":
            for i in range(4):
                add(("wout", i), cols(I["w_out"], CW * i))

    ring_names = []

    def ring_bank(name):
        n = len(ring_names)
        if n >= 4:
            PE[0].wait_ge(*when(f"read {ring_names[n - 4]}"))
        ring_names.append(name)
        banks[name] = n % 4
        return pm[n % 4]

    banks = {} if known is None else known["#banks"]
    if known is None:
        S.marks["#banks"] = banks
    PE = [None]
    free = {}

    def take(b, reader):
        if b in free:
            PE[0].wait_ge(*when(free[b]))
        free[b] = reader
        return pm[b]

    def rb(name):
        return pm[banks.get(name, 0)]

    def mm(out, lhsT, rhs, start=True, stop=True):
        return T.matmul(out, lhsT, rhs, start=start, stop=stop)

    def tr(out, in_, n):
        return T.transpose(out, in_, ident[0:n, 0:n])

    def bc(ap, n):
        return ap.unsqueeze(2).to_broadcast([ap.shape[0], ap.shape[1], n])

    def mid(ap, n):
        return ap.unsqueeze(1).to_broadcast([ap.shape[0], n, ap.shape[1]])

    def y_free(s):
        kind = PROJ[s][0] if s >= 0 else None
        if kind in ("qa", "ka", None):
            return []
        return [f"tr{s} ready"] if kind == "va" else [f"act{s}", f"ln{s}"]

    def sg_free(s):
        kind = PROJ[s][0] if s >= 0 else None
        if kind in ("qa", "ka", "va", None):
            return []
        return [f"act{s}"] + ([f"tr{s} ready"] if kind == "cv" and PROJ[s][1] >= 16 else [])

    def named(prefix, names):
        return {n: ctx.enter_context(nc.semaphore(f"{prefix}_{n}")) for n in names}

    STEPS = ("dispatch", "scatter_matrix", "scatter_matrix_read", "gathered", "gather_read0", "gather_read1", "gate",
             "up", "softplus_step", "softplus", "log_sigmoid", "sigmoid", "silu", "hidden", "turned", "turned_read",
             "down", "down_read0", "down_read1", "scattered", "added", "picked")
    main_sems, over_sems = named("expert", STEPS), named("overflow", STEPS)
    expert_loaded = [ctx.enter_context(nc.semaphore(f"expert_loaded{i}")) for i in range(3)]
    over_loaded = [ctx.enter_context(nc.semaphore(f"overflow_loaded{i}")) for i in range(3)]

    def overflow(eng, one_block):
        blocks = eng.value_load(tab[0:1, 0:1], min_val=0, max_val=OVER)
        with eng.If(blocks > 0):
            with eng.Fori(0, blocks) as j:
                one_block(j)

    def run(fns):
        for item in schedule:
            f = fns.get(item[0])
            if f is not None:
                f(*item[1:])

    @block.tensor
    def _(pe):
        PE[0] = pe

        def head():
            pe.wait_ge(*when("consts"))
            pe.wait_ge(*when("vec rows"))
            b = ring_bank("vec")
            tr(b[:, 0:NVEC], vrow[0:NVEC, :], NVEC)
            tr(b[:, 128:224], cvrow[0:96, :], 96).then_inc(mark("head_transposed", "vec ready"), 1)
            pe.wait_ge(*when("x rows"))
            for d in range(KD):
                b = ring_bank(f"x{d}")
                for m, (o, n) in enumerate(TILES):
                    last = tr(b[:, o:o + n], xr[0:n, m, 128 * d:128 * d + 128], n)
                last.then_inc(mark("head_transposed", f"x{d} ready"), 1)
            pe.wait_ge(*when("cb rows"))
            for g in range(2):
                b = ring_bank(f"cb{g}")
                for j in range(12):
                    c = 12 * g + j
                    last = tr(b[:, 24 * j:24 * j + 24], cbrow[0:24, 128 * c:128 * c + 128], 24)
                last.then_inc(mark("head_transposed", f"cb{g} ready"), 1)
            b = ring_bank("c")
            for k in range(KD):
                last = tr(b[:, NC9 * k:NC9 * k + NC9], crow[0:NC9, 128 * k:128 * k + 128], NC9)
            last.then_inc(mark("head_transposed", "c ready"), 1)

        def ada(c):
            pe.wait_ge(*when(loaded(("ada", c))))
            pe.wait_ge(*when("read c"))
            w = slot(("ada", c))
            b = ring_bank(f"ada{c}")
            for j in range(2):
                for k in range(KD):
                    last = mm(b[:, NC9 * j:NC9 * j + NC9], w[:, k, 128 * j:128 * j + 128], csT[:, k, :],
                              k == 0, k == KD - 1)
            last.then_inc(mark("ada_products", f"ada{c} ready", used(("ada", c))), 1)

        def norm(i):
            b = ring_bank(f"norm{i}")
            for d in range(KD):
                pe.wait_ge(*when(f"square{i} {d}"))
                last = mm(b[:, 0:TOK], ones, hT[:, d, :], d == 0, d == KD - 1)
            last.then_inc(mark("norm_sums", f"norm{i} ready"), 1)

        def small():
            pe.wait_ge(*when("small weights"))
            for d in range(KD):
                pe.wait_ge(*when(f"h1 {d}"))
            b = ring_bank("ra")
            for k in range(KD):
                last = mm(b[0:RANK, 0:TOK], wsm[:, k, 0:RANK], hT[:, k, :], k == 0, k == KD - 1)
            last.then_inc(mark("small_products", "ra ready"), 1)
            b = ring_bank("ba")
            for m, (o, n) in enumerate(TILES):
                for k in range(KD):
                    last = mm(b[0:n, 16 * m:16 * m + 16], hT[:, k, o:o + n], wsm[:, k, 16:32], k == 0, k == KD - 1)
            last.then_inc(mark("small_products", "ba ready"), 1)
            pe.wait_ge(*when("g"))
            b = ring_bank("bcum")
            for m, (o, n) in enumerate(TILES):
                mm(b[0:n, 8 * m:8 * m + 8], TRI[m][0:n, 0:n], gB[0:n, m, :])
                mm(b[0:n, 32 + 8 * m:40 + 8 * m], LAST[m][0:n, 0:n], gB[0:n, m, :])
            last = mm(b[:, 64:64 + 64], ones[0:32, :], gseq[0:32].rearrange("p s h -> p (s h)"))
            last.then_inc(mark("small_products", "bcum ready"), 1)

        def step(s):
            if s < NPROJ:
                name = ("win", s - s % 2)
                pe.wait_ge(*when(loaded(name)))
                w = slot(name)
                j = s % 2
                b = ring_bank(f"proj{s}")
                for k in range(KD):
                    last = mm(b[:, 0:TOK], w[:, k, 128 * j:128 * j + 128], hT[:, k, :], k == 0, k == KD - 1)
                last.then_inc(mark("projected", f"proj{s} ready", *([used(name)] if j == 1 else [])), 1)
            s5 = s - 5
            if 0 <= s5 < NPROJ:
                kind, i, _ = PROJ[s5]
                if kind == "cv" and i < 16:
                    pe.wait_ge(*when(f"sq{s5}"))
                    b = ring_bank(f"ssq{s5}")
                    mm(b[:, 0:TOK], ones, sqb[:, s5 % 2, :]).then_inc(mark("norm_sums", f"ssq{s5} ready"), 1)
                if kind == "va" or (kind == "cv" and i >= 16):
                    pe.wait_ge(*when(f"y{s5}" if kind == "va" else f"act{s5}"))
                    b = ring_bank(f"tr{s5}")
                    src = yb[:, s5 % 4] if kind == "va" else sgm[:, s5 % 4]
                    for m, (o, n) in enumerate(TILES):
                        last = tr(b[0:n, 128 * m:128 * m + 128], src[:, o:o + n], 128)
                    last.then_inc(mark("transposed", f"tr{s5} ready"), 1)

        def gla(m):
            o, n = TILES[m]
            t = f"gla{m} "
            pe.wait_ge(*when("wa2"))
            b = take(4, t + "logits read")
            mm(b[0:n, :], raT[0:RANK + 1, o:o + n], wa2[0:RANK + 1, :]) \
                .then_inc(mark("gla_products", t + "logits"), 1)
            pe.wait_ge(*when(t + "log decay"))
            b = take(5, t + "cum read")
            for h in range(HA):
                last = mm(b[:, n * h:n * h + n], gA[0:n, h, :], TRI[m][0:n, 0:n])
            last.then_inc(mark("gla_products", t + "cum"), 1)
            pe.wait_ge(*when(t + "qq"))
            pe.wait_ge(*when(t + "kk"))
            b = take(6, t + "A read")
            for h in range(HA):
                last = mm(b[0:n, n * h:n * h + n], Em[:, h, 0:n], Ep[:, h, 0:n])
            last.then_inc(mark("gla_products", t + "A"), 1)
            pe.wait_ge(*when(t + "ke"))
            b = take(7, t + "keT")
            for h in range(HA):
                last = tr(b[0:n, 128 * h:128 * h + 128], El[:, h, 0:n], 128)
            last.then_inc(mark("gla_products", t + "ke transposed"), 1)
            if m == 2:
                pe.wait_ge(*when(t + "qb"))
                b = take(6, t + "oS")
                for c in range(4):
                    pe.wait_ge(*when(loaded(("sgla", c))))
                    w = slot(("sgla", c)).rearrange("p (s h) v -> p s h v", h=HA)
                    for s2 in range(2):
                        s = 2 * c + s2
                        for h in range(HA):
                            for half in range(2):
                                j = 32 * (2 * h + half) + DT * s
                                last = mm(b[:, j:j + DT], w[:, s2, h, 128 * half:128 * half + 128],
                                          Eb[:, h, DT * s:DT * s + DT])
                last.then_inc(mark("gla_products", t + "oS ready"), 1)
                pe.wait_ge(*when(t + "oS"))
            pe.wait_ge(*when(t + "AT"))
            for g in range(2):
                b = take(4 + g, t + f"o{g} read")
                for hh in range(2):
                    h = 2 * g + hh
                    out = b[0:n, 256 * hh:256 * hh + 256]
                    last = mm(out, ATa[0:n, h, 0:n], vA[0:n, m, 256 * h:256 * h + 256], True, m == 0)
                    if m == 1:
                        last = mm(out, Eb[:, h, 0:n], SA[:, h, :], False, True)
                    if m == 2:
                        for half in range(2):
                            last = mm(out[:, 128 * half:128 * half + 128], oSt[:, 2 * h + half, :], ident,
                                      False, half == 1)
                last.then_inc(mark("gla_products", t + f"o{g} ready"), 1)
            pe.wait_ge(*when(t + "keT"))
            if m < 2:
                for g in range(2):
                    b = take(6 + g, t + f"S{g} read")
                    for hh in range(2):
                        h = 2 * g + hh
                        last = mm(b[:, 256 * hh:256 * hh + 256], keTa[0:n, h, :], vA[0:n, m, 256 * h:256 * h + 256])
                    last.then_inc(mark("gla_products", t + f"S{g} ready"), 1)
            else:
                for s in range(NSEQ):
                    pe.wait_ge(*when(f"kem1 {s}"))
                    for g in range(2):
                        b = take(6 + g, f"gla state {s} {g}")
                        for hh in range(2):
                            h = 2 * g + hh
                            last = mm(b[:, 256 * hh:256 * hh + 256], kem1[0:32, s % 2, 128 * h:128 * h + 128],
                                      vA[0:32, 2, 256 * h:256 * h + 256])
                        last.then_inc(mark("gla_products", f"gla state product {s} {g}"), 1)
            for g in range(2):
                pe.wait_ge(*when(t + "oN"))
                b = take(4 + g, t + f"oT{g}")
                for j in range(4):
                    c = 4 * g + j
                    last = tr(b[:, 128 * j:128 * j + n], oNa[0:n, 128 * c:128 * c + 128], n)
                last.then_inc(mark("gla_products", t + f"oT{g} ready"), 1)

        def conv_out():
            for i in range(CT):
                pe.wait_ge(*when(f"cc{i}"))
            for g in range(6):
                b = ring_bank(f"cvo{g}")
                for j in range(4):
                    last = tr(b[0:27, 128 * j:128 * j + 128], ccT[:, 4 * g + j, :], 128)
                last.then_inc(mark("transposed", f"cvo{g} ready"), 1)

        def gdn(m):
            o, n = TILES[m]
            t = f"gdn{m} "
            HG = 4
            pe.wait_ge(*when(t + "tg"))
            for g in range(2):
                b = take(4 + g, t + f"D{g}")
                mm(b[0:n, 0:HG * n], ones[0:n, 0:n], tg[0:n, HG * g:HG * g + HG, 0:n]) \
                    .then_inc(mark("gdn_products", t + f"bc{g}"), 1)
            for g in range(2):
                b = take(6 + g, t + f"KK{g} read")
                for j in range(HG):
                    h = HG * g + j
                    last = mm(b[0:n, n * j:n * j + n], kB[:, h, o:o + n], kB[:, h, o:o + n])
                last.then_inc(mark("gdn_products", t + f"KK{g}"), 1)
            for g in range(2):
                b = take(4 + g, t + f"AT{g}")
                for j in range(HG):
                    h = HG * g + j
                    last = mm(b[0:n, n * j:n * j + n], kB[:, h, o:o + n], qB[:, h, o:o + n])
                last.then_inc(mark("gdn_products", t + f"QK{g}"), 1)
            levels = LEVELS if m < 2 else 2
            for lv in range(levels):
                for g in range(2):
                    pe.wait_ge(*when(t + f"Lm{lv} {g}"))
                    b = take(4 + g, t + f"Y{lv} {g}")
                    for j in range(HG):
                        h = HG * g + j
                        rhs = ident[0:n, 0:n] if lv == 0 else X[0:n, h, 1, 0:n]
                        last = mm(b[0:n, n * j:n * j + n], Lm[0:n, h, 0:n], rhs)
                    last.then_inc(mark("gdn_products", t + f"Y{lv} {g} ready"), 1)
                if lv == 0:
                    continue
                for g in range(2):
                    pe.wait_ge(*when(t + f"Y{lv} {g}"))
                    b = take(6 + g, t + f"XT{lv} {g}")
                    for j in range(HG):
                        h = HG * g + j
                        last = mm(b[0:n, n * j:n * j + n], Y[0:n, h, 0:n], X[0:n, h, 0, 0:n])
                    last.then_inc(mark("gdn_products", t + f"ZT{lv} {g}"), 1)
                    if lv < levels - 1:
                        b = take(4 + g, t + f"X{lv} {g}")
                        for j in range(HG):
                            h = HG * g + j
                            last = mm(b[0:n, n * j:n * j + n], X[0:n, h, 0, 0:n], Y[0:n, h, 0:n])
                        last.then_inc(mark("gdn_products", t + f"Z{lv} {g}"), 1)
            for g in range(2):
                b = take(4 + g, t + f"ke{g}")
                for j in range(HG):
                    last = tr(b[0:n, 128 * j:128 * j + 128], kB[:, HG * g + j, o:o + n], 128)
                last.then_inc(mark("gdn_products", t + f"kT{g}"), 1)
            if m == 1:
                for g in range(2):
                    b = take(6 + g, t + f"R{g}")
                    for j in range(HG):
                        h = HG * g + j
                        last = mm(b[:, 128 * j:128 * j + 128], kB[:, h, o:o + n], SB[:, h, :])
                    last.then_inc(mark("gdn_products", t + f"kS{g}"), 1)
            if m == 2:
                bk, bq = take(6, t + "kSs"), take(7, t + "qSs")
                for c in range(4):
                    pe.wait_ge(*when(loaded(("sgdn", c))))
                    w = slot(("sgdn", c)).rearrange("p k n -> p (k n)").rearrange("p (s h v) -> p s h v", h=HB, v=DVB)
                    for s2 in range(2):
                        s = 2 * c + s2
                        for h in range(HB):
                            j = 32 * h + DT * s
                            at = SEQ + DT * s
                            mm(bk[:, j:j + DT], w[:, s2, h, :], kB[:, h, at:at + DT])
                            last = mm(bq[:, j:j + DT], w[:, s2, h, :], qB[:, h, at:at + DT])
                last.then_inc(mark("gdn_products", t + "Ss"), 1)
                pe.wait_ge(*when(t + "kSs"))
                for g in range(2):
                    b = take(6 + g, t + f"R{g}")
                    for j in range(HG):
                        last = tr(b[0:n, 128 * j:128 * j + 128], oSt[:, HG * g + j, :], 128)
                    last.then_inc(mark("gdn_products", t + f"kS{g}"), 1)
            for g in range(2):
                pe.wait_ge(*when(t + f"XT{levels - 1} {g}"))
                if m:
                    pe.wait_ge(*when(t + f"R{g}"))
                else:
                    for c in range(8):
                        pe.wait_ge(*when(f"vbtok{c}"))
                b = take(4 + g, t + f"vn{g}")
                for j in range(HG):
                    h = HG * g + j
                    rhs = vB[0:n, m, 128 * h:128 * h + 128] if m == 0 else R[0:n, h, :]
                    last = mm(b[0:n, 128 * j:128 * j + 128], X[0:n, h, 0, 0:n], rhs)
                last.then_inc(mark("gdn_products", t + f"y{g}"), 1)
            for g in range(2):
                if m == 1:
                    b = take(6 + g, t + f"qS{g} read")
                    for j in range(HG):
                        h = HG * g + j
                        last = mm(b[:, 128 * j:128 * j + 128], qB[:, h, o:o + n], SB[:, h, :])
                    last.then_inc(mark("gdn_products", t + f"qS{g}"), 1)
                if m == 2:
                    b = take(6 + g, t + f"qS{g} read")
                    for j in range(HG):
                        last = tr(b[0:n, 128 * j:128 * j + 128], oSt2[:, HG * g + j, :], 128)
                    last.then_inc(mark("gdn_products", t + f"qS{g}"), 1)
            for g in range(2):
                pe.wait_ge(*when(t + f"vn{g}"))
                b = take(4 + g, t + f"o{g}")
                for j in range(HG):
                    h = HG * g + j
                    last = mm(b[0:n, 128 * j:128 * j + 128], AT[0:n, h, 0:n], R[0:n, h, :])
                last.then_inc(mark("gdn_products", t + f"o{g} ready"), 1)
            if m < 2:
                for g in range(2):
                    b = take(6 + g, t + f"state{g}")
                    for j in range(HG):
                        h = HG * g + j
                        last = mm(b[:, 128 * j:128 * j + 128], ke[0:n, h, :], R[0:n, h, :])
                    last.then_inc(mark("gdn_products", t + f"S{g} ready"), 1)
            else:
                for s in range(NSEQ):
                    pe.wait_ge(*when(f"kem2 {s}"))
                    for g in range(2):
                        b = take(6 + g, f"gdn state {s} {g}")
                        for j in range(HG):
                            h = HG * g + j
                            last = mm(b[:, 128 * j:128 * j + 128], kem2[0:32, s % 2, 128 * h:128 * h + 128],
                                      R[0:32, h, :])
                        last.then_inc(mark("gdn_products", f"gdn state product {s} {g}"), 1)
            for g in range(2):
                pe.wait_ge(*when(t + "oN"))
                b = take(4 + g, t + f"oT{g}")
                for j in range(4):
                    c = 4 * g + j
                    last = tr(b[:, 128 * j:128 * j + n], oNb[0:n, 128 * c:128 * c + 128], n)
                last.then_inc(mark("gdn_products", t + f"oT{g} ready"), 1)

        def wout():
            for c in range(4):
                pe.wait_ge(*when(loaded(("wout", c))))
                w = slot(("wout", c))
                for j in range(2):
                    d = 2 * c + j
                    if d == 0:
                        for k in range(KD):
                            pe.wait_ge(*when(f"merged {k}"))
                    b = ring_bank(f"wout{d}")
                    for k in range(KD):
                        last = mm(b[:, 0:TOK], w[:, k, 128 * j:128 * j + 128], GA[:, k, :], k == 0, k == KD - 1)
                    last \
                        .then_inc(mark("projected", f"wout{d} ready", *([used(("wout", c))] if j == 1 else [])), 1)

        def router():
            pe.wait_ge(*when("router weights"))
            for d in range(KD):
                pe.wait_ge(*when(f"h2 {d}"))
            b = ring_bank("router")
            for m, (o, n) in enumerate(TILES):
                for k in range(KD):
                    last = mm(b[0:n, 20 * m:20 * m + 20], hT[:, k, o:o + n], rtw[:, k, :], k == 0, k == KD - 1)
            last.then_inc(mark("router_products", "router ready"), 1)
            for m, (o, n) in enumerate(TILES):
                for g in range(2):
                    b = ring_bank(f"h2t{m}{g}")
                    for c in range(4):
                        last = tr(b[0:n, 128 * c:128 * c + 128], hT[:, 4 * g + c, o:o + n], 128)
                    last.then_inc(mark("transposed", f"h2t{m}{g} ready"), 1)
            b = ring_bank("rank")
            for m, (o, n) in enumerate(TILES):
                for q in range(m):
                    mm(b[0:n, NE * m:NE * m + NE], ones[:, 0:n], sel[:, q, :], q == 0, False)
                mm(b[0:n, NE * m:NE * m + NE], tri[0:n, 0:n], sel[0:n, m, :], m == 0, True)
            for m, (o, n) in enumerate(TILES):
                last = mm(b[0:MORE * NE, 64:65], sel4[0:n, m, :], ones[0:n, 0:1], m == 0, m == 2)
            last.then_inc(mark("router_products", "rank ready"), 1)
            pe.wait_ge(*when("over flags"))
            q = MORE * NE
            b = ring_bank("over")
            mm(b[0:q, 0:1], tri[0:q, 0:q], over[0:q, 0:1])
            mm(b[0:1, 8:9], over[0:q, 0:1], ones[0:q, 0:1]).then_inc(mark("router_products", "over ready"), 1)
            pe.wait_ge(*when("one-hot"))
            b = ring_bank("table")
            mm(b[:, 0:OVER], const("over_expert")[0:q, :], oneh[0:q, :])
            mm(b[:, 16:16 + OVER], const("over_base")[0:q, :], oneh[0:q, :]) \
                .then_inc(mark("router_products", "table ready"), 1)

        def expert_block(i, n, loaded_sem, second):
            def products(out, lhs, kind, k, half, K):
                for x in range(2):
                    wt = EW[:, kind, x * second, :].rearrange("p (k n) -> p k n", k=K)
                    last = mm(out[SLOTS * x:SLOTS * x + SLOTS, :], lhs[:, k, SLOTS * x:SLOTS * x + SLOTS],
                              wt[:, k, 512 * half:512 * half + 512], k == 0, k == K - 1)
                return last

            pe.wait_ge(n["dispatch"], i + 1)
            for g in range(2):
                for k in range(4):
                    for m, (o, w) in enumerate(TILES):
                        last = mm(pm[g][:, PAIR * k:PAIR * k + PAIR],
                                  h2t[0:w, m, 512 * g + 128 * k:512 * g + 128 * k + 128],
                                  Dg[0:w, m].rearrange("p a b -> p (a b)"), m == 0, m == 2)
                last.then_inc(n["gathered"], 1)
            pe.wait_ge(loaded_sem[0], 16 * (i + 1))
            pe.wait_ge(n["gather_read0"], i + 1)
            for k in range(KD):
                if k == 4:
                    pe.wait_ge(n["gather_read1"], i + 1)
                last = products(pm[2], hg, 0, k, 0, KD)
            last.then_inc(n["gate"], 1)
            pe.wait_ge(n["added"], KD * i + 1)
            for m, (o, w) in enumerate(TILES):
                last = tr(pm[4][0:PAIR, o:o + w], Dc[0:w, m].rearrange("p a b -> p (a b)"), w)
            last.then_inc(n["scatter_matrix"], 1)
            pe.wait_ge(loaded_sem[1], 16 * (i + 1))
            for k in range(KD):
                last = products(pm[3], hg, 1, k, 0, KD)
            last.then_inc(n["up"], 1)
            pe.wait_ge(n["hidden"], i + 1)
            for f in range(4):
                last = tr(pm[5][:, PAIR * f:PAIR * f + PAIR], hid[0:PAIR, 128 * f:128 * f + 128], PAIR)
            last.then_inc(n["turned"], 1)
            pe.wait_ge(loaded_sem[2], 16 * (i + 1))
            pe.wait_ge(n["turned_read"], i + 1)
            for g in range(2):
                for k in range(4):
                    last = products(pm[6 + g], hidT, 2, k, g, 4)
                last.then_inc(n["down"], 1)
            pe.wait_ge(n["down_read0"], i + 1)
            for d in range(KD):
                if d == 3:
                    pe.wait_ge(n["down_read1"], i + 1)
                if d >= 4:
                    pe.wait_ge(n["added"], KD * i + d - 2)
                last = mm(pm[4 + d % 4][:, 0:TOK], yt[0:PAIR, 128 * d:128 * d + 128], DT_[0:PAIR, :])
                last.then_inc(n["scattered"], 1)

        def experts():
            pe.wait_ge(*when("router done"))
            with pe.Fori(0, NE // 2) as i:
                expert_block(i, main_sems, expert_loaded, 1)
            pe.wait_ge(main_sems["added"], KD * (NE // 2) + 1)
            overflow(pe, lambda j: expert_block(j, over_sems, over_loaded, 0))

        def final():
            b = ring_bank("norm3")
            for d in range(KD):
                pe.wait_ge(*when(f"square3 {d}"))
                last = mm(b[:, 0:TOK], ones, hT[:, d, :], d == 0, d == KD - 1)
            last.then_inc(mark("norm_sums", "norm3 ready"), 1)
            for g in range(2):
                for m, (o, n) in enumerate(TILES):
                    for j in range(4):
                        pe.wait_ge(*when(f"yf {4 * g + j}"))
                    b = ring_bank(f"y{g}{m}")
                    for j in range(4):
                        last = tr(b[0:n, 128 * j:128 * j + 128], hT[:, 4 * g + j, o:o + n], 128)
                    last.then_inc(mark("transposed", f"y{g}{m} ready"), 1)

        run(locals())

    @block.vector
    def _(dve):
        def head():
            dve.wait_ge(*when("c exp1"))
            dve.wait_ge(*when("c rows"))
            V.scalar_tensor_tensor(csx[0:NC9, 1, :], crow[0:NC9, :], 0.0, csx[0:NC9, 0, :], ALU.min, ALU.subtract) \
                .then_inc(mark("head_by_vector", "c ls"), 1)
            dve.wait_ge(*when("c sig"))
            V.tensor_tensor(crow[0:NC9, :], crow[0:NC9, :], csx[0:NC9, 1, :], ALU.mult) \
                .then_inc(mark("head_by_vector", "silu(c)"), 1)
            dve.wait_ge(*when("vec ready"))
            V.tensor_copy(vecT[:, 0:NVEC], rb("vec")[:, 0:NVEC])
            V.tensor_copy(convT[:, 0:96], rb("vec")[:, 128:224]).then_inc(mark("head_by_vector", "read vec"), 1)
            for d in range(KD):
                dve.wait_ge(*when(f"x{d} ready"))
                V.tensor_copy(xT[:, d, :], rb(f"x{d}")[:, 0:TOK]) \
                    .then_inc(mark("head_by_vector", f"read x{d}"), 1)
            for g in range(2):
                dve.wait_ge(*when(f"cb{g} ready"))
                V.tensor_copy(cbT[:, 12 * g:12 * g + 12, :],
                                   rb(f"cb{g}")[:, 0:288].rearrange("p (a b) -> p a b", b=24)) \
                    .then_inc(mark("head_by_vector", f"read cb{g}"), 1)
            dve.wait_ge(*when("c ready"))
            V.tensor_copy(csT, rb("c")[:, 0:KD * NC9].rearrange("p (a b) -> p a b", b=NC9)) \
                .then_inc(mark("head_by_vector", "read c"), 1)

        def ada(c):
            dve.wait_ge(*when(f"ada{c} ready"))
            dve.wait_ge(*when("read vec"))
            V.tensor_tensor(modT[:, 2 * c:2 * c + 2, :],
                                 rb(f"ada{c}")[:, 0:2 * NC9].rearrange("p (a b) -> p a b", b=NC9),
                                 bc(vecT[:, 2 * c:2 * c + 2], NC9), ALU.add) \
                .then_inc(mark("ada_by_vector", f"read ada{c}"), 1)

        def norm(i):
            base = 24 * (i - 1)
            dve.wait_ge(*when(f"read ada{(base + 15) // 2}"))
            AA = A1 if i == 1 else A2
            o, _ = VEC[f"norm{i}"]
            V.scalar_tensor_tensor(AA, modT[:, base + 8:base + 16, :], 1.0, bc(vecT[:, o:o + 8], NC9),
                                        ALU.add, ALU.mult) \
                .then_inc(mark("norm_by_vector", f"A{i}"), 1)
            dve.wait_ge(*when(f"rstd{i}"))
            dve.wait_ge(*when(f"A{i}"))
            dve.wait_ge(*when(f"norm{i} ready"))
            for d in range(KD):
                V.tensor_tensor(hT[:, d, :], xT[:, d, :], rsB, ALU.mult) \
                    .then_inc(mark("norm_by_vector", f"n{i} {d}"), 1)
            for d in range(KD):
                dve.wait_ge(*when(f"n{i} {d}"))
                V.tensor_scalar(hT[:, d, 0:SEQ], hT[:, d, 0:SEQ], AA[:, d, 0:1], modT[:, base + d, 0:1], ALU.mult,
                                ALU.add)
                hs = hT[:, d, SEQ:TOK].rearrange("p (s t) -> p s t", t=DT)
                V.tensor_tensor(hs, hs, bc(AA[:, d, 1:NC9], DT), ALU.mult) \
                    .then_inc(mark("norm_by_vector", f"m{i} {d}"), 1)
            for d in range(KD):
                dve.wait_ge(*when(f"m{i} {d}"))
                hs = hT[:, d, SEQ:TOK].rearrange("p (s t) -> p s t", t=DT)
                V.tensor_tensor(hs, hs, bc(modT[:, base + d, 1:NC9], DT), ALU.add) \
                    .then_inc(mark("norm_by_vector", f"h{i} {d}"), 1)

        def small():
            dve.wait_ge(*when("ra ready"))
            dve.wait_ge(*when("raT ones"))
            V.tensor_copy(raT[0:RANK, :], rb("ra")[0:RANK, 0:TOK]) \
                .then_inc(mark("small_by_vector", "read ra", "raT"), 1)
            dve.wait_ge(*when("ba ready"))
            dve.wait_ge(*when("adt"))
            V.tensor_copy(ba[:, 0:2, :], rb("ba")[:, 0:32].rearrange("p (a b) -> p a b", b=16))
            V.tensor_copy(ba[0:32, 2, :], rb("ba")[0:32, 32:48]).then_inc(mark("small_by_vector", "read ba"), 1)
            dve.wait_ge(*when("read ba"))
            V.tensor_tensor(ba[:, :, 8:16], ba[:, :, 8:16], mid(adt[:, 1, :], 3), ALU.add) \
                .then_inc(mark("small_by_vector", "a + dt"), 1)
            dve.wait_ge(*when("small ln"))
            V.scalar_tensor_tensor(beta, ba[:, :, 0:8], 0.0, bcum_tmp(0), ALU.min, ALU.subtract)
            V.scalar_tensor_tensor(gt, ba[:, :, 8:16], 0.0, bcum_tmp(1), ALU.max, ALU.add) \
                .then_inc(mark("small_by_vector", "softplus"), 1)
            dve.wait_ge(*when("softplus"))
            dve.wait_ge(*when("exp A"))
            V.scalar_tensor_tensor(gB, gt, -1.0, mid(adt[:, 0, :], 3), ALU.mult, ALU.mult) \
                .then_inc(mark("small_by_vector", "g main"), 1)
            dve.wait_ge(*when("g main"))
            V.tensor_tensor(gseq[0:32], mid(gB[0:32, 2, :], NSEQ), bc(const("seq")[0:32, :], HB), ALU.mult) \
                .then_inc(mark("small_by_vector", "g"), 1)
            dve.wait_ge(*when("bcum ready"))
            for m, (o, n) in enumerate(TILES):
                V.tensor_copy(bcum[0:n, m, :], rb("bcum")[0:n, 8 * m:8 * m + 8])
                V.tensor_copy(blast[0:n, m, :], rb("bcum")[0:n, 32 + 8 * m:40 + 8 * m]) \
                    .then_inc(mark("small_by_vector", f"b{m}"), 1)
            dve.wait_ge(*when("b2"))
            V.tensor_tensor(gt, blast, bcum, ALU.subtract).then_inc(mark("small_by_vector", "b rest"), 1)

        def bcum_tmp(i):
            return sgm[:, 0, 24 * i:24 * i + 24].rearrange("p (a b) -> p a b", b=8)

        def step(s):
            s6, s4, s3, s1 = s - 6, s - 4, s - 3, s - 1
            if 0 <= s6 < NPROJ:
                kind, i, _ = PROJ[s6]
                if kind == "cv" and i < 16:
                    q = (qB if i < 8 else kB)[:, i % 8, :]
                    dve.wait_ge(*when(f"rs{s6}"))
                    V.tensor_tensor(q, q, rsb[:, s6 % 2, :], ALU.mult) \
                        .then_inc(mark("proj_by_vector", f"qkn{s6}"), 1)
                if kind == "va" or (kind == "cv" and i >= 16):
                    dve.wait_ge(*when(f"tr{s6} ready"))
                    dst = vA if kind == "va" else vB
                    c = i if kind == "va" else i - 16
                    b = rb(f"tr{s6}")
                    V.tensor_copy(dst[:, 0:2, 128 * c:128 * c + 128], b[:, 0:256].rearrange("p (a b) -> p a b", b=128))
                    V.tensor_copy(dst[0:32, 2, 128 * c:128 * c + 128], b[0:32, 256:384]) \
                        .then_inc(mark("proj_by_vector", f"read tr{s6}", f"vtok{i}" if kind == "va" else f"vbtok{c}"), 1)
            if 0 <= s4 < NPROJ:
                kind, i, _ = PROJ[s4]
                sg, y = sgm[:, s4 % 4], yb[:, s4 % 4]
                if kind in ("cv", "ga", "zb", "gsa", "gsb"):
                    dve.wait_ge(*when(f"sig{s4}"))
                if kind == "cv":
                    if i < 16:
                        out = (qB if i < 8 else kB)[:, i % 8, :]
                        V.tensor_tensor(out[:, 0:SEQ], y[:, 0:SEQ], sg[:, 0:SEQ], ALU.mult)
                        V.tensor_tensor(out[:, SEQ:TOK].rearrange("p (s t) -> p s t", t=DT), sampled(y),
                                             sampled(sg), ALU.mult) \
                            .then_inc(mark("proj_by_vector", f"act{s4}"), 1)
                    else:
                        V.tensor_tensor(sg[:, 0:SEQ], y[:, 0:SEQ], sg[:, 0:SEQ], ALU.mult) \
                            .then_inc(mark("proj_by_vector", f"actp{s4}"), 1)
                        dve.wait_ge(*when(f"actp{s4}"))
                        V.tensor_tensor(y[:, 0:32].rearrange("p (s t) -> p s t", t=DT), sampled(y), sampled(sg),
                                             ALU.mult) \
                            .then_inc(mark("proj_by_vector", f"acty{s4}"), 1)
                        dve.wait_ge(*when(f"acty{s4}"))
                        V.tensor_copy(sg[:, SEQ:TOK], y[:, 0:32]) \
                            .then_inc(mark("proj_by_vector", f"act{s4}"), 1)
                if kind == "ga":
                    V.tensor_tensor(GA[:, i, :], y[:, 0:TOK], sg[:, 0:TOK], ALU.mult) \
                        .then_inc(mark("proj_by_vector", f"act{s4}"), 1)
                if kind == "zb":
                    V.tensor_tensor(GB[:, i, :], y[:, 0:TOK], sg[:, 0:TOK], ALU.mult) \
                        .then_inc(mark("proj_by_vector", f"act{s4}"), 1)
                if kind in ("gsa", "gsb"):
                    GG = GA if kind == "gsa" else GB
                    dve.wait_ge(*when(f"act{s4 - 8}"))
                    V.tensor_tensor(GG[:, i, :], GG[:, i, :], sg[:, 0:TOK], ALU.mult) \
                        .then_inc(mark("proj_by_vector", f"act{s4}"), 1)
            if 0 <= s3 < NPROJ:
                kind, i, _ = PROJ[s3]
                if kind in ("cv", "ga", "zb", "gsa", "gsb"):
                    n = YW if kind == "cv" else TOK
                    dve.wait_ge(*when(f"ln{s3}"))
                    sg, y = sgm[:, s3 % 4, 0:n], yb[:, s3 % 4, 0:n]
                    V.scalar_tensor_tensor(sg, y, 0.0, sg, ALU.min, ALU.subtract) \
                        .then_inc(mark("proj_by_vector", f"ls{s3}"), 1)
            if 0 <= s1 < NPROJ:
                kind, i, _ = PROJ[s1]
                if kind == "cv":
                    dve.wait_ge(*when(f"xp{s1}"))
                    x, y = xp[:, s1 % 2], yb[:, s1 % 4]
                    dve.wait_ge(*when("read c"))
                    for event in y_free(s1 - 4):
                        dve.wait_ge(*when(event))
                    wv = lambda j: convT[:, 24 * j + i:24 * j + i + 1]
                    V.tensor_scalar(y, x[:, 0:YW], wv(0), None, ALU.mult) \
                        .then_inc(mark("proj_by_vector", f"tap0 {s1}"), 1)
                    for j in range(1, TAPS):
                        dve.wait_ge(*when(f"tap{j - 1} {s1}"))
                        V.scalar_tensor_tensor(y, x[:, j:j + YW], wv(j), y, ALU.mult, ALU.add) \
                            .then_inc(mark("proj_by_vector", f"tap{j} {s1}"), 1)

        def sampled(a):
            return a[:, SEQ:SEQ + 7 * NSEQ].rearrange("p (s t) -> p s t", t=7)[:, :, 3:7]

        def gla(m):
            o, n = TILES[m]
            t = f"gla{m} "
            dve.wait_ge(*when(t + "ln"))
            V.scalar_tensor_tensor(gA[0:n].rearrange("p a b -> p (a b)"), pm[4][0:n, :], 0.0,
                                        gA[0:n].rearrange("p a b -> p (a b)"), ALU.min, ALU.subtract) \
                .then_inc(mark("gla_by_vector", t + "logits read", t + "log decay"), 1)
            dve.wait_ge(*when(t + "cum"))
            dve.wait_ge(*when(t + "eb"))
            cum = pm[5][:, 0:HA * n].rearrange("p (h t) -> p h t", t=n)
            if m < 2:
                V.tensor_copy(ebl[:, :, 0:1], Eb[:, :, n - 1:n])
                V.tensor_copy(ebl[:, :, 1:2], cum[:, :, n // 2 - 1:n // 2]) \
                    .then_inc(mark("gla_by_vector", t + "ref"), 1)
                V.tensor_copy(ebl[:, :, 2:3], cum[:, :, n - 1:n]).then_inc(mark("gla_by_vector", t + "ref2"), 1)
                dve.wait_ge(*when(t + "ref2"))
                V.tensor_tensor(Ep, cum, ebl[:, :, 1:2].to_broadcast([P, HA, n]), ALU.subtract)
                V.tensor_tensor(El, ebl[:, :, 2:3].to_broadcast([P, HA, n]), cum, ALU.subtract) \
                    .then_inc(mark("gla_by_vector", t + "cum read", t + "D"), 1)
            else:
                V.tensor_copy(Em[:, :, 0:n], cum).then_inc(mark("gla_by_vector", t + "cumc"), 1)
                dve.wait_ge(*when(t + "cumc"))
                V.tensor_copy(Ep[:, :, 0:n], Em[:, :, 0:n])
                for h in range(HA):
                    c4 = Em[:, h, 0:n].rearrange("p (s t) -> p s t", t=DT)
                    e4 = Eb[:, h, 0:n].rearrange("p (s t) -> p s t", t=DT)
                    V.tensor_copy(ebl[:, h, :].unsqueeze(2), e4[:, :, DT - 1:DT])
                    last = V.tensor_tensor(El[:, h, 0:n].rearrange("p (s t) -> p s t", t=DT),
                                           c4[:, :, DT - 1:DT].to_broadcast([P, NSEQ, DT]), c4, ALU.subtract)
                last.then_inc(mark("gla_by_vector", t + "cum read", t + "D"), 1)
            q, k = QKA[:, 0:HA, o:o + n], QKA[:, HA:2 * HA, o:o + n]
            dve.wait_ge(*when(t + "exps"))
            V.tensor_tensor(Ep[:, :, 0:n], q, Ep[:, :, 0:n], ALU.mult) \
                .then_inc(mark("gla_by_vector", t + "qq"), 1)
            V.tensor_tensor(Em[:, :, 0:n], k, Em[:, :, 0:n], ALU.mult) \
                .then_inc(mark("gla_by_vector", t + "kk"), 1)
            V.tensor_tensor(El[:, :, 0:n], k, El[:, :, 0:n], ALU.mult) \
                .then_inc(mark("gla_by_vector", t + "ke"), 1)
            V.tensor_tensor(Eb[:, :, 0:n], q, Eb[:, :, 0:n], ALU.mult) \
                .then_inc(mark("gla_by_vector", t + "qb"), 1)
            dve.wait_ge(*when(t + "A"))
            V.tensor_tensor(ATa[0:n, :, 0:n], pm[6][0:n, 0:HA * n].rearrange("p (h t) -> p h t", t=n),
                                 mid(TRI[m][0:n, 0:n], HA), ALU.mult) \
                .then_inc(mark("gla_by_vector", t + "A read", t + "AT"), 1)
            if m == 2:
                dve.wait_ge(*when(t + "oS ready"))
                V.tensor_copy(oSt, pm[6][:, 0:256].rearrange("p (a b) -> p a b", b=32)) \
                    .then_inc(mark("gla_by_vector", t + "oS"), 1)
            if m == 1:
                for g in range(2):
                    dve.wait_ge(*when(t + f"S{g} ready"))
                    dve.wait_ge(*when(t + f"o{g} ready"))
                    for hh in range(2):
                        h = 2 * g + hh
                        last = V.scalar_tensor_tensor(SA[:, h, :], SA[:, h, :], ebl[:, h, 0:1],
                                                      pm[6 + g][:, 256 * hh:256 * hh + 256], ALU.mult, ALU.add)
                    last.then_inc(mark("gla_by_vector", t + f"S{g} read", f"gla state prompt {g}"), 1)
            dve.wait_ge(*when(t + "rstd"))
            dve.wait_ge(*when(t + "o1 ready"))
            for g in range(2):
                last = V.tensor_tensor(oNa[0:n, 512 * g:512 * g + 512].rearrange("p (a b) -> p a b", b=256),
                                       pm[4 + g][0:n, :].rearrange("p (a b) -> p a b", b=256),
                                       bc(srs[0:n, 2 * g:2 * g + 2], 256), ALU.mult)
                last.then_inc(mark("gla_by_vector", t + f"o{g} read", *([t + "oN"] if g else [])), 1)
            if m == 2:
                for s in range(NSEQ):
                    w = slot(("sgla", s // 2)).rearrange("p (s h) v -> p s h v", h=HA)
                    for g in range(2):
                        dve.wait_ge(*when(f"gla state product {s} {g}"))
                        for hh in range(2):
                            h = 2 * g + hh
                            st = w[:, s % 2, h, :]
                            last = V.scalar_tensor_tensor(st, st, ebl[:, h, s:s + 1],
                                                          pm[6 + g][:, 256 * hh:256 * hh + 256], ALU.mult, ALU.add)
                        last.then_inc(mark("gla_by_vector", f"gla state {s} {g}"), 1)
            for g in range(2):
                dve.wait_ge(*when(t + f"oT{g} ready"))
                V.tensor_copy(QKA[:, 4 * g:4 * g + 4, o:o + n],
                                   pm[4 + g][:, 0:512].rearrange("p (a b) -> p a b", b=128)[:, :, 0:n]) \
                    .then_inc(mark("gla_by_vector", t + f"oT{g}"), 1)

        def conv_out():
            for g in range(6):
                dve.wait_ge(*when(f"cvo{g} ready"))
                V.tensor_copy(newconv[0:27, 512 * g:512 * g + 512], rb(f"cvo{g}")[0:27, :]) \
                    .then_inc(mark("proj_by_vector", f"read cvo{g}"), 1)

        def gdn(m):
            o, n = TILES[m]
            t = f"gdn{m} "
            HG = 4
            if m == 0:
                dve.wait_ge(*when("gla2 oT1"))
            else:
                pass
            V.tensor_tensor(tg[0:n, :, 0:n], mid(TRI[m][0:n, 0:n], HB), bc(gB[0:n, m, :], n), ALU.mult) \
                .then_inc(mark("gdn_by_vector", t + "tg"), 1)
            for g in range(2):
                dve.wait_ge(*when(t + f"bc{g}"))
                for j in range(HG):
                    h = HG * g + j
                    last = V.tensor_scalar(E[0:n, h, 0:n], pm[4 + g][0:n, n * j:n * j + n], bcum[0:n, m, h:h + 1],
                                           0.0, ALU.subtract, ALU.min)
                last.then_inc(mark("gdn_by_vector", t + f"D{g}"), 1)
            for g in range(2):
                dve.wait_ge(*when(t + f"E{g}"))
                ee = E[0:n, HG * g:HG * g + HG, 0:n]
                V.tensor_tensor(ee, ee, mid(TRI[m][0:n, 0:n], HG), ALU.mult) \
                    .then_inc(mark("gdn_by_vector", t + f"Em{g}"), 1)
            for g in range(2):
                dve.wait_ge(*when(t + f"KK{g}"))
                dve.wait_ge(*when(t + f"Em{g}"))
                dve.wait_ge(*when("beta"))
                for j in range(HG):
                    h = HG * g + j
                    last = V.scalar_tensor_tensor(LT[0:n, h, 0:n], pm[6 + g][0:n, n * j:n * j + n],
                                                  beta[0:n, m, h:h + 1], E[0:n, h, 0:n], ALU.mult, ALU.mult)
                last.then_inc(mark("gdn_by_vector", t + f"KK{g} read"), 1)
            for g in range(2):
                dve.wait_ge(*when(t + f"QK{g}"))
                V.tensor_tensor(AT[0:n, HG * g:HG * g + HG, 0:n],
                                     pm[4 + g][0:n, 0:HG * n].rearrange("p (h t) -> p h t", t=n),
                                     E[0:n, HG * g:HG * g + HG, 0:n], ALU.mult) \
                    .then_inc(mark("gdn_by_vector", t + f"AT{g}"), 1)
            levels = LEVELS if m < 2 else 2
            idm = mid(ident[0:n, 0:n], HG)
            for lv in range(levels):
                for g in range(2):
                    hs = slice(HG * g, HG * g + HG)
                    dve.wait_ge(*when(t + f"KK{g} read"))
                    if lv == 1:
                        dve.wait_ge(*when(t + f"XT0 {g}"))
                    V.tensor_tensor(Lm[0:n, hs, 0:n], LT[0:n, hs, 0:n],
                                         mid(const(f"level{lv}")[0:n, 0:n], HG), ALU.mult) \
                        .then_inc(mark("gdn_by_vector", t + f"Lm{lv} {g}"), 1)
                for g in range(2):
                    hs = slice(HG * g, HG * g + HG)
                    view = lambda b: pm[b][0:n, 0:HG * n].rearrange("p (h t) -> p h t", t=n)
                    if lv == 0:
                        dve.wait_ge(*when(t + f"Lm0 {g}"))
                        V.tensor_tensor(X[0:n, hs, 0, 0:n], idm, Lm[0:n, hs, 0:n], ALU.subtract) \
                            .then_inc(mark("gdn_by_vector", t + f"XT0 {g}"), 1)
                        dve.wait_ge(*when(t + f"Y0 {g} ready"))
                        V.tensor_tensor(X[0:n, hs, 1, 0:n], idm, view(4 + g), ALU.subtract) \
                            .then_inc(mark("gdn_by_vector", t + f"Y0 {g}", t + f"X0 {g}"), 1)
                    else:
                        dve.wait_ge(*when(t + f"ZT{lv} {g}"))
                        if lv < levels - 1:
                            dve.wait_ge(*when(t + f"Z{lv} {g}"))
                        V.tensor_tensor(X[0:n, hs, 0, 0:n], X[0:n, hs, 0, 0:n], view(6 + g), ALU.subtract) \
                            .then_inc(mark("gdn_by_vector", t + f"XT{lv} {g}"), 1)
                        if lv < levels - 1:
                            V.tensor_tensor(X[0:n, hs, 1, 0:n], X[0:n, hs, 1, 0:n], view(4 + g), ALU.subtract) \
                                .then_inc(mark("gdn_by_vector", t + f"X{lv} {g}"), 1)
            full = lambda b: pm[b][0:n, :].rearrange("p (h t) -> p h t", t=128)
            for g in range(2):
                hs = slice(HG * g, HG * g + HG)
                dve.wait_ge(*when(t + f"kT{g}"))
                dve.wait_ge(*when("exp b"))
                for x in range(2):
                    dve.wait_ge(*when(t + f"Lm{levels - 1} {x}"))
                V.tensor_tensor(ke[0:n, hs, :], full(4 + g), bc(elB[0:n, m, hs], 128), ALU.mult) \
                    .then_inc(mark("gdn_by_vector", t + f"ke{g}"), 1)
            if m == 2:
                dve.wait_ge(*when(t + "Ss"))
                V.tensor_copy(oSt, pm[6][:, 0:256].rearrange("p (a b) -> p a b", b=32)) \
                    .then_inc(mark("gdn_by_vector", t + "kSs"), 1)
                V.tensor_copy(oSt2, pm[7][:, 0:256].rearrange("p (a b) -> p a b", b=32)) \
                    .then_inc(mark("gdn_by_vector", t + "qSs"), 1)
            for g in range(2):
                hs = slice(HG * g, HG * g + HG)
                vtok = vB[0:n, m, 512 * g:512 * g + 512].rearrange("p (h v) -> p h v", v=128)
                if m == 0:
                    continue
                dve.wait_ge(*when(t + f"kS{g}"))
                V.tensor_tensor(R[0:n, hs, :], full(6 + g), bc(ebB[0:n, m, hs], 128), ALU.mult) \
                    .then_inc(mark("gdn_by_vector", t + f"ekS{g}"), 1)
                dve.wait_ge(*when(t + f"ekS{g}"))
                V.tensor_tensor(R[0:n, hs, :], vtok, R[0:n, hs, :], ALU.subtract) \
                    .then_inc(mark("gdn_by_vector", t + f"R{g}"), 1)
            for g in range(2):
                hs = slice(HG * g, HG * g + HG)
                dve.wait_ge(*when(t + f"y{g}"))
                V.tensor_tensor(R[0:n, hs, :], full(4 + g), bc(beta[0:n, m, hs], 128), ALU.mult) \
                    .then_inc(mark("gdn_by_vector", t + f"vn{g}"), 1)
            for g in range(2):
                hs = slice(HG * g, HG * g + HG)
                if m:
                    dve.wait_ge(*when(t + f"qS{g}"))
                    V.tensor_tensor(E[0:n, hs, :], full(6 + g), bc(ebB[0:n, m, hs], 128), ALU.mult) \
                        .then_inc(mark("gdn_by_vector", t + f"qS{g} read"), 1)
            for g in range(2):
                hs = slice(HG * g, HG * g + HG)
                dve.wait_ge(*when(t + f"o{g} ready"))
                if m:
                    dve.wait_ge(*when(t + f"qS{g} read"))
                    V.tensor_tensor(E[0:n, hs, :], E[0:n, hs, :], full(4 + g), ALU.add) \
                        .then_inc(mark("gdn_by_vector", t + f"o{g}"), 1)
                else:
                    V.tensor_copy(E[0:n, hs, :], full(4 + g)).then_inc(mark("gdn_by_vector", t + f"o{g}"), 1)
            if m < 2:
                for g in range(2):
                    hs = slice(HG * g, HG * g + HG)
                    dve.wait_ge(*when(t + f"S{g} ready"))
                    if m == 0:
                        last = V.tensor_copy(SB[:, hs, :], full(6 + g))
                    else:
                        for j in range(HG):
                            h = HG * g + j
                            last = V.scalar_tensor_tensor(SB[:, h, :], SB[:, h, :], eSd[:, m, h:h + 1],
                                                          pm[6 + g][:, 128 * j:128 * j + 128], ALU.mult, ALU.add)
                    last.then_inc(mark("gdn_by_vector", t + f"state{g}"), 1)
            dve.wait_ge(*when(t + "squares"))
            V.tensor_reduce(ssum[0:n, :], sqo[0:n], AX, ALU.add).then_inc(mark("gdn_by_vector", t + "ssum"), 1)
            dve.wait_ge(*when(t + "rstd"))
            V.tensor_tensor(Y[0:n], E[0:n], bc(srs[0:n, :], 128), ALU.mult) \
                .then_inc(mark("gdn_by_vector", t + "oN"), 1)
            if m == 2:
                for s in range(NSEQ):
                    w = slot(("sgdn", s // 2)).rearrange("p k n -> p (k n)").rearrange("p (s h v) -> p s h v", h=HB, v=DVB)
                    for g in range(2):
                        dve.wait_ge(*when(f"gdn state product {s} {g}"))
                        for j in range(HG):
                            h = HG * g + j
                            st = w[:, s % 2, h, :]
                            last = V.scalar_tensor_tensor(st, st, eSs[:, s, h:h + 1],
                                                          pm[6 + g][:, 128 * j:128 * j + 128], ALU.mult, ALU.add)
                        last.then_inc(mark("gdn_by_vector", f"gdn state {s} {g}"), 1)
            for g in range(2):
                dve.wait_ge(*when(t + f"oT{g} ready"))
                V.tensor_copy(qB[:, 4 * g:4 * g + 4, o:o + n],
                                   pm[4 + g][:, 0:512].rearrange("p (a b) -> p a b", b=128)[:, :, 0:n]) \
                    .then_inc(mark("gdn_by_vector", t + f"oT{g}"), 1)

        def merge():
            dve.wait_ge(*when("gdn2 oT1"))
            for s in range(NPROJ - 32, NPROJ):
                dve.wait_ge(*when(f"act{s}"))
            an, bn = VEC["gla_norm"][0], VEC["gdn_norm"][0]
            for d in range(KD):
                V.scalar_tensor_tensor(GA[:, d, :], QKA[:, d, :], vecT[:, an + d % 2:an + d % 2 + 1], GA[:, d, :],
                                            ALU.mult, ALU.mult) \
                    .then_inc(mark("merge_by_vector", f"ma {d}"), 1)
                V.scalar_tensor_tensor(GB[:, d, :], qB[:, d, :], vecT[:, bn:bn + 1], GB[:, d, :],
                                            ALU.mult, ALU.mult) \
                    .then_inc(mark("merge_by_vector", f"mb {d}"), 1)
            for d in range(KD):
                dve.wait_ge(*when(f"mb {d}"))
                V.tensor_tensor(GA[:, d, :], GA[:, d, :], GB[:, d, :], ALU.add) \
                    .then_inc(mark("merge_by_vector", f"merged {d}"), 1)

        def wout():
            dve.wait_ge(*when("read ada11"))
            for d in range(KD):
                dve.wait_ge(*when(f"wout{d} ready"))
                residual(d, rb(f"wout{d}")[:, 0:TOK], 16, f"read wout{d}", f"x2 {d}", "merge_by_vector")

        def residual(d, src, gate, read, new, kind):
            V.scalar_tensor_tensor(xT[:, d, 0:SEQ], src[:, 0:SEQ], modT[:, gate + d, 0:1], xT[:, d, 0:SEQ],
                                   ALU.mult, ALU.add)
            V.tensor_tensor(gs[:, d % 2, :].rearrange("p (s t) -> p s t", t=DT),
                                 src[:, SEQ:TOK].rearrange("p (s t) -> p s t", t=DT),
                                 bc(modT[:, gate + d, 1:NC9], DT), ALU.mult) \
                .then_inc(mark(kind, read), 1)
            dve.wait_ge(*when(read))
            V.tensor_tensor(xT[:, d, SEQ:TOK], xT[:, d, SEQ:TOK], gs[:, d % 2, :], ALU.add) \
                .then_inc(mark(kind, new), 1)

        def router():
            dve.wait_ge(*when("router ready"))
            dve.wait_ge(*when("router bias"))
            dve.wait_ge(*when("rt zero"))
            V.tensor_copy(rt[:, 0:2, :], rb("router")[:, 0:40].rearrange("p (a b) -> p a b", b=20))
            V.tensor_copy(rt[0:32, 2, :], rb("router")[0:32, 40:60]) \
                .then_inc(mark("router_by_vector", "read router"), 1)
            k = [0]

            def st(ins, *ev):
                k[0] += 1
                ins.then_inc(mark("router_by_vector", f"rstep{k[0]}", *ev), 1)
                dve.wait_ge(*when(f"rstep{k[0]}"))
            dve.wait_ge(*when("read router"))
            st(V.tensor_tensor(rt, rt, mid(rtb, 3), ALU.add))
            r = rs_
            iota = mid(const("iota")[:, 0:4], 3)
            one = lambda n: r[n][:, :, 0:1]
            spread = lambda n: r[n][:, :, 0:1].to_broadcast([P, 3, 4])

            def first_max(vals, mx, sel, i):
                st(V.tensor_reduce(one(mx), vals, AX, ALU.max))
                st(V.tensor_tensor(r["hit"], vals, spread(mx), ALU.is_equal))
                st(V.scalar_tensor_tensor(r["idx"], iota, -4.0, r["hit"], ALU.add, ALU.mult))
                st(V.tensor_reduce(one("i1"), r["idx"], AX, ALU.min))
                st(V.tensor_scalar(one("tmp"), one("i1"), 4.0, None, ALU.add))
                st(V.tensor_tensor(r[sel], iota, spread("tmp"), ALU.is_equal))

            first_max(rt[:, :, 0:4], "gmax", "gsel", 0)
            st(V.tensor_tensor(r["dd"], rt[:, :, 0:4], spread("gmax"), ALU.subtract), "gd")
            dve.wait_ge(*when("gexp"))
            st(V.tensor_reduce(one("gden"), r["dd"], AX, ALU.add))
            st(V.reciprocal(one("gw"), one("gden")))
            e4 = el16.rearrange("p m (g e) -> p m g e", e=4)
            l4 = rt[:, :, 4:20].rearrange("p m (g e) -> p m g e", e=4)
            for m in range(3):
                st(V.tensor_tensor(e4[:, m], l4[:, m], bc(r["gsel"][:, m, :], 4), ALU.mult))
                st(V.tensor_reduce(r["el"][:, m, :], e4[:, m].rearrange("p g e -> p e g"), AX, ALU.add))
            first_max(r["el"], "emax", "h1", 1)
            st(V.tensor_tensor(r["p1"], r["el"], spread("emax"), ALU.subtract), "ed")
            dve.wait_ge(*when("eexp"))
            st(V.scalar_tensor_tensor(r["p2"], r["h1"], -4.0, r["p1"], ALU.mult, ALU.add))
            first_max(r["p2"], "w2", "hh", 2)
            st(V.tensor_scalar(one("w1"), one("w2"), 1.0, None, ALU.add))
            st(V.reciprocal(one("w1"), one("w1")))
            st(V.tensor_tensor(r["within"], r["hh"], spread("w2"), ALU.mult))
            st(V.tensor_tensor(r["within"], r["within"], r["h1"], ALU.add))
            st(V.tensor_tensor(one("w1"), one("w1"), one("gw"), ALU.mult))
            st(V.tensor_tensor(r["within"], r["within"], spread("w1"), ALU.mult))
            c4 = comb[:, :, 0:NE].rearrange("p m (g e) -> p m g e", e=4)
            for m in range(3):
                st(V.tensor_tensor(c4[:, m], bc(r["gsel"][:, m, :], 4), mid(r["within"][:, m, :], 4), ALU.mult),
                   *(["comb"] if m == 2 else []))
            for m in range(3):
                st(V.tensor_tensor(r["tmp"][:, m, :], r["hh"][:, m, :], r["h1"][:, m, :], ALU.add))
                st(V.tensor_tensor(sel.rearrange("p m (g e) -> p m g e", e=4)[:, m], bc(r["gsel"][:, m, :], 4),
                                   mid(r["tmp"][:, m, :], 4), ALU.mult))
            st(V.tensor_copy(sel4.rearrange("p m (r e) -> p m r e", e=NE),
                             sel.unsqueeze(2).to_broadcast([P, 3, MORE, NE])), "sel4")
            for m, (o, n) in enumerate(TILES):
                for g in range(2):
                    dve.wait_ge(*when(f"h2t{m}{g} ready"))
                    V.tensor_copy(h2t[0:n, m, 512 * g:512 * g + 512], rb(f"h2t{m}{g}")[0:n, :]) \
                        .then_inc(mark("router_by_vector", f"read h2t{m}{g}"), 1)
            q = MORE * NE
            dve.wait_ge(*when("rank ready"))
            b = rb("rank")
            for m, (o, n) in enumerate(TILES):
                st(V.tensor_tensor(rank[0:n, m, 0:NE], b[0:n, NE * m:NE * m + NE], sel[0:n, m, :], ALU.mult))
                st(V.tensor_scalar(rank[0:n, m, 0:NE], rank[0:n, m, 0:NE], -1.0, None, ALU.add))
            st(V.tensor_tensor(over[0:q, 0:1], b[0:q, 64:65], const("over_at")[0:q, :], ALU.is_gt), "read rank",
               "over flags")
            dve.wait_ge(*when("over ready"))
            b = rb("over")
            st(V.tensor_scalar(over[0:q, 1:2], b[0:q, 0:1], -1.0, None, ALU.add))
            st(V.tensor_copy(tab[0:1, 0:1], b[0:1, 8:9]), "read over")
            st(V.tensor_scalar(oneh[0:q, :], const("iota")[0:q, 0:OVER], over[0:q, 1:2], over[0:q, 0:1],
                               ALU.is_equal, ALU.mult), "one-hot")
            dve.wait_ge(*when("table ready"))
            b = rb("table")
            st(V.tensor_copy(tab[0:1, 1:1 + OVER], b[0:1, 0:OVER]), "tables")
            st(V.tensor_copy(expB, b[:, 0:OVER]))
            st(V.tensor_copy(rankO, mid(b[:, 16:16 + OVER], 3)), "read table")
            st(V.tensor_copy(over_scratch, rankO), "router done")

        over_scratch = combO

        def dispatch(places, n):
            for s0, ns, iota, rank_of, comb_of in places:
                for m, (o, w) in enumerate(TILES):
                    dg, dc = [t[0:w, m].rearrange("p a b -> p (a b)")[:, s0:s0 + ns] for t in (Dg, Dc)]
                    V.tensor_scalar(dg, iota[0:w], rank_of(m, w), None, ALU.is_equal)
                    last = V.tensor_scalar(dc, iota[0:w], rank_of(m, w), comb_of(m, w), ALU.is_equal, ALU.mult)
            last.then_inc(n["dispatch"], 1)

        def dispatch_pair(first):
            def place(x):
                def column(table):
                    return lambda m, w: table[0:w, m, bass.ds(first + x, 1)]
                return SLOTS * x, SLOTS, const("iota")[:, 0:SLOTS], column(rank), column(comb)
            dispatch([place(0), place(1)], main_sems)

        def expert_block(i, n, next_dispatch):
            dve.wait_ge(n["gathered"], 2 * i + 1)
            V.tensor_copy(hg[:, 0:4, :], pm[0][:, 0:4 * PAIR].rearrange("p (k s) -> p k s", s=PAIR)) \
                .then_inc(n["gather_read0"], 1)
            s = sg2[0:PAIR]
            dve.wait_ge(n["softplus"], i + 1)
            V.scalar_tensor_tensor(s, pm[2][0:PAIR, :], 0.0, s, ALU.min, ALU.subtract).then_inc(n["log_sigmoid"], 1)
            dve.wait_ge(n["scatter_matrix"], i + 1)
            V.tensor_copy(DT_[0:PAIR, :], pm[4][0:PAIR, 0:TOK]).then_inc(n["scatter_matrix_read"], 1)
            dve.wait_ge(n["sigmoid"], i + 1)
            V.tensor_tensor(s, pm[2][0:PAIR, :], s, ALU.mult).then_inc(n["silu"], 1)
            next_dispatch()
            dve.wait_ge(n["silu"], i + 1)
            dve.wait_ge(n["up"], i + 1)
            V.tensor_tensor(hid[0:PAIR], pm[3][0:PAIR, :], s, ALU.mult).then_inc(n["hidden"], 1)
            dve.wait_ge(n["turned"], i + 1)
            V.tensor_copy(hidT, pm[5][:, 0:4 * PAIR].rearrange("p (k s) -> p k s", s=PAIR)) \
                .then_inc(n["turned_read"], 1)
            dve.wait_ge(n["down"], 2 * i + 1)
            V.tensor_copy(yt[0:PAIR, 0:512], pm[6][0:PAIR, :]).then_inc(n["down_read0"], 1)
            dve.wait_ge(n["added"], KD * i + 1)
            for d in range(KD):
                dve.wait_ge(n["scattered"], KD * i + d + 1)
                V.tensor_tensor(acc[:, d, :], acc[:, d, :], pm[4 + d % 4][:, 0:TOK], ALU.add).then_inc(n["added"], 1)

        def experts():
            V.memset(acc, 0.0).then_inc(main_sems["added"], 1)
            V.memset(combJ, 0.0).then_inc(over_sems["added"], 1)
            dispatch_pair(0)
            with dve.Fori(0, NE // 2) as i:
                expert_block(i, main_sems, lambda: dispatch_pair(2 * i + 2))
            dve.wait_ge(main_sems["added"], KD * (NE // 2) + 1)
            dve.wait_ge(main_sems["dispatch"], NE // 2 + 1)

            def one_over(j):
                V.tensor_tensor(hitE, const("iota")[:, 0:NE], expB[:, bass.ds(j, 1)].to_broadcast([P, NE]),
                                ALU.is_equal).then_inc(over_sems["picked"], 1)
                dve.wait_ge(over_sems["picked"], 6 * j + 1)
                V.tensor_tensor(el16, rank[:, :, 0:NE], mid(hitE, 3), ALU.mult).then_inc(over_sems["picked"], 1)
                dve.wait_ge(over_sems["picked"], 6 * j + 2)
                V.tensor_reduce(rankJ, el16, AX, ALU.add).then_inc(over_sems["picked"], 1)
                dve.wait_ge(over_sems["picked"], 6 * j + 3)
                V.tensor_tensor(rankJ, rankJ, rankO[:, :, bass.ds(j, 1)].rearrange("p m a -> p (m a)"),
                                ALU.subtract).then_inc(over_sems["picked"], 1)
                V.tensor_tensor(el16, comb[:, :, 0:NE], mid(hitE, 3), ALU.mult).then_inc(over_sems["picked"], 1)
                dve.wait_ge(over_sems["picked"], 6 * j + 5)
                V.tensor_reduce(combJ, el16, AX, ALU.add).then_inc(over_sems["picked"], 1)
                dve.wait_ge(over_sems["picked"], 6 * j + 6)
                dispatch([(0, PAIR, const("iota")[:, 0:PAIR], lambda m, w: rankJ[0:w, m:m + 1],
                           lambda m, w: combJ[0:w, m:m + 1])], over_sems)
                expert_block(j, over_sems, lambda: None)
                dve.wait_ge(over_sems["added"], KD * (j + 1) + 1)

            overflow(dve, one_over)

        def final():
            dve.wait_ge(*when("read ada23"))
            for d in range(KD):
                residual(d, acc[:, d, :], 40, f"moe {d}", f"x3 {d}", "final_by_vector")
            fo = VEC["final"][0]
            dve.wait_ge(*when("rstd3"))
            dve.wait_ge(*when("norm3 ready"))
            for d in range(KD):
                V.scalar_tensor_tensor(hT[:, d, :], xT[:, d, :], vecT[:, fo + d:fo + d + 1], rsB, ALU.mult,
                                            ALU.mult) \
                    .then_inc(mark("final_by_vector", f"yf {d}"), 1)
            for g in range(2):
                for m, (o, n) in enumerate(TILES):
                    dve.wait_ge(*when(f"y{g}{m} ready"))
                    V.tensor_copy(yrow[0:n, m, 512 * g:512 * g + 512], rb(f"y{g}{m}")[0:n, :]) \
                        .then_inc(mark("final_by_vector", f"read y{g}{m}"), 1)

        run(locals())

    @block.scalar
    def _(act):
        A.preload_act_table_set("natural_log_exp_and_others")
        one = ones[:, 0:1]

        def lnexp(dst, src, n=P, kind="", event=None):
            A.activation(dst, src, ACT.Abs).then_inc(mark(kind, event + " abs"), 1)
            act.wait_ge(*when(event + " abs"))
            A.activation(dst, dst, ACT.Exp, scale=-1.0).then_inc(mark(kind, event + " exp"), 1)
            act.wait_ge(*when(event + " exp"))
            A.activation(dst, dst, ACT.Ln, bias=one[0:n]).then_inc(mark(kind, event), 1)

        def rstd(dst, src, scale, kind, event, n=P, bias=None, mid_event=None):
            ev = [mid_event] if mid_event else []
            A.activation(dst, src, ACT.Ln, bias=const("eps")[0:n], scale=scale) \
                .then_inc(mark(kind, event + " ln", *ev), 1)
            act.wait_ge(*when(event + " ln"))
            if bias is None:
                ins = A.activation(dst, dst, ACT.Exp, scale=-0.5)
            else:
                ins = A.activation(dst, dst, ACT.Exp, scale=-0.5, bias=bias)
            ins.then_inc(mark(kind, event), 1)

        def head():
            act.wait_ge(*when("consts"))
            act.wait_ge(*when("c rows"))
            lnexp(csx[0:NC9, 0, :], crow[0:NC9, :], NC9, "head_by_scalar", "c exp1")
            act.wait_ge(*when("c ls"))
            A.activation(csx[0:NC9, 1, :], csx[0:NC9, 1, :], ACT.Exp) \
                .then_inc(mark("head_by_scalar", "c sig"), 1)
            for d in range(KD):
                act.wait_ge(*when(f"read x{d}"))
                A.activation(hT[:, d, :], xT[:, d, :], ACT.Square) \
                    .then_inc(mark("head_by_scalar", f"square1 {d}"), 1)

        def norm(i):
            if i == 2:
                for d in range(KD):
                    act.wait_ge(*when(f"x2 {d}"))
                    A.activation(hT[:, d, :], xT[:, d, :], ACT.Square) \
                        .then_inc(mark("norm_by_scalar", f"square2 {d}"), 1)
            act.wait_ge(*when(f"norm{i} ready"))
            if i == 2:
                act.wait_ge(*when("h1 7"))
            rstd(rsB, rb(f"norm{i}")[:, 0:TOK], 1.0 / D, "norm_by_scalar", f"rstd{i}", mid_event=f"read norm{i}")

        def small():
            act.wait_ge(*when("a + dt"))
            t0 = sgm[:, 0, 0:24].rearrange("p (a b) -> p a b", b=8)
            t1 = sgm[:, 0, 24:48].rearrange("p (a b) -> p a b", b=8)
            A.activation(t0, ba[:, :, 0:8], ACT.Abs)
            A.activation(t1, ba[:, :, 8:16], ACT.Abs).then_inc(mark("small_by_scalar", "small abs"), 1)
            act.wait_ge(*when("small abs"))
            tt = sgm[:, 0, 0:48]
            A.activation(tt, tt, ACT.Exp, scale=-1.0).then_inc(mark("small_by_scalar", "small exp"), 1)
            act.wait_ge(*when("small exp"))
            A.activation(tt, tt, ACT.Ln, bias=one).then_inc(mark("small_by_scalar", "small ln"), 1)
            A.activation(adt[:, 0, :], adt[:, 0, :], ACT.Exp).then_inc(mark("small_by_scalar", "exp A"), 1)
            act.wait_ge(*when("softplus"))
            A.activation(beta, beta, ACT.Exp).then_inc(mark("small_by_scalar", "beta"), 1)
            act.wait_ge(*when("b rest"))
            A.activation(eSs, rb("bcum")[:, 64:128].rearrange("p (s h) -> p s h", h=HB), ACT.Exp) \
                .then_inc(mark("small_by_scalar", "read bcum"), 1)
            A.activation(ebB, bcum, ACT.Exp)
            A.activation(eSd, blast, ACT.Exp)
            A.activation(elB, gt, ACT.Exp).then_inc(mark("small_by_scalar", "exp b"), 1)

        def step(s):
            s5, s4, s3, s2, s0 = s - 5, s - 4, s - 3, s - 2, s
            if 0 <= s5 < NPROJ:
                kind, i, _ = PROJ[s5]
                if kind == "cv" and i < 16:
                    act.wait_ge(*when(f"ssq{s5} ready"))
                    rstd(rsb[:, s5 % 2, :], rb(f"ssq{s5}")[:, 0:TOK], 1.0, "proj_by_scalar", f"rs{s5}",
                         bias=const("lnq") if i < 8 else None, mid_event=f"read ssq{s5}")
            if 0 <= s4 < NPROJ:
                kind, i, _ = PROJ[s4]
                if kind == "cv" and i < 16:
                    act.wait_ge(*when(f"act{s4}"))
                    q = (qB if i < 8 else kB)[:, i % 8, :]
                    A.activation(sqb[:, s4 % 2, :], q, ACT.Square) \
                        .then_inc(mark("proj_by_scalar", f"sq{s4}"), 1)
            if 0 <= s3 < NPROJ:
                kind, i, _ = PROJ[s3]
                if kind in ("cv", "ga", "zb", "gsa", "gsb"):
                    n = YW if kind == "cv" else TOK
                    act.wait_ge(*when(f"ls{s3}"))
                    sg = sgm[:, s3 % 4, 0:n]
                    A.activation(sg, sg, ACT.Exp).then_inc(mark("proj_by_scalar", f"sig{s3}"), 1)
            if 0 <= s2 < NPROJ:
                kind, i, _ = PROJ[s2]
                if kind in ("cv", "ga", "zb", "gsa", "gsb"):
                    n = YW if kind == "cv" else TOK
                    act.wait_ge(*when(f"tap3 {s2}" if kind == "cv" else f"y{s2}"))
                    for event in sg_free(s2 - 4):
                        act.wait_ge(*when(event))
                    lnexp(sgm[:, s2 % 4, 0:n], yb[:, s2 % 4, 0:n], P, "proj_by_scalar", f"ln{s2}")
            if s0 < NPROJ:
                kind, i, _ = PROJ[s0]
                act.wait_ge(*when(f"proj{s0} ready"))
                b = rb(f"proj{s0}")
                if kind == "qa":
                    A.activation(QKA[:, i, :], b[:, 0:TOK], ACT.Copy, scale=DKA ** -0.5) \
                        .then_inc(mark("proj_by_scalar", f"read proj{s0}"), 1)
                elif kind == "ka":
                    A.activation(QKA[:, 4 + i, :], b[:, 0:TOK], ACT.Copy) \
                        .then_inc(mark("proj_by_scalar", f"read proj{s0}"), 1)
                elif kind == "cv":
                    x = xp[:, s0 % 2]
                    act.wait_ge(*when("xp zero"))
                    act.wait_ge(*when("read cb1"))
                    if i >= 2:
                        act.wait_ge(*when(f"cc{i - 2}"))
                    A.activation(x[:, 3:3 + SEQ], b[:, 0:SEQ], ACT.Copy)
                    blk = x[:, SAMP0:XPW].rearrange("p (s t) -> p s t", t=7)
                    A.activation(blk[:, :, 0:3], cbT[:, i, :].rearrange("p (s t) -> p s t", t=3), ACT.Copy)
                    A.activation(blk[:, :, 3:7], b[:, SEQ:TOK].rearrange("p (s t) -> p s t", t=DT), ACT.Copy) \
                        .then_inc(mark("proj_by_scalar", f"read proj{s0}", f"xp{s0}"), 1)
                else:
                    for event in y_free(s0 - 4):
                        act.wait_ge(*when(event))
                    A.activation(yb[:, s0 % 4, 0:TOK], b[:, 0:TOK], ACT.Copy) \
                        .then_inc(mark("proj_by_scalar", f"read proj{s0}", f"y{s0}"), 1)

        def gla(m):
            o, n = TILES[m]
            t = f"gla{m} "
            act.wait_ge(*when(t + "logits"))
            lnexp(gA[0:n].rearrange("p a b -> p (a b)"), pm[4][0:n, :], n, "gla_by_scalar", t + "ln")
            act.wait_ge(*when(t + "cum"))
            sc = 1.0 / TAU
            cum = pm[5][:, 0:HA * n].rearrange("p (h t) -> p h t", t=n)
            A.activation(Eb[:, :, 0:n], cum, ACT.Exp, scale=sc).then_inc(mark("gla_by_scalar", t + "eb"), 1)
            act.wait_ge(*when(t + "D"))
            A.activation(Em[:, :, 0:n], Ep[:, :, 0:n], ACT.Exp, scale=-sc)
            A.activation(El[:, :, 0:n], El[:, :, 0:n], ACT.Exp, scale=sc) \
                .then_inc(mark("gla_by_scalar", t + "em"), 1)
            act.wait_ge(*when(t + "em"))
            A.activation(Ep[:, :, 0:n], Ep[:, :, 0:n], ACT.Exp, scale=sc) \
                .then_inc(mark("gla_by_scalar", t + "exps"), 1)
            act.wait_ge(*when(t + "ke transposed"))
            A.activation(keTa[0:n], pm[7][0:n, :].rearrange("p (h t) -> p h t", t=128), ACT.Copy) \
                .then_inc(mark("gla_by_scalar", t + "keT"), 1)
            if m == 0:
                for g in range(2):
                    act.wait_ge(*when(t + f"S{g} ready"))
                    A.activation(SA[:, 2 * g:2 * g + 2, :], pm[6 + g][:, :].rearrange("p (a b) -> p a b", b=256),
                                      ACT.Copy) \
                        .then_inc(mark("gla_by_scalar", t + f"S{g} read", *(["gla0 state"] if g else [])), 1)
            for g in range(2):
                act.wait_ge(*when(t + f"o{g} ready"))
                for hh in range(2):
                    h = 2 * g + hh
                    A.activation(oNa[0:n, 256 * h:256 * h + 256], pm[4 + g][0:n, 256 * hh:256 * hh + 256],
                                      ACT.Square, accum_out=ssum[0:n, h:h + 1]) \
                        .then_inc(mark("gla_by_scalar", *([t + "ss"] if h == HA - 1 else [])), 1)
            act.wait_ge(*when(t + "ss"))
            rstd(srs[0:n, 0:HA], ssum[0:n, 0:HA], 1.0 / DVA, "gla_by_scalar", t + "rstd", n=n)

        def gdn(m):
            o, n = TILES[m]
            t = f"gdn{m} "
            HG = 4
            for g in range(2):
                act.wait_ge(*when(t + f"D{g}"))
                ee = E[0:n, HG * g:HG * g + HG, 0:n]
                A.activation(ee, ee, ACT.Exp).then_inc(mark("gdn_by_scalar", t + f"E{g}"), 1)
            levels = LEVELS if m < 2 else 2
            for lv in range(1, levels):
                for g in range(2):
                    act.wait_ge(*when(t + f"Y{lv} {g} ready"))
                    A.activation(Y[0:n, HG * g:HG * g + HG, 0:n],
                                      pm[4 + g][0:n, 0:HG * n].rearrange("p (h t) -> p h t", t=n), ACT.Copy) \
                        .then_inc(mark("gdn_by_scalar", t + f"Y{lv} {g}"), 1)
            act.wait_ge(*when(t + "o0"))
            act.wait_ge(*when(t + "o1"))
            A.activation(sqo[0:n], E[0:n], ACT.Square).then_inc(mark("gdn_by_scalar", t + "squares"), 1)
            act.wait_ge(*when(t + "ssum"))
            rstd(srs[0:n, :], ssum[0:n, :], 1.0 / DVB, "gdn_by_scalar", t + "rstd", n=n)

        def router():
            act.wait_ge(*when("gd"))
            A.activation(rs_["dd"], rs_["dd"], ACT.Exp).then_inc(mark("router_by_scalar", "gexp"), 1)
            act.wait_ge(*when("ed"))
            A.activation(rs_["p1"], rs_["p1"], ACT.Exp).then_inc(mark("router_by_scalar", "eexp"), 1)

        def expert_block(i, n):
            act.wait_ge(n["gathered"], 2 * i + 2)
            A.activation(hg[:, 4:8, :], pm[1][:, 0:4 * PAIR].rearrange("p (k s) -> p k s", s=PAIR), ACT.Copy) \
                .then_inc(n["gather_read1"], 1)
            s = sg2[0:PAIR]
            act.wait_ge(n["gate"], i + 1)
            A.activation(s, pm[2][0:PAIR, :], ACT.Abs).then_inc(n["softplus_step"], 1)
            act.wait_ge(n["softplus_step"], 2 * i + 1)
            A.activation(s, s, ACT.Exp, scale=-1.0).then_inc(n["softplus_step"], 1)
            act.wait_ge(n["softplus_step"], 2 * i + 2)
            A.activation(s, s, ACT.Ln, bias=one[0:PAIR]).then_inc(n["softplus"], 1)
            act.wait_ge(n["log_sigmoid"], i + 1)
            A.activation(s, s, ACT.Exp).then_inc(n["sigmoid"], 1)
            act.wait_ge(n["down"], 2 * i + 2)
            A.activation(yt[0:PAIR, 512:1024], pm[7][0:PAIR, :], ACT.Copy).then_inc(n["down_read1"], 1)

        def experts():
            act.wait_ge(*when("router done"))
            with act.Fori(0, NE // 2) as i:
                expert_block(i, main_sems)
            overflow(act, lambda j: expert_block(j, over_sems))

        def final():
            for d in range(KD):
                act.wait_ge(*when(f"x3 {d}"))
                A.activation(hT[:, d, :], xT[:, d, :], ACT.Square) \
                    .then_inc(mark("norm_by_scalar", f"square3 {d}"), 1)
            act.wait_ge(*when("norm3 ready"))
            act.wait_ge(*when("h2 7"))
            rstd(rsB, rb("norm3")[:, 0:TOK], 1.0 / D, "norm_by_scalar", "rstd3", mid_event="read norm3")

        run(locals())

    @block.gpsimd
    def _(pool):
        def head():
            pool.wait_ge(*when("x rows"))
            G.memset(ba, 0.0).then_inc(mark("cleared", "ba zero"), 1)
            G.memset(bcum, 0.0)
            G.memset(blast, 0.0).then_inc(mark("cleared", "bcum zero"), 1)
            G.memset(xp, 0.0).then_inc(mark("cleared", "xp zero"), 1)
            G.memset(raT[0:32, :], 1.0).then_inc(mark("cleared", "raT ones"), 1)

        def step(s):
            s1 = s - 1
            if 0 <= s1 < NPROJ and PROJ[s1][0] == "cv":
                i = PROJ[s1][1]
                pool.wait_ge(*when(f"xp{s1}"))
                x = xp[:, s1 % 2]
                G.tensor_copy(ccT[:, i, 0:3], x[:, SEQ:SEQ + 3])
                G.tensor_copy(ccT[:, i, 3:27].rearrange("p (s t) -> p s t", t=3),
                                   x[:, SAMP0:XPW].rearrange("p (s t) -> p s t", t=7)[:, :, 4:7]) \
                    .then_inc(mark("conv_tails", f"cc{i}"), 1)

        def gla(m):
            if m == 2:
                for s in range(NSEQ):
                    pool.wait_ge(*when("gla2 keT"))
                    if s >= 2:
                        pool.wait_ge(*when(f"gla state product {s - 2} 1"))
                    G.tensor_scalar(kem1[0:32, s % 2, :], keTa[0:32].rearrange("p a b -> p (a b)"),
                                         const("seq")[0:32, s:s + 1], None, ALU.mult) \
                        .then_inc(mark("masked_keys", f"kem1 {s}"), 1)

        def gdn(m):
            if m == 2:
                for s in range(NSEQ):
                    pool.wait_ge(*when("gdn2 ke0"))
                    pool.wait_ge(*when("gdn2 ke1"))
                    pool.wait_ge(*when("gdn2 y0"))
                    pool.wait_ge(*when("gdn2 y1"))
                    if s >= 2:
                        pool.wait_ge(*when(f"gdn state product {s - 2} 1"))
                    G.tensor_scalar(kem2[0:32, s % 2, :], ke[0:32].rearrange("p a b -> p (a b)"),
                                         const("seq")[0:32, s:s + 1], None, ALU.mult) \
                        .then_inc(mark("masked_keys", f"kem2 {s}"), 1)

        def router():
            pool.wait_ge(*when("merged 7"))
            pool.wait_ge(*when("wout7 ready"))
            G.memset(rank, 0.0)
            G.memset(comb, 0.0)
            G.memset(rt, 0.0).then_inc(mark("cleared", "rt zero"), 1)

        run(locals())

    @block.sync
    def _(sp):
        n = [0]

        def load(dst, src, event, kind=None):
            kind = kind or f"loaded_{event.replace(' ', '_')}"
            sp.dma_start(dst, src).then_inc(mark(kind, event, by=16), 16)

        load(cst, I["const"], "consts")
        load(crow[0:NC9, :], I["cc"], "c rows")
        for i, (k, (r, c)) in enumerate(VEC.items()):
            src = {"b_ada": I["b_ada"], "norm1": I["norm1_w"], "norm2": I["norm2_w"], "final": I["final_norm_w"],
                   "gla_norm": I["gla_norm_w"], "gdn_norm": I["gdn_norm_w"]}[k]
            sp.dma_start(vrow[r:r + c, :], src.rearrange("(n p) -> n p", p=P)) \
                .then_inc(mark("loaded_vectors", by=16), 16)
        sp.dma_start(cvrow[0:96, :], I["w_conv"].rearrange("t (n p) -> (t n) p", p=P)) \
            .then_inc(mark("loaded_vectors", "vec rows", by=16), 16)
        sp.dma_start(xr[:, 0:2, :], I["x_prompt"].rearrange("(m p) d -> p m d", p=P)) \
            .then_inc(mark("loaded_x", by=16), 16)
        sp.dma_start(xr[0:32, 2, :], I["x_sample"]).then_inc(mark("loaded_x", "x rows", by=16), 16)
        load(cbrow[0:24, :], I["state_conv"], "cb rows")
        sp.dma_start(wsm[:, :, 0:RANK], I["w_in"][:, 3072:3088].rearrange("(k p) n -> p k n", p=P)) \
            .then_inc(mark("loaded_small", by=16), 16)
        sp.dma_start(wsm[:, :, 16:32], I["w_in"][:, 7184:7200].rearrange("(k p) n -> p k n", p=P)) \
            .then_inc(mark("loaded_small", "small weights", by=16), 16)
        sp.dma_start(wa2[0:RANK, :], I["w_gla_a2"]).then_inc(mark("loaded_wa2", by=16), 16)
        sp.dma_start(wa2[RANK:RANK + 1, :], I["b_gla_a"].rearrange("(a n) -> a n", a=1)) \
            .then_inc(mark("loaded_wa2", "wa2", by=16), 16)
        sp.dma_start(adt[:, 0, :], I["gdn_A_log"].rearrange("(a n) -> a n", a=1).to_broadcast([P, HB])) \
            .then_inc(mark("loaded_adt", by=16), 16)
        sp.dma_start(adt[:, 1, :], I["gdn_dt_bias"].rearrange("(a n) -> a n", a=1).to_broadcast([P, HB])) \
            .then_inc(mark("loaded_adt", "adt", by=16), 16)
        sp.dma_start(rtw[:, :, 0:4], I["w_group_router"].rearrange("(k p) n -> p k n", p=P)) \
            .then_inc(mark("loaded_router", by=16), 16)
        sp.dma_start(rtw[:, :, 4:20], I["w_expert_router"].rearrange("(k p) n -> p k n", p=P)) \
            .then_inc(mark("loaded_router", "router weights", by=16), 16)
        sp.dma_start(rtb[:, 0:4], I["b_group_router"].rearrange("(a n) -> a n", a=1).to_broadcast([P, 4])) \
            .then_inc(mark("loaded_rtb", by=16), 16)
        sp.dma_start(rtb[:, 4:20], I["b_expert_router"].rearrange("(a n) -> a n", a=1).to_broadcast([P, 16])) \
            .then_inc(mark("loaded_rtb", "router bias", by=16), 16)
        outs = []
        for n, (name, src) in enumerate(chunks):
            if n >= RING:
                prev = chunks[n - RING][0]
                if prev[0] in ("sgla", "sgdn"):
                    c = prev[1]
                    for s in (2 * c, 2 * c + 1):
                        for g in range(2):
                            sp.wait_ge(*when(f"{'gla' if prev[0] == 'sgla' else 'gdn'} state {s} {g}"))
                    if prev[0] == "sgla":
                        dst = O["gla_s"][2 * c:2 * c + 2].rearrange("s h k v -> k (s h) v")
                    else:
                        dst = O["gdn_s"][2 * c:2 * c + 2].rearrange("s (h a) k v -> k (s h) a v", a=2)
                    s_ = slot(prev)
                    if prev[0] == "sgdn":
                        s_ = s_.rearrange("p k (a v) -> p k a v", a=2)
                    sp.dma_start(dst, s_) \
                        .then_inc(mark(f"stored_slot{(n - RING) % RING}", f"stored {n - RING}", by=16), 16)
                    sp.wait_ge(*when(f"stored {n - RING}"))
                else:
                    sp.wait_ge(*when(used(prev)))
            d_ = slot(name)
            if name[0] == "sgdn":
                d_ = d_.rearrange("p k (a v) -> p k a v", a=2)
            sp.dma_start(d_, src).then_inc(mark(f"loaded_slot{n % RING}", loaded(name), by=16), 16)
        for g in range(6):
            sp.wait_ge(*when(f"read cvo{g}"))
        sp.dma_start(O["conv_p"], newconv[0:3, :]).then_inc(mark("stored", by=16), 16)
        sp.dma_start(O["conv_s"], newconv[3:27, :]).then_inc(mark("stored", by=16), 16)
        sp.dma_start(O["gla_p"].rearrange("h k v -> k h v"), SA).then_inc(mark("stored", by=16), 16)
        sp.dma_start(O["gdn_p"].rearrange("h k v -> k h v"), SB) \
            .then_inc(mark("stored", "small outputs stored", by=16), 16)

        wts = [I[k].rearrange("g e a b -> (g e) a b") for k in ("w_exp_gate", "w_exp_up", "w_exp_down")]

        def load_expert(kind, experts, n, sems):
            sp.dma_start(EW[:, kind, 0:n, :].rearrange("p a (k n) -> p (a k) n", k=4 if kind == 2 else KD),
                         wts[kind][experts].rearrange("a (k p) n -> p (a k) n", p=P)).then_inc(sems[kind], 16)

        sp.wait_ge(*when("gdn2 oT1"))
        sp.wait_ge(*when("gdn2 oT1 ready"))
        sp.wait_ge(*when("small outputs stored"))
        sp.wait_ge(*when(f"act{NPROJ - 1}"))
        for kind in range(3):
            load_expert(kind, slice(0, 2), 2, expert_loaded)
        with sp.Fori(1, NE // 2) as i:
            pair = bass.ds(2 * i, 2)
            sp.wait_ge(main_sems["gate"], i)
            load_expert(0, pair, 2, expert_loaded)
            sp.wait_ge(main_sems["up"], i)
            load_expert(1, pair, 2, expert_loaded)
            sp.wait_ge(main_sems["down"], 2 * i)
            load_expert(2, pair, 2, expert_loaded)

        def over_load(j):
            sp.wait_ge(over_sems["dispatch"], j + 1)
            e = bass.ds(sp.value_load(tab[0:1, bass.ds(j + 1, 1)], min_val=0, max_val=NE - 1), 1)
            for kind in range(3):
                load_expert(kind, e, 1, over_loaded)

        sp.wait_ge(*when("router done"))
        sp.wait_ge(main_sems["down"], NE)
        overflow(sp, over_load)
        for g in range(2):
            for m in range(3):
                sp.wait_ge(*when(f"read y{g}{m}"))
            cs = slice(512 * g, 512 * g + 512)
            sp.dma_start(O["y_p"].rearrange("(m p) d -> p m d", p=P)[:, :, cs], yrow[:, 0:2, cs]) \
                .then_inc(mark("stored", by=16), 16)
            sp.dma_start(O["y_s"][:, cs], yrow[0:32, 2, cs]) \
                .then_inc(mark("stored", f"all stored{g}", by=16), 16)
        sp.wait_ge(*when("all stored1"))

    return S.marks


_SHAPES = {
    "y_p": (SEQ, D), "y_s": (NSEQ * DT, D), "gla_p": (HA, DKA, DVA), "gdn_p": (HB, DKB, DVB), "conv_p": (3, 3072),
    "gla_s": (NSEQ, HA, DKA, DVA), "gdn_s": (NSEQ, HB, DKB, DVB), "conv_s": (NSEQ * 3, 3072),
}
_NAMES = ("w_ada", "b_ada", "norm1_w", "w_in", "w_gla_a2", "b_gla_a", "gla_norm_w", "w_conv", "gdn_A_log",
          "gdn_dt_bias", "gdn_norm_w", "w_out", "norm2_w", "w_group_router", "b_group_router", "w_expert_router",
          "b_expert_router", "w_exp_gate", "w_exp_up", "w_exp_down")


def lay_out(inputs):
    a = {k: np.ascontiguousarray(np.asarray(inputs[k])[0]) for k in _NAMES}
    a["final_norm_w"] = np.asarray(inputs["final_norm_w"])
    a["x_prompt"] = np.asarray(inputs["x_prompt"]).reshape(SEQ, D)
    a["x_sample"] = np.asarray(inputs["x_sample"]).reshape(NSEQ * DT, D)
    a["cc"] = np.concatenate([np.asarray(inputs["c_prompt"]), np.asarray(inputs["c_sample"])], axis=0)
    a["state_gla"] = np.asarray(inputs["state_gla"])[0]
    a["state_gdn"] = np.asarray(inputs["state_gdn"])[0]
    a["state_conv"] = np.asarray(inputs["state_conv"]).reshape(NSEQ * 3, 3072)
    a["const"] = CONST
    return {k: np.ascontiguousarray(v) for k, v in a.items()}


def kernel(**inputs):
    import concourse.bacc as bacc
    from concourse.bass_utils import run_bass_kernel_spmd

    arrays = lay_out(inputs)
    counts = None
    for _ in range(2):
        nc = bacc.Bacc("TRN2", target_bir_lowering=False, num_devices=1)
        ins = {k: nc.dram_tensor("in_" + k, v.shape, F32, kind="ExternalInput").ap() for k, v in arrays.items()}
        outs = {k: nc.dram_tensor("out_" + k, s, F32, kind="ExternalOutput").ap() for k, s in _SHAPES.items()}
        counts = program(nc, ins, outs, counts)
    r = run_bass_kernel_spmd(nc, [{"in_" + k: v for k, v in arrays.items()}], core_ids=[0]).results[0]
    o = {k: r["out_" + k] for k in _SHAPES}
    return (o["y_p"].reshape(1, SEQ, D), o["y_s"].reshape(NSEQ, DT, D),
            o["gla_p"].reshape(1, 1, HA, DKA, DVA), o["gdn_p"].reshape(1, 1, HB, DKB, DVB),
            o["conv_p"].reshape(1, 1, 3, 3072), o["gla_s"].reshape(1, NSEQ, HA, DKA, DVA),
            o["gdn_s"].reshape(1, NSEQ, HB, DKB, DVB), o["conv_s"].reshape(1, NSEQ, 3, 3072))
```

```python
from contextlib import ExitStack

import numpy as np

import concourse.bass as bass
import concourse.mybir as mybir

F32 = mybir.dt.float32
ALU = mybir.AluOpType
ACT = mybir.ActivationFunctionType
AX = mybir.AxisListType.X

P = 128
D = 1024
KD = D // P
SEQ, NSEQ, DT = 256, 8, 4
TOK = SEQ + NSEQ * DT
NC9 = 1 + NSEQ
TILES = ((0, 128), (128, 128), (256, 32))
HA, DKA, DVA = 4, 128, 256
HB, DKB, DVB = 8, 128, 128
RANK = 16
TAU = 16.0
TAPS = 4
NG, EPG = 4, 4
NE = NG * EPG
DE = 512
EPS = 1e-6
CONV0 = 3088
CT = 24
XPW = 3 + SEQ + NSEQ * (3 + DT)
YW = XPW - 3
SAMP0 = 3 + SEQ
LEVELS = 7

PROJ = ([("qa", i, 128 * i) for i in range(4)] + [("ka", i, 512 + 128 * i) for i in range(4)]
        + [("va", i, 1024 + 128 * i) for i in range(8)]
        + [("cv", i, CONV0 + 128 * i) for i in range(CT)]
        + [("ga", i, 2048 + 128 * i) for i in range(8)]
        + [("gsa", i, 7200 + 128 * i) for i in range(8)]
        + [("zb", i, 6160 + 128 * i) for i in range(8)]
        + [("gsb", i, 8224 + 128 * i) for i in range(8)])
NPROJ = len(PROJ)
GSA0 = 48
NPROJ_CV = 32
SLOTS = 64
PAIR = 2 * SLOTS
MORE = -(-(TOK - SLOTS) // PAIR)
OVER = 2 * TOK // (SLOTS + 1)
CW = 256
RING = 5
ADA_FIRST, ADA_STEP = 1, 2
GLA_AT = ((21, 22, 23, 23, 24, 25), (25, 26, 27, 27, 28, 29), (29, 30, 31, 33, 34, 35))
GDN_AT = (38, 53, 68)
CONV_OUT_AT = 46
MERGE_GLA_AT = 64

VEC = {"b_ada": (0, 48), "norm1": (48, 8), "norm2": (56, 8), "final": (64, 8), "gla_norm": (72, 2),
       "gdn_norm": (74, 1)}
NVEC = 75


def constants():
    p = np.arange(P)
    parts = {"ident": np.eye(P), "ones": np.ones((P, P)), "tri": (p[:, None] <= p[None, :]) * 1.0}
    for lv in range(LEVELS):
        b = 1 << lv
        s, t = p[:, None], p[None, :]
        parts[f"level{lv}"] = ((s // (2 * b) == t // (2 * b)) & (s % (2 * b) < b) & (t % (2 * b) >= b)) * 1.0
    q = np.arange(32)
    same = (q[:, None] // DT == q[None, :] // DT)
    pad = lambda a: np.concatenate([a, np.zeros((P - a.shape[0], a.shape[1]))])
    parts["tri_s"] = pad(same & (q[:, None] <= q[None, :]))
    parts["same_s"] = pad(same)
    parts["seq"] = pad(q[:, None] // DT == np.arange(NSEQ)[None, :])
    parts["eps"] = np.full((P, 1), EPS)
    q32 = np.arange(P)
    parts["fold"] = (q32[:, None] % 32 == np.arange(32)[None, :]) * 1.0
    parts["lnq"] = np.full((P, 1), np.log(DKB ** -0.5))
    parts["iota"] = np.tile(np.arange(float(P))[None, :], (P, 1))
    r, e = np.arange(MORE * NE) // NE, np.arange(MORE * NE) % NE
    parts["over_at"] = pad((SLOTS + PAIR * r * 1.0)[:, None])
    parts["over_expert"] = pad(np.tile((1.0 * e)[:, None], (1, P)))
    parts["over_base"] = pad(np.tile((SLOTS + PAIR * r * 1.0)[:, None], (1, P)))
    off, at = 0, {}
    for k, a in parts.items():
        at[k] = (off, a.shape[1])
        off += a.shape[1]
    return np.concatenate([np.asarray(a, np.float32) for a in parts.values()], axis=1), at


CONST, CONST_AT = constants()


class Signals:

    def __init__(self, nc, ctx, counts):
        self.nc, self.ctx, self.counts = nc, ctx, counts
        self.sems, self.value, self.marks = {}, {}, {}

    def sem(self, kind):
        if kind not in self.sems:
            self.sems[kind] = self.ctx.enter_context(self.nc.semaphore(kind))
            self.value[kind] = 0
        return self.sems[kind]

    def mark(self, kind, *events, by=1):
        sem = self.sem(kind)
        self.value[kind] += by
        for event in events:
            assert event not in self.marks, event
            self.marks[event] = (kind, self.value[kind])
        return sem

    def when(self, event):
        kind, value = ("first_building", 1) if self.counts is None else self.counts[event]
        return self.sem(kind), value



def program(nc, ins, outs, known=None):
    ctx = ExitStack()
    with ctx:
        return _program(nc, ctx, ins, outs, known)


def _program(nc, ctx, I, O, known):
    S = Signals(nc, ctx, known)
    mark, when = S.mark, S.when

    ARENA = 53200
    arena = ctx.enter_context(nc.sbuf_tensor("arena", [P, ARENA], F32))
    top = [0]

    def carve(*shape, at=None):
        n = int(np.prod(shape))
        o = top[0] if at is None else at
        if at is None:
            top[0] += n
        assert o + n <= ARENA, (o, n)
        v = arena[:, o:o + n]
        if len(shape) == 2:
            v = v.rearrange("p (a b) -> p a b", b=shape[1])
        elif len(shape) == 3:
            v = v.rearrange("p (a b c) -> p a b c", b=shape[1], c=shape[2])
        return v

    xT = carve(KD, TOK)
    hT = carve(KD, TOK)
    modT = carve(48, NC9)
    A1, A2 = carve(KD, NC9), carve(KD, NC9)
    csT = carve(KD * NC9 + 32 - NC9)
    adaq = carve(CW)
    vecT = carve(NVEC)
    cst = carve(CONST.shape[1])
    rsB = carve(TOK)
    rtw = carve(KD * 20 + 12)
    rtb = carve(20)
    gs = carve(2, 32)
    persistent = top[0]

    def const(name):
        o, n = CONST_AT[name]
        return cst[:, o:o + n]

    ident, ones, tri = const("ident"), const("ones"), const("tri")
    FOLD = const("fold")
    TRI = (tri, tri, const("tri_s"))
    LAST = (ones, ones, const("same_s"))

    W = carve(RING, KD, CW)
    GA = carve(KD, TOK)
    QKA = carve(KD, TOK)
    GB_at = top[0]
    GB = carve(KD, TOK)
    qB = carve(KD, TOK)
    mixer_only = top[0]
    kB = carve(KD, TOK)
    vA_at = top[0]
    vA = carve(3, D)
    vB = carve(3, D)
    convT_at = top[0]
    convT = carve(96)
    cbT = carve(CT, 24)
    ccT = carve(CT, 27)
    wsm = carve(KD, 32)
    raT_at = top[0]
    raT = carve(TOK)
    wa2_at = top[0]
    wa2 = carve(512)
    ba = carve(3, 16)
    beta = carve(3, HB)
    gB = carve(3, HB)
    gt = carve(3, HB)
    adt = carve(2, HB)
    bcum = carve(3, HB)
    blast = carve(3, HB)
    ebB, elB, eSd = carve(3, HB), carve(3, HB), carve(3, HB)
    gseq = carve(NSEQ, HB)
    eSs = carve(NSEQ, HB)
    xp = carve(2, XPW)
    yb = carve(4, YW)
    sgm = carve(4, YW)
    sqb = carve(2, TOK)
    rsb = carve(2, TOK)
    SA_at = top[0]
    SA = carve(HA, DVA)
    SB = carve(HB, DVB)
    ebl = carve(HA, NSEQ)
    ssum = carve(HB)
    srs = carve(HB)
    oSt = carve(256, at=raT_at)
    oSt2 = carve(256, at=wa2_at)
    work = top[0]
    E = carve(HB, P)
    AT = carve(HB, P)
    LT = carve(HB, P)
    Lm = carve(HB, P)
    Y = carve(HB, P)
    X_at = top[0]
    X = carve(HB, 2, P)
    R = carve(HB, P)
    tg = carve(HB, P, at=X_at)
    kem2 = carve(2, D, at=X_at)
    ke = LT
    gA = carve(HA, P, at=work)
    Eb = carve(HA, P, at=work + 512)
    Ep = carve(HA, P, at=work + 1024)
    Em = carve(HA, P, at=work + 1536)
    El = carve(HA, P, at=work + 2048)
    ATa = carve(HA, P, at=work + 2560)
    keTa = carve(HA, P, at=work + 3072)
    oNa = carve(D, at=work + 3584)
    kem1 = carve(2, 512, at=work + 4608)
    oNb = Y.rearrange("p a b -> p (a b)")
    BLK = 32 + DT
    qbM = carve(HA, NSEQ * BLK, at=work + 5632)
    kM = carve(HB, NSEQ * BLK, at=vA_at)
    qM = (carve(HA, NSEQ * BLK, at=SA_at), carve(HA, NSEQ * BLK, at=convT_at))
    sqo = Lm
    xr = vB
    cbrow = carve(3072, at=persistent + RING * KD * CW)
    crow = carve(D, at=GB_at)
    csx = carve(2, D, at=vA_at + 0)
    vrow = carve(P, at=GB_at + 1024)
    cvrow = carve(P, at=GB_at + 1152)
    newconv = carve(3072, at=vA_at)
    EW = carve(3, 2, 4096, at=mixer_only)
    yrow = carve(3, D, at=mixer_only)
    top[0] = persistent
    h2t = carve(3, D)
    acc = carve(KD, TOK)
    Dg, Dc = carve(3, 2, SLOTS), carve(3, 2, SLOTS)
    DT_ = carve(TOK)
    hg = carve(KD, PAIR)
    hid = carve(DE)
    sg2 = carve(DE)
    hidT = carve(4, PAIR)
    yt = carve(D)
    rparts = carve(TOK)
    rt = carve(3, 20)
    rs_ = {}
    for n in ["gmax", "gden", "gw", "hit", "idx", "gsel", "el", "emax", "p1", "h1", "p2", "within", "tmp", "i1",
              "w1", "w2", "dd", "hh"]:
        rs_[n] = carve(3, 4)
    el16 = carve(3, 16)
    sel = carve(3, NE)
    comb, rank = carve(3, NE + 2), carve(3, NE + 2)
    sel4 = carve(3, MORE * NE)
    over = carve(40)
    oneh = carve(OVER)
    expB, rankO, combO = carve(OVER), carve(3, OVER), carve(3, OVER)
    rankJ, combJ = carve(3), carve(3)
    hitE = carve(NE)
    tabf = carve(2 * OVER + 2)
    tab = carve(2 * OVER + 2).bitcast(mybir.dt.int32)
    assert top[0] <= mixer_only

    pm = [ctx.enter_context(nc.psum_tensor(f"bank{i}", [P, 512], F32)) for i in range(8)]

    T, V, A, G = nc.tensor, nc.vector, nc.scalar, nc.gpsimd
    block = ctx.enter_context(nc.Block())

    def cols(w, c0, n=CW):
        return w[:, c0:c0 + n].rearrange("(k p) n -> p k n", p=P)

    chunks = []
    chunk_of = {}

    def add(name, src):
        chunk_of[name] = len(chunks)
        chunks.append((name, src))

    def slot(name):
        return W[:, chunk_of[name] % RING]

    def loaded(name):
        return f"chunk {chunk_of[name]}"

    def used(name):
        return f"used {chunk_of[name]}"

    GLA_PARTS = ("decays", "sums", "scores", "states_read", "out", "turn")

    def gdn_parts(m):
        levels = LEVELS if m < 2 else 2
        return ["gdn_scores"] + [("gdn_level", lv) for lv in range(levels)] + ["gdn_values", "gdn_out", "gdn_turn"]

    stands_after = {}
    for m, steps in enumerate(GLA_AT):
        for part, at in zip(GLA_PARTS, steps):
            stands_after.setdefault(at, []).append((f"gla_{part}", m))
    for m, first in enumerate(GDN_AT):
        for i, part in enumerate(gdn_parts(m)):
            item = (part, m) if isinstance(part, str) else (part[0], m, part[1])
            stands_after.setdefault(first + i, []).append(item)
    schedule = [("head",)]
    for c in range(8):
        schedule += [("ada", c)] + ([("fold", c - 1)] if c else [])
        if c == 2:
            schedule.append(("norm_sums", 1))
    schedule += [("fold", 7), ("norm", 1), ("small",)]
    ADA_AT = {ADA_FIRST + ADA_STEP * i: 8 + i for i in range(16)}
    for s in range(NPROJ + 6):
        schedule.append(("step", s))
        if s == 1:
            schedule.append(("sums",))
        if s in ADA_AT:
            schedule.append(("ada", ADA_AT[s]))
        if s - 1 in ADA_AT:
            schedule.append(("fold", ADA_AT[s - 1]))
        schedule += stands_after.get(s, [])
        if s == MERGE_GLA_AT:
            schedule.append(("merge_gla",))
        if s == CONV_OUT_AT:
            schedule.append(("conv_out",))
    schedule += [("merge",), ("wout",), ("norm_sums", 2), ("norm", 2), ("router",), ("experts",), ("final",)]

    for item in schedule:
        kind, c = item[0], item[-1]
        if kind == "ada":
            add(("ada", c), cols(I["w_ada"], CW * c))
        elif kind == "step" and c % 2 == 0 and c < NPROJ:
            add(("win", c), cols(I["w_in"], PROJ[c][2]))
        elif item == ("gla_states_read", 2):
            for i in range(4):
                add(("sgla", i), I["state_gla"][2 * i:2 * i + 2].rearrange("s h k v -> k (s h) v"))
        elif item == ("gdn_values", 2):
            for i in range(4):
                add(("sgdn", i), I["state_gdn"][2 * i:2 * i + 2].rearrange("s (h a) k v -> k (s h) a v", a=2))
        elif kind == "wout":
            for i in range(4):
                add(("wout", i), cols(I["w_out"], CW * i))

    ring_names = []

    def ring_bank(name):
        n = len(ring_names)
        if n >= 4:
            PE[0].wait_ge(*when(f"read {ring_names[n - 4]}"))
        ring_names.append(name)
        banks[name] = n % 4
        return pm[n % 4]

    banks = {} if known is None else known["#banks"]
    if known is None:
        S.marks["#banks"] = banks
    PE = [None]
    free = {}

    def take(b, reader):
        if b in free:
            PE[0].wait_ge(*when(free[b]))
        free[b] = reader
        return pm[b]

    def rb(name):
        return pm[banks.get(name, 0)]

    def mm(out, lhsT, rhs, start=True, stop=True):
        return T.matmul(out, lhsT, rhs, start=start, stop=stop)

    def tr(out, in_, n):
        return T.transpose(out, in_, ident[0:n, 0:n])

    def bc(ap, n):
        return ap.unsqueeze(2).to_broadcast([ap.shape[0], ap.shape[1], n])

    def mid(ap, n):
        return ap.unsqueeze(1).to_broadcast([ap.shape[0], n, ap.shape[1]])

    def y_free(s):
        kind = PROJ[s][0] if s >= 0 else None
        if kind in ("qa", "ka", None):
            return []
        return [f"tr{s} ready"] if kind == "va" else [f"act{s}", f"ln{s}"]

    def sg_free(s):
        kind = PROJ[s][0] if s >= 0 else None
        if kind in ("qa", "ka", "va", None):
            return []
        return [f"act{s}"] + ([f"tr{s} ready"] if kind == "cv" and PROJ[s][1] >= 16 else [])

    def named(prefix, names):
        return {n: ctx.enter_context(nc.semaphore(f"{prefix}_{n}")) for n in names}

    STEPS = ("dispatch", "scatter_matrix", "scatter_matrix_read", "gathered", "gather_read0", "gather_read1", "gate",
             "up", "softplus_step", "softplus", "log_sigmoid", "sigmoid", "silu", "hidden", "turned", "turned_read",
             "down", "down_read0", "down_read1", "scattered", "added", "picked")
    main_sems, over_sems = named("expert", STEPS), named("overflow", STEPS)
    expert_loaded = [ctx.enter_context(nc.semaphore(f"expert_loaded{i}")) for i in range(3)]
    over_loaded = [ctx.enter_context(nc.semaphore(f"overflow_loaded{i}")) for i in range(3)]

    def overflow(eng, one_block):
        blocks = eng.value_load(tab[0:1, 0:1], min_val=0, max_val=OVER)
        with eng.If(blocks > 0):
            with eng.Fori(0, blocks) as j:
                one_block(j)

    def run(fns):
        for item in schedule:
            f = fns.get(item[0])
            if f is not None:
                f(*item[1:])

    @block.tensor
    def _(pe):
        PE[0] = pe

        def head():
            pe.wait_ge(*when("consts"))
            pe.wait_ge(*when("vec rows"))
            b = ring_bank("vec")
            tr(b[:, 0:NVEC], vrow[0:NVEC, :], NVEC)
            tr(b[:, 128:224], cvrow[0:96, :], 96).then_inc(mark("head_transposed", "vec ready"), 1)
            pe.wait_ge(*when("x rows"))
            for d in range(KD):
                b = ring_bank(f"x{d}")
                for m, (o, n) in enumerate(TILES):
                    last = tr(b[:, o:o + n], xr[0:n, m, 128 * d:128 * d + 128], n)
                last.then_inc(mark("head_transposed", f"x{d} ready"), 1)
            pe.wait_ge(*when("cb rows"))
            for g in range(2):
                b = ring_bank(f"cb{g}")
                for j in range(12):
                    c = 12 * g + j
                    last = tr(b[:, 24 * j:24 * j + 24], cbrow[0:24, 128 * c:128 * c + 128], 24)
                last.then_inc(mark("head_transposed", f"cb{g} ready"), 1)
            b = ring_bank("c")
            for k in range(KD):
                last = tr(b[:, NC9 * k:NC9 * k + NC9], crow[0:NC9, 128 * k:128 * k + 128], NC9)
            last.then_inc(mark("head_transposed", "c ready"), 1)

        def ada(c):
            pe.wait_ge(*when(loaded(("ada", c))))
            pe.wait_ge(*when("read c"))
            pe.wait_ge(*when("c padding"))
            w = slot(("ada", c))
            b = take(7 - 2 * (c % 2), f"read ada{c}")
            for k in range(KD):
                q = k % 4
                last = mm(b[32 * q:32 * q + 32, 0:CW], csT[:, NC9 * k:NC9 * k + 32], w[:, k, :], k < 4, k >= 4)
            last.then_inc(mark("ada_products", f"ada{c} ready", used(("ada", c))), 1)

        def fold(c):
            pe.wait_ge(*when(f"read ada{c}"))
            b = take(6, f"read fold{c}")
            for j in range(2):
                last = mm(b[:, NC9 * j:NC9 * j + NC9], adaq[:, 128 * j:128 * j + 128], FOLD[:, 0:NC9])
            last.then_inc(mark("ada_products", f"fold{c} ready"), 1)

        def norm_sums(i):
            b = ring_bank(f"norm{i}")
            for d in range(KD):
                pe.wait_ge(*when(f"square{i} {d}"))
                last = mm(b[:, 0:TOK], ones, hT[:, d, :], d == 0, d == KD - 1)
            last.then_inc(mark("norm_sums", f"norm{i} ready"), 1)

        def small():
            pe.wait_ge(*when("small weights"))
            b = ring_bank("small parts")
            for k in range(KD):
                pe.wait_ge(*when(f"h1 {k}"))
                pe.wait_ge(*when(f"hp1 {k}"))
                q = k % 4
                last = mm(b[32 * q:32 * q + 32, 0:TOK], wsm[:, k, :], hT[:, k, :], k < 4, k >= 4)
            last.then_inc(mark("small_products", "small parts ready"), 1)
            pe.wait_ge(*when("read small parts"))
            parts = yb[:, 0, 0:TOK]
            b = ring_bank("ra")
            mm(b[0:RANK, 0:TOK], FOLD[:, 0:RANK], parts).then_inc(mark("small_products", "ra ready"), 1)
            b = ring_bank("ba")
            for m, (o, n) in enumerate(TILES):
                last = mm(b[0:n, 16 * m:16 * m + 16], parts[:, o:o + n], FOLD[:, RANK:RANK + 16])
            last.then_inc(mark("small_products", "ba ready"), 1)

        def sums():
            pe.wait_ge(*when("g"))
            b = ring_bank("bcum")
            for m, (o, n) in enumerate(TILES):
                mm(b[0:n, 8 * m:8 * m + 8], TRI[m][0:n, 0:n], gB[0:n, m, :])
                mm(b[0:n, 32 + 8 * m:40 + 8 * m], LAST[m][0:n, 0:n], gB[0:n, m, :])
            last = mm(b[:, 64:64 + 64], ones[0:32, :], gseq[0:32].rearrange("p s h -> p (s h)"))
            last.then_inc(mark("small_products", "bcum ready"), 1)

        def step(s):
            if s < NPROJ:
                name = ("win", s - s % 2)
                pe.wait_ge(*when(loaded(name)))
                w = slot(name)
                j = s % 2
                b = ring_bank(f"proj{s}")
                for k in range(KD):
                    last = mm(b[:, 0:TOK], w[:, k, 128 * j:128 * j + 128], hT[:, k, :], k == 0, k == KD - 1)
                last.then_inc(mark("projected", f"proj{s} ready", *([used(name)] if j == 1 else [])), 1)
            s5 = s - 5
            if 0 <= s5 < NPROJ:
                kind, i, _ = PROJ[s5]
                if kind == "cv" and i < 16:
                    pe.wait_ge(*when(f"sq{s5}"))
                    b = ring_bank(f"ssq{s5}")
                    mm(b[:, 0:TOK], ones, sqb[:, s5 % 2, :]).then_inc(mark("norm_sums", f"ssq{s5} ready"), 1)
                if kind == "va" or (kind == "cv" and i >= 16):
                    pe.wait_ge(*when(f"y{s5}" if kind == "va" else f"act{s5}"))
                    b = ring_bank(f"tr{s5}")
                    src = yb[:, s5 % 4] if kind == "va" else sgm[:, s5 % 4]
                    for m, (o, n) in enumerate(TILES):
                        last = tr(b[0:n, 128 * m:128 * m + 128], src[:, o:o + n], 128)
                    last.then_inc(mark("transposed", f"tr{s5} ready"), 1)

        def gla_decays(m):
            o, n = TILES[m]
            t = f"gla{m} "
            pe.wait_ge(*when("wa2"))
            b = take(4, t + "logits read")
            mm(b[0:n, :], raT[0:RANK + 1, o:o + n], wa2[0:RANK + 1, :]) \
                .then_inc(mark("gla_products", t + "logits"), 1)

        def gla_sums(m):
            o, n = TILES[m]
            t = f"gla{m} "
            pe.wait_ge(*when(t + "log decay"))
            b = take(5, t + "cum read")
            for h in range(HA):
                last = mm(b[:, n * h:n * h + n], gA[0:n, h, :], TRI[m][0:n, 0:n])
            last.then_inc(mark("gla_products", t + "cum"), 1)

        def gla_scores(m):
            o, n = TILES[m]
            t = f"gla{m} "
            pe.wait_ge(*when(t + "qq"))
            pe.wait_ge(*when(t + "kk"))
            b = take(6, t + "A read")
            for h in range(HA):
                last = mm(b[0:n, n * h:n * h + n], Em[:, h, 0:n], Ep[:, h, 0:n])
            last.then_inc(mark("gla_products", t + "A"), 1)
            pe.wait_ge(*when(t + "ke"))
            b = take(7, t + "keT")
            for h in range(HA):
                last = tr(b[0:n, 128 * h:128 * h + 128], El[:, h, 0:n], 128)
            last.then_inc(mark("gla_products", t + "ke transposed"), 1)

        def gla_states_read(m):
            o, n = TILES[m]
            t = f"gla{m} "
            if m == 2:
                b = take(6, t + "oS")
                for s_ in range(NSEQ):
                    pe.wait_ge(*when(loaded(("sgla", s_ // 2))))
                    w = slot(("sgla", s_ // 2)).rearrange("p (s h) v -> p s h v", h=HA)
                    for h in range(HA):
                        last = mm(b[32 * h:32 * h + 32, 0:DVA], qbM[:, h, 32 * s_:32 * s_ + 32], w[:, s_ % 2, h, :],
                                  s_ == 0, s_ == NSEQ - 1)
                last.then_inc(mark("gla_products", t + "oS ready"), 1)
                pe.wait_ge(*when(t + "oS"))

        def gla_out(m):
            o, n = TILES[m]
            t = f"gla{m} "
            for g in range(2):
                b = take(4 + g, t + f"o{g} read")
                for hh in range(2):
                    h = 2 * g + hh
                    out = b[0:n, 256 * hh:256 * hh + 256]
                    last = mm(out, ATa[0:n, h, 0:n], vA[0:n, m, 256 * h:256 * h + 256], True, m == 0)
                    if m == 1:
                        last = mm(out, Eb[:, h, 0:n], SA[:, h, :], False, True)
                    if m == 2:
                        last = mm(out, ident[:, 32 * h:32 * h + 32], oSt, False, True)
                last.then_inc(mark("gla_products", t + f"o{g} ready"), 1)
            pe.wait_ge(*when(t + "keT"))
            if m < 2:
                for g in range(2):
                    b = take(6 + g, t + f"S{g} read")
                    for hh in range(2):
                        h = 2 * g + hh
                        last = mm(b[:, 256 * hh:256 * hh + 256], keTa[0:n, h, :], vA[0:n, m, 256 * h:256 * h + 256])
                    last.then_inc(mark("gla_products", t + f"S{g} ready"), 1)
            else:
                for s in range(NSEQ):
                    pe.wait_ge(*when(f"kem1 {s}"))
                    for g in range(2):
                        b = take(6 + g, f"gla state {s} {g}")
                        for hh in range(2):
                            h = 2 * g + hh
                            last = mm(b[:, 256 * hh:256 * hh + 256], kem1[0:32, s % 2, 128 * h:128 * h + 128],
                                      vA[0:32, 2, 256 * h:256 * h + 256])
                        last.then_inc(mark("gla_products", f"gla state product {s} {g}"), 1)

        def gla_turn(m):
            o, n = TILES[m]
            t = f"gla{m} "
            for g in range(2):
                pe.wait_ge(*when(t + "oN"))
                b = take(4 + g, t + f"oT{g}")
                for j in range(4):
                    c = 4 * g + j
                    last = tr(b[:, 128 * j:128 * j + n], oNa[0:n, 128 * c:128 * c + 128], n)
                last.then_inc(mark("gla_products", t + f"oT{g} ready"), 1)

        def conv_out():
            for i in range(CT):
                pe.wait_ge(*when(f"cc{i}"))
            for g in range(6):
                b = ring_bank(f"cvo{g}")
                for j in range(4):
                    last = tr(b[0:27, 128 * j:128 * j + 128], ccT[:, 4 * g + j, :], 128)
                last.then_inc(mark("transposed", f"cvo{g} ready"), 1)

        def gdn_scores(m):
            o, n = TILES[m]
            t = f"gdn{m} "
            HG = 4
            pe.wait_ge(*when(t + "tg"))
            for g in range(2):
                b = take(4 + g, t + f"D{g}")
                mm(b[0:n, 0:HG * n], ones[0:n, 0:n], tg[0:n, HG * g:HG * g + HG, 0:n]) \
                    .then_inc(mark("gdn_products", t + f"bc{g}"), 1)
            for g in range(2):
                b = take(6 + g, t + f"KK{g} read")
                for j in range(HG):
                    h = HG * g + j
                    last = mm(b[0:n, n * j:n * j + n], kB[:, h, o:o + n], kB[:, h, o:o + n])
                last.then_inc(mark("gdn_products", t + f"KK{g}"), 1)
            for g in range(2):
                b = take(4 + g, t + f"AT{g}")
                for j in range(HG):
                    h = HG * g + j
                    last = mm(b[0:n, n * j:n * j + n], kB[:, h, o:o + n], qB[:, h, o:o + n])
                last.then_inc(mark("gdn_products", t + f"QK{g}"), 1)

        def gdn_level(m, lv):
            o, n = TILES[m]
            t = f"gdn{m} "
            HG = 4
            levels = LEVELS if m < 2 else 2
            for g in range(2):
                pe.wait_ge(*when(t + f"Lm{lv} {g}"))
                b = take(4 + g, t + f"Y{lv} {g}")
                for j in range(HG):
                    h = HG * g + j
                    rhs = ident[0:n, 0:n] if lv == 0 else X[0:n, h, 1, 0:n]
                    last = mm(b[0:n, n * j:n * j + n], Lm[0:n, h, 0:n], rhs)
                last.then_inc(mark("gdn_products", t + f"Y{lv} {g} ready"), 1)
            if lv == 0:
                return
            for g in range(2):
                pe.wait_ge(*when(t + f"Y{lv} {g}"))
                b = take(6 + g, t + f"XT{lv} {g}")
                for j in range(HG):
                    h = HG * g + j
                    last = mm(b[0:n, n * j:n * j + n], Y[0:n, h, 0:n], X[0:n, h, 0, 0:n])
                last.then_inc(mark("gdn_products", t + f"ZT{lv} {g}"), 1)
                if lv < levels - 1:
                    b = take(4 + g, t + f"X{lv} {g}")
                    for j in range(HG):
                        h = HG * g + j
                        last = mm(b[0:n, n * j:n * j + n], X[0:n, h, 0, 0:n], Y[0:n, h, 0:n])
                    last.then_inc(mark("gdn_products", t + f"Z{lv} {g}"), 1)

        def gdn_values(m):
            o, n = TILES[m]
            t = f"gdn{m} "
            HG = 4
            levels = LEVELS if m < 2 else 2
            for g in range(2):
                b = take(4 + g, t + f"ke{g}")
                for j in range(HG):
                    last = tr(b[0:n, 128 * j:128 * j + 128], kB[:, HG * g + j, o:o + n], 128)
                last.then_inc(mark("gdn_products", t + f"kT{g}"), 1)
            if m == 1:
                for g in range(2):
                    b = take(6 + g, t + f"R{g}")
                    for j in range(HG):
                        h = HG * g + j
                        last = mm(b[:, 128 * j:128 * j + 128], kB[:, h, o:o + n], SB[:, h, :])
                    last.then_inc(mark("gdn_products", t + f"kS{g}"), 1)
            if m == 2:
                bk, bq = take(6, t + "kSs"), take(7, t + "qSs")
                pe.wait_ge(*when(t + "kM"))
                pe.wait_ge(*when(t + "qM"))
                for bank, blocks in ((bk, (kM[:, 0:HG], kM[:, HG:HB])), (bq, qM)):
                    for g in range(2):
                        for s_ in range(NSEQ):
                            pe.wait_ge(*when(loaded(("sgdn", s_ // 2))))
                            w = slot(("sgdn", s_ // 2)).rearrange("p k n -> p (k n)") \
                                .rearrange("p (s h v) -> p s h v", h=HB, v=DVB)
                            for j in range(HG):
                                last = mm(bank[32 * j:32 * j + 32, DVB * g:DVB * g + DVB],
                                          blocks[g][:, j, 32 * s_:32 * s_ + 32], w[:, s_ % 2, HG * g + j, :],
                                          s_ == 0, s_ == NSEQ - 1)
                last.then_inc(mark("gdn_products", t + "Ss"), 1)
                pe.wait_ge(*when(t + "kSs"))
                for g in range(2):
                    b = take(6 + g, t + f"R{g}")
                    for j in range(HG):
                        last = mm(b[0:n, 128 * j:128 * j + 128], ident[:, 32 * j:32 * j + 32],
                                  oSt[:, 128 * g:128 * g + 128])
                    last.then_inc(mark("gdn_products", t + f"kS{g}"), 1)
            for g in range(2):
                pe.wait_ge(*when(t + f"XT{levels - 1} {g}"))
                if m:
                    pe.wait_ge(*when(t + f"R{g}"))
                else:
                    for c in range(8):
                        pe.wait_ge(*when(f"vbtok{c}"))
                b = take(4 + g, t + f"vn{g}")
                for j in range(HG):
                    h = HG * g + j
                    rhs = vB[0:n, m, 128 * h:128 * h + 128] if m == 0 else R[0:n, h, :]
                    last = mm(b[0:n, 128 * j:128 * j + 128], X[0:n, h, 0, 0:n], rhs)
                last.then_inc(mark("gdn_products", t + f"y{g}"), 1)

        def gdn_out(m):
            o, n = TILES[m]
            t = f"gdn{m} "
            HG = 4
            for g in range(2):
                if m == 1:
                    b = take(6 + g, t + f"qS{g} read")
                    for j in range(HG):
                        h = HG * g + j
                        last = mm(b[:, 128 * j:128 * j + 128], qB[:, h, o:o + n], SB[:, h, :])
                    last.then_inc(mark("gdn_products", t + f"qS{g}"), 1)
                if m == 2:
                    b = take(6 + g, t + f"qS{g} read")
                    for j in range(HG):
                        last = mm(b[0:n, 128 * j:128 * j + 128], ident[:, 32 * j:32 * j + 32],
                                  oSt2[:, 128 * g:128 * g + 128])
                    last.then_inc(mark("gdn_products", t + f"qS{g}"), 1)
            for g in range(2):
                pe.wait_ge(*when(t + f"vn{g}"))
                b = take(4 + g, t + f"o{g}")
                for j in range(HG):
                    h = HG * g + j
                    last = mm(b[0:n, 128 * j:128 * j + 128], AT[0:n, h, 0:n], R[0:n, h, :])
                last.then_inc(mark("gdn_products", t + f"o{g} ready"), 1)
            if m < 2:
                for g in range(2):
                    b = take(6 + g, t + f"state{g}")
                    for j in range(HG):
                        h = HG * g + j
                        last = mm(b[:, 128 * j:128 * j + 128], ke[0:n, h, :], R[0:n, h, :])
                    last.then_inc(mark("gdn_products", t + f"S{g} ready"), 1)
            else:
                for s in range(NSEQ):
                    pe.wait_ge(*when(f"kem2 {s}"))
                    for g in range(2):
                        b = take(6 + g, f"gdn state {s} {g}")
                        for j in range(HG):
                            h = HG * g + j
                            last = mm(b[:, 128 * j:128 * j + 128], kem2[0:32, s % 2, 128 * h:128 * h + 128],
                                      R[0:32, h, :])
                        last.then_inc(mark("gdn_products", f"gdn state product {s} {g}"), 1)

        def gdn_turn(m):
            o, n = TILES[m]
            t = f"gdn{m} "
            HG = 4
            for g in range(2):
                pe.wait_ge(*when(t + "oN"))
                b = take(4 + g, t + f"oT{g}")
                for j in range(4):
                    c = 4 * g + j
                    last = tr(b[:, 128 * j:128 * j + n], oNb[0:n, 128 * c:128 * c + 128], n)
                last.then_inc(mark("gdn_products", t + f"oT{g} ready"), 1)

        def wout():
            for c in range(4):
                pe.wait_ge(*when(loaded(("wout", c))))
                w = slot(("wout", c))
                for j in range(2):
                    d = 2 * c + j
                    b = ring_bank(f"wout{d}")
                    for k in range(KD):
                        pe.wait_ge(*when(f"merged {k}"))
                        last = mm(b[:, 0:TOK], w[:, k, 128 * j:128 * j + 128], GA[:, k, :], k == 0, k == KD - 1)
                    last \
                        .then_inc(mark("projected", f"wout{d} ready", *([used(("wout", c))] if j == 1 else [])), 1)

        def router():
            pe.wait_ge(*when("router weights"))
            pe.wait_ge(*when("router padding"))
            b = ring_bank("router parts")
            for k in range(KD):
                pe.wait_ge(*when(f"h2 {k}"))
                pe.wait_ge(*when(f"hp2 {k}"))
                q = k % 4
                last = mm(b[32 * q:32 * q + 32, 0:TOK], rtw[:, 20 * k:20 * k + 32], hT[:, k, :], k < 4, k >= 4)
            last.then_inc(mark("router_products", "router parts ready"), 1)

            def token_major(m):
                o, n = TILES[m]
                for g in range(2):
                    b = ring_bank(f"h2t{m}{g}")
                    for c in range(4):
                        last = tr(b[0:n, 128 * c:128 * c + 128], hT[:, 4 * g + c, o:o + n], 128)
                    last.then_inc(mark("transposed", f"h2t{m}{g} ready"), 1)

            token_major(0)
            pe.wait_ge(*when("read router parts"))
            b = ring_bank("router")
            for m, (o, n) in enumerate(TILES):
                last = mm(b[0:n, 20 * m:20 * m + 20], rparts[:, o:o + n], FOLD[:, 0:20])
            last.then_inc(mark("router_products", "router ready"), 1)
            token_major(1)
            token_major(2)
            pe.wait_ge(*when("sel4"))
            b = ring_bank("rank")
            for m, (o, n) in enumerate(TILES):
                for q in range(m):
                    mm(b[0:n, NE * m:NE * m + NE], ones[:, 0:n], sel[:, q, :], q == 0, False)
                mm(b[0:n, NE * m:NE * m + NE], tri[0:n, 0:n], sel[0:n, m, :], m == 0, True)
            for m, (o, n) in enumerate(TILES):
                last = mm(b[0:MORE * NE, 64:65], sel4[0:n, m, :], ones[0:n, 0:1], m == 0, m == 2)
            last.then_inc(mark("router_products", "rank ready"), 1)
            pe.wait_ge(*when("over flags"))
            q = MORE * NE
            b = ring_bank("over")
            mm(b[0:q, 0:1], tri[0:q, 0:q], over[0:q, 0:1])
            mm(b[0:1, 8:9], over[0:q, 0:1], ones[0:q, 0:1]).then_inc(mark("router_products", "over ready"), 1)

        def expert_block(i, n, loaded_sem, second):
            def products(out, lhs, kind, k, half, K):
                for x in range(2):
                    wt = EW[:, kind, x * second, :].rearrange("p (k n) -> p k n", k=K)
                    last = mm(out[SLOTS * x:SLOTS * x + SLOTS, :], lhs[:, k, SLOTS * x:SLOTS * x + SLOTS],
                              wt[:, k, 512 * half:512 * half + 512], k == 0, k == K - 1)
                return last

            pe.wait_ge(n["dispatch"], i + 1)
            for g in range(2):
                for k in range(4):
                    for m, (o, w) in enumerate(TILES):
                        last = mm(pm[g][:, PAIR * k:PAIR * k + PAIR],
                                  h2t[0:w, m, 512 * g + 128 * k:512 * g + 128 * k + 128],
                                  Dg[0:w, m].rearrange("p a b -> p (a b)"), m == 0, m == 2)
                last.then_inc(n["gathered"], 1)
            pe.wait_ge(loaded_sem[0], 16 * (i + 1))
            pe.wait_ge(n["gather_read0"], i + 1)
            for k in range(KD):
                if k == 4:
                    pe.wait_ge(n["gather_read1"], i + 1)
                last = products(pm[2], hg, 0, k, 0, KD)
            last.then_inc(n["gate"], 1)
            pe.wait_ge(n["added"], KD * i + 1)
            for m, (o, w) in enumerate(TILES):
                last = tr(pm[4][0:PAIR, o:o + w], Dc[0:w, m].rearrange("p a b -> p (a b)"), w)
            last.then_inc(n["scatter_matrix"], 1)
            pe.wait_ge(loaded_sem[1], 16 * (i + 1))
            for k in range(KD):
                last = products(pm[3], hg, 1, k, 0, KD)
            last.then_inc(n["up"], 1)
            pe.wait_ge(n["hidden"], i + 1)
            for f in range(4):
                last = tr(pm[5][:, PAIR * f:PAIR * f + PAIR], hid[0:PAIR, 128 * f:128 * f + 128], PAIR)
            last.then_inc(n["turned"], 1)
            pe.wait_ge(loaded_sem[2], 16 * (i + 1))
            pe.wait_ge(n["turned_read"], i + 1)
            for g in range(2):
                for k in range(4):
                    last = products(pm[6 + g], hidT, 2, k, g, 4)
                last.then_inc(n["down"], 1)
            pe.wait_ge(n["down_read0"], i + 1)
            for d in range(KD):
                if d == 3:
                    pe.wait_ge(n["down_read1"], i + 1)
                if d >= 4:
                    pe.wait_ge(n["added"], KD * i + d - 2)
                last = mm(pm[4 + d % 4][:, 0:TOK], yt[0:PAIR, 128 * d:128 * d + 128], DT_[0:PAIR, :])
                last.then_inc(n["scattered"], 1)

        def experts():
            pe.wait_ge(*when("one-hot"))
            b = ring_bank("table")
            q = MORE * NE
            mm(b[:, 0:OVER], const("over_expert")[0:q, :], oneh[0:q, :])
            mm(b[:, 16:16 + OVER], const("over_base")[0:q, :], oneh[0:q, :]) \
                .then_inc(mark("router_products", "table ready"), 1)
            pe.wait_ge(*when("read h2t21"))
            with pe.Fori(0, NE // 2) as i:
                expert_block(i, main_sems, expert_loaded, 1)
            pe.wait_ge(main_sems["added"], KD * (NE // 2) + 1)
            pe.wait_ge(*when("tables"))
            overflow(pe, lambda j: expert_block(j, over_sems, over_loaded, 0))

        def final():
            b = ring_bank("norm3")
            for d in range(KD):
                pe.wait_ge(*when(f"square3 {d}"))
                last = mm(b[:, 0:TOK], ones, hT[:, d, :], d == 0, d == KD - 1)
            last.then_inc(mark("norm_sums", "norm3 ready"), 1)
            for g in range(2):
                for m, (o, n) in enumerate(TILES):
                    for j in range(4):
                        pe.wait_ge(*when(f"yf {4 * g + j}"))
                    b = ring_bank(f"y{g}{m}")
                    for j in range(4):
                        last = tr(b[0:n, 128 * j:128 * j + 128], hT[:, 4 * g + j, o:o + n], 128)
                    last.then_inc(mark("transposed", f"y{g}{m} ready"), 1)

        run(locals())

    @block.vector
    def _(dve):
        def head():
            dve.wait_ge(*when("c exp1"))
            dve.wait_ge(*when("c rows"))
            V.scalar_tensor_tensor(csx[0:NC9, 1, :], crow[0:NC9, :], 0.0, csx[0:NC9, 0, :], ALU.min, ALU.subtract) \
                .then_inc(mark("head_by_vector", "c ls"), 1)
            dve.wait_ge(*when("c sig"))
            V.tensor_tensor(crow[0:NC9, :], crow[0:NC9, :], csx[0:NC9, 1, :], ALU.mult) \
                .then_inc(mark("head_by_vector", "silu(c)"), 1)
            dve.wait_ge(*when("vec ready"))
            V.tensor_copy(vecT[:, 0:NVEC], rb("vec")[:, 0:NVEC])
            V.tensor_copy(convT[:, 0:96], rb("vec")[:, 128:224]).then_inc(mark("head_by_vector", "read vec"), 1)
            for d in range(KD):
                dve.wait_ge(*when(f"x{d} ready"))
                V.tensor_copy(xT[:, d, :], rb(f"x{d}")[:, 0:TOK]) \
                    .then_inc(mark("head_by_vector", f"read x{d}"), 1)
            for g in range(2):
                dve.wait_ge(*when(f"cb{g} ready"))
                V.tensor_copy(cbT[:, 12 * g:12 * g + 12, :],
                                   rb(f"cb{g}")[:, 0:288].rearrange("p (a b) -> p a b", b=24)) \
                    .then_inc(mark("head_by_vector", f"read cb{g}"), 1)
            dve.wait_ge(*when("c ready"))
            V.tensor_copy(csT[:, 0:KD * NC9], rb("c")[:, 0:KD * NC9]) \
                .then_inc(mark("head_by_vector", "read c"), 1)

        def fold(c):
            dve.wait_ge(*when(f"fold{c} ready"))
            dve.wait_ge(*when("read vec"))
            V.tensor_tensor(modT[:, 2 * c:2 * c + 2, :],
                                 pm[6][:, 0:2 * NC9].rearrange("p (a b) -> p a b", b=NC9),
                                 bc(vecT[:, 2 * c:2 * c + 2], NC9), ALU.add) \
                .then_inc(mark("ada_by_vector", f"read fold{c}"), 1)

        def norm_sums(i):
            dve.wait_ge(*when(f"rstd{i}"))
            dve.wait_ge(*when(f"norm{i} ready"))
            for d in range(KD):
                V.tensor_tensor(hT[:, d, :], xT[:, d, :], rsB, ALU.mult) \
                    .then_inc(mark("norm_by_vector", f"n{i} {d}"), 1)

        def norm(i):
            base = 24 * (i - 1)
            dve.wait_ge(*when(f"read fold{(base + 15) // 2}"))
            AA = A1 if i == 1 else A2
            o, _ = VEC[f"norm{i}"]
            V.scalar_tensor_tensor(AA, modT[:, base + 8:base + 16, :], 1.0, bc(vecT[:, o:o + 8], NC9),
                                        ALU.add, ALU.mult) \
                .then_inc(mark("norm_by_vector", f"A{i}"), 1)
            dve.wait_ge(*when(f"A{i}"))
            for d in range(KD):
                hs = hT[:, d, SEQ:TOK].rearrange("p (s t) -> p s t", t=DT)
                V.tensor_tensor(hs, hs, bc(AA[:, d, 1:NC9], DT), ALU.mult) \
                    .then_inc(mark("norm_by_vector", f"m{i} {d}"), 1)
            for d in range(KD):
                dve.wait_ge(*when(f"m{i} {d}"))
                hs = hT[:, d, SEQ:TOK].rearrange("p (s t) -> p s t", t=DT)
                V.tensor_tensor(hs, hs, bc(modT[:, base + d, 1:NC9], DT), ALU.add) \
                    .then_inc(mark("norm_by_vector", f"h{i} {d}"), 1)

        def small():
            dve.wait_ge(*when("ra ready"))
            dve.wait_ge(*when("raT ones"))
            V.tensor_copy(raT[0:RANK, :], rb("ra")[0:RANK, 0:TOK]) \
                .then_inc(mark("small_by_vector", "read ra", "raT"), 1)
            dve.wait_ge(*when("ba ready"))
            dve.wait_ge(*when("adt"))
            V.tensor_copy(ba[:, 0:2, :], rb("ba")[:, 0:32].rearrange("p (a b) -> p a b", b=16))
            V.tensor_copy(ba[0:32, 2, :], rb("ba")[0:32, 32:48]).then_inc(mark("small_by_vector", "read ba"), 1)
            dve.wait_ge(*when("read ba"))
            V.tensor_tensor(ba[:, :, 8:16], ba[:, :, 8:16], mid(adt[:, 1, :], 3), ALU.add) \
                .then_inc(mark("small_by_vector", "a + dt"), 1)
            dve.wait_ge(*when("small ln"))
            V.scalar_tensor_tensor(beta, ba[:, :, 0:8], 0.0, bcum_tmp(0), ALU.min, ALU.subtract)
            V.scalar_tensor_tensor(gt, ba[:, :, 8:16], 0.0, bcum_tmp(1), ALU.max, ALU.add) \
                .then_inc(mark("small_by_vector", "softplus"), 1)
            dve.wait_ge(*when("softplus"))
            dve.wait_ge(*when("exp A"))
            V.scalar_tensor_tensor(gB, gt, -1.0, mid(adt[:, 0, :], 3), ALU.mult, ALU.mult) \
                .then_inc(mark("small_by_vector", "g main"), 1)
            dve.wait_ge(*when("g main"))
            V.tensor_tensor(gseq[0:32], mid(gB[0:32, 2, :], NSEQ), bc(const("seq")[0:32, :], HB), ALU.mult) \
                .then_inc(mark("small_by_vector", "g"), 1)

        def sums():
            dve.wait_ge(*when("bcum ready"))
            for m, (o, n) in enumerate(TILES):
                V.tensor_copy(bcum[0:n, m, :], rb("bcum")[0:n, 8 * m:8 * m + 8])
                V.tensor_copy(blast[0:n, m, :], rb("bcum")[0:n, 32 + 8 * m:40 + 8 * m]) \
                    .then_inc(mark("small_by_vector", f"b{m}"), 1)
            dve.wait_ge(*when("b2"))
            V.tensor_tensor(gt, blast, bcum, ALU.subtract).then_inc(mark("small_by_vector", "b rest"), 1)

        def bcum_tmp(i):
            return sgm[:, 0, 24 * i:24 * i + 24].rearrange("p (a b) -> p a b", b=8)

        def step(s):
            s6, s4, s3, s1 = s - 6, s - 4, s - 3, s - 1
            if 0 <= s6 < NPROJ:
                kind, i, _ = PROJ[s6]
                if kind == "cv" and i < 16:
                    q = (qB if i < 8 else kB)[:, i % 8, :]
                    dve.wait_ge(*when(f"rs{s6}"))
                    V.tensor_tensor(q, q, rsb[:, s6 % 2, :], ALU.mult) \
                        .then_inc(mark("proj_by_vector", f"qkn{s6}"), 1)
                if kind == "va" or (kind == "cv" and i >= 16):
                    dve.wait_ge(*when(f"tr{s6} ready"))
                    dst = vA if kind == "va" else vB
                    c = i if kind == "va" else i - 16
                    b = rb(f"tr{s6}")
                    V.tensor_copy(dst[:, 0:2, 128 * c:128 * c + 128], b[:, 0:256].rearrange("p (a b) -> p a b", b=128))
                    V.tensor_copy(dst[0:32, 2, 128 * c:128 * c + 128], b[0:32, 256:384]) \
                        .then_inc(mark("proj_by_vector", f"read tr{s6}", f"vtok{i}" if kind == "va" else f"vbtok{c}"), 1)
            if 0 <= s4 < NPROJ:
                kind, i, _ = PROJ[s4]
                sg, y = sgm[:, s4 % 4], yb[:, s4 % 4]
                if kind in ("cv", "ga", "zb", "gsa", "gsb"):
                    dve.wait_ge(*when(f"sig{s4}"))
                if kind == "cv":
                    if i < 16:
                        out = (qB if i < 8 else kB)[:, i % 8, :]
                        V.tensor_tensor(out[:, 0:SEQ], y[:, 0:SEQ], sg[:, 0:SEQ], ALU.mult)
                        V.tensor_tensor(out[:, SEQ:TOK].rearrange("p (s t) -> p s t", t=DT), sampled(y),
                                             sampled(sg), ALU.mult) \
                            .then_inc(mark("proj_by_vector", f"act{s4}"), 1)
                    else:
                        V.tensor_tensor(sg[:, 0:SEQ], y[:, 0:SEQ], sg[:, 0:SEQ], ALU.mult) \
                            .then_inc(mark("proj_by_vector", f"actp{s4}"), 1)
                        dve.wait_ge(*when(f"actp{s4}"))
                        V.tensor_tensor(y[:, 0:32].rearrange("p (s t) -> p s t", t=DT), sampled(y), sampled(sg),
                                             ALU.mult) \
                            .then_inc(mark("proj_by_vector", f"acty{s4}"), 1)
                        dve.wait_ge(*when(f"acty{s4}"))
                        V.tensor_copy(sg[:, SEQ:TOK], y[:, 0:32]) \
                            .then_inc(mark("proj_by_vector", f"act{s4}"), 1)
                if kind == "ga":
                    V.tensor_tensor(GA[:, i, :], y[:, 0:TOK], sg[:, 0:TOK], ALU.mult) \
                        .then_inc(mark("proj_by_vector", f"act{s4}"), 1)
                if kind == "zb":
                    V.tensor_tensor(GB[:, i, :], y[:, 0:TOK], sg[:, 0:TOK], ALU.mult) \
                        .then_inc(mark("proj_by_vector", f"act{s4}"), 1)
                if kind in ("gsa", "gsb"):
                    GG = GA if kind == "gsa" else GB
                    dve.wait_ge(*when(f"act{s4 - 8}"))
                    V.tensor_tensor(GG[:, i, :], GG[:, i, :], sg[:, 0:TOK], ALU.mult) \
                        .then_inc(mark("proj_by_vector", f"act{s4}"), 1)
            if 0 <= s3 < NPROJ:
                kind, i, _ = PROJ[s3]
                if kind in ("cv", "ga", "zb", "gsa", "gsb"):
                    n = YW if kind == "cv" else TOK
                    dve.wait_ge(*when(f"ln{s3}"))
                    sg, y = sgm[:, s3 % 4, 0:n], yb[:, s3 % 4, 0:n]
                    V.scalar_tensor_tensor(sg, y, 0.0, sg, ALU.min, ALU.subtract) \
                        .then_inc(mark("proj_by_vector", f"ls{s3}"), 1)
            if 0 <= s1 < NPROJ:
                kind, i, _ = PROJ[s1]
                if kind == "cv":
                    dve.wait_ge(*when(f"xp{s1}"))
                    x, y = xp[:, s1 % 2], yb[:, s1 % 4]
                    dve.wait_ge(*when("read c"))
                    for event in y_free(s1 - 4):
                        dve.wait_ge(*when(event))
                    wv = lambda j: convT[:, 24 * j + i:24 * j + i + 1]
                    V.tensor_scalar(y, x[:, 0:YW], wv(0), None, ALU.mult) \
                        .then_inc(mark("proj_by_vector", f"tap0 {s1}"), 1)
                    for j in range(1, TAPS):
                        dve.wait_ge(*when(f"tap{j - 1} {s1}"))
                        V.scalar_tensor_tensor(y, x[:, j:j + YW], wv(j), y, ALU.mult, ALU.add) \
                            .then_inc(mark("proj_by_vector", f"tap{j} {s1}"), 1)

        def sampled_in(a):
            return a.rearrange("p (s t) -> p s t", t=DT)

        def blocks(a):
            return a.rearrange("p (s t) -> p s t", t=BLK)[:, :, 0:DT]

        def sampled(a):
            return a[:, SEQ:SEQ + 7 * NSEQ].rearrange("p (s t) -> p s t", t=7)[:, :, 3:7]

        def gla_decays(m):
            o, n = TILES[m]
            t = f"gla{m} "
            dve.wait_ge(*when(t + "ln"))
            V.scalar_tensor_tensor(gA[0:n].rearrange("p a b -> p (a b)"), pm[4][0:n, :], 0.0,
                                        gA[0:n].rearrange("p a b -> p (a b)"), ALU.min, ALU.subtract) \
                .then_inc(mark("gla_by_vector", t + "logits read", t + "log decay"), 1)

        def gla_sums(m):
            o, n = TILES[m]
            t = f"gla{m} "
            dve.wait_ge(*when(t + "cum"))
            dve.wait_ge(*when(t + "eb"))
            cum = pm[5][:, 0:HA * n].rearrange("p (h t) -> p h t", t=n)
            if m < 2:
                V.tensor_copy(ebl[:, :, 0:1], Eb[:, :, n - 1:n])
                V.tensor_copy(ebl[:, :, 1:2], cum[:, :, n // 2 - 1:n // 2]) \
                    .then_inc(mark("gla_by_vector", t + "ref"), 1)
                V.tensor_copy(ebl[:, :, 2:3], cum[:, :, n - 1:n]).then_inc(mark("gla_by_vector", t + "ref2"), 1)
                dve.wait_ge(*when(t + "ref2"))
                V.tensor_tensor(Ep, cum, ebl[:, :, 1:2].to_broadcast([P, HA, n]), ALU.subtract)
                V.tensor_tensor(El, ebl[:, :, 2:3].to_broadcast([P, HA, n]), cum, ALU.subtract) \
                    .then_inc(mark("gla_by_vector", t + "cum read", t + "D"), 1)
            else:
                V.tensor_copy(Em[:, :, 0:n], cum).then_inc(mark("gla_by_vector", t + "cumc"), 1)
                dve.wait_ge(*when(t + "cumc"))
                V.tensor_copy(Ep[:, :, 0:n], Em[:, :, 0:n])
                for h in range(HA):
                    c4 = Em[:, h, 0:n].rearrange("p (s t) -> p s t", t=DT)
                    e4 = Eb[:, h, 0:n].rearrange("p (s t) -> p s t", t=DT)
                    V.tensor_copy(ebl[:, h, :].unsqueeze(2), e4[:, :, DT - 1:DT])
                    last = V.tensor_tensor(El[:, h, 0:n].rearrange("p (s t) -> p s t", t=DT),
                                           c4[:, :, DT - 1:DT].to_broadcast([P, NSEQ, DT]), c4, ALU.subtract)
                last.then_inc(mark("gla_by_vector", t + "cum read", t + "D"), 1)
            q, k = QKA[:, 0:HA, o:o + n], QKA[:, HA:2 * HA, o:o + n]
            dve.wait_ge(*when(t + "exps"))
            V.tensor_tensor(Ep[:, :, 0:n], q, Ep[:, :, 0:n], ALU.mult) \
                .then_inc(mark("gla_by_vector", t + "qq"), 1)
            V.tensor_tensor(Em[:, :, 0:n], k, Em[:, :, 0:n], ALU.mult) \
                .then_inc(mark("gla_by_vector", t + "kk"), 1)
            V.tensor_tensor(El[:, :, 0:n], k, El[:, :, 0:n], ALU.mult) \
                .then_inc(mark("gla_by_vector", t + "ke"), 1)
            if m < 2:
                V.tensor_tensor(Eb[:, :, 0:n], q, Eb[:, :, 0:n], ALU.mult) \
                    .then_inc(mark("gla_by_vector", t + "qb"), 1)
            else:
                for h in range(HA):
                    last = V.tensor_tensor(blocks(qbM[:, h]), sampled_in(q[:, h]), sampled_in(Eb[:, h, 0:n]), ALU.mult)
                last.then_inc(mark("gla_by_vector", t + "qb"), 1)

        def gla_scores(m):
            o, n = TILES[m]
            t = f"gla{m} "
            dve.wait_ge(*when(t + "A"))
            V.tensor_tensor(ATa[0:n, :, 0:n], pm[6][0:n, 0:HA * n].rearrange("p (h t) -> p h t", t=n),
                                 mid(TRI[m][0:n, 0:n], HA), ALU.mult) \
                .then_inc(mark("gla_by_vector", t + "A read", t + "AT"), 1)

        def gla_states_read(m):
            o, n = TILES[m]
            t = f"gla{m} "
            if m == 2:
                dve.wait_ge(*when(t + "oS ready"))
                V.tensor_copy(oSt, pm[6][:, 0:256]).then_inc(mark("gla_by_vector", t + "oS"), 1)

        def gla_out(m):
            o, n = TILES[m]
            t = f"gla{m} "
            if m == 1:
                for g in range(2):
                    dve.wait_ge(*when(t + f"S{g} ready"))
                    dve.wait_ge(*when(t + f"o{g} ready"))
                    for hh in range(2):
                        h = 2 * g + hh
                        last = V.scalar_tensor_tensor(SA[:, h, :], SA[:, h, :], ebl[:, h, 0:1],
                                                      pm[6 + g][:, 256 * hh:256 * hh + 256], ALU.mult, ALU.add)
                    last.then_inc(mark("gla_by_vector", t + f"S{g} read", f"gla state prompt {g}"), 1)
            dve.wait_ge(*when(t + "rstd"))
            dve.wait_ge(*when(t + "o1 ready"))
            for g in range(2):
                last = V.tensor_tensor(oNa[0:n, 512 * g:512 * g + 512].rearrange("p (a b) -> p a b", b=256),
                                       pm[4 + g][0:n, :].rearrange("p (a b) -> p a b", b=256),
                                       bc(srs[0:n, 2 * g:2 * g + 2], 256), ALU.mult)
                last.then_inc(mark("gla_by_vector", t + f"o{g} read", *([t + "oN"] if g else [])), 1)

        def gla_turn(m):
            o, n = TILES[m]
            t = f"gla{m} "
            if m == 2:
                for s in range(NSEQ):
                    w = slot(("sgla", s // 2)).rearrange("p (s h) v -> p s h v", h=HA)
                    for g in range(2):
                        dve.wait_ge(*when(f"gla state product {s} {g}"))
                        for hh in range(2):
                            h = 2 * g + hh
                            st = w[:, s % 2, h, :]
                            last = V.scalar_tensor_tensor(st, st, ebl[:, h, s:s + 1],
                                                          pm[6 + g][:, 256 * hh:256 * hh + 256], ALU.mult, ALU.add)
                        last.then_inc(mark("gla_by_vector", f"gla state {s} {g}"), 1)
            for g in range(2):
                dve.wait_ge(*when(t + f"oT{g} ready"))
                V.tensor_copy(QKA[:, 4 * g:4 * g + 4, o:o + n],
                                   pm[4 + g][:, 0:512].rearrange("p (a b) -> p a b", b=128)[:, :, 0:n]) \
                    .then_inc(mark("gla_by_vector", t + f"oT{g}"), 1)

        def conv_out():
            for g in range(6):
                dve.wait_ge(*when(f"cvo{g} ready"))
                V.tensor_copy(newconv[0:27, 512 * g:512 * g + 512], rb(f"cvo{g}")[0:27, :]) \
                    .then_inc(mark("proj_by_vector", f"read cvo{g}"), 1)

        def block_matrix(m, lv):
            n, t, HG = TILES[m][1], f"gdn{m} ", 4
            for g in range(2):
                hs = slice(HG * g, HG * g + HG)
                dve.wait_ge(*when(t + f"KK{g} read"))
                if lv:
                    dve.wait_ge(*when(t + f"Y{lv - 1} {g} ready"))
                if lv == 1:
                    dve.wait_ge(*when(t + f"XT0 {g}"))
                V.tensor_tensor(Lm[0:n, hs, 0:n], LT[0:n, hs, 0:n],
                                     mid(const(f"level{lv}")[0:n, 0:n], HG), ALU.mult) \
                    .then_inc(mark("gdn_by_vector", t + f"Lm{lv} {g}"), 1)

        def gdn_scores(m):
            o, n = TILES[m]
            t = f"gdn{m} "
            HG = 4
            if m == 0:
                dve.wait_ge(*when("gla2 oT1"))
            else:
                pass
            V.tensor_tensor(tg[0:n, :, 0:n], mid(TRI[m][0:n, 0:n], HB), bc(gB[0:n, m, :], n), ALU.mult) \
                .then_inc(mark("gdn_by_vector", t + "tg"), 1)
            for g in range(2):
                dve.wait_ge(*when(t + f"bc{g}"))
                for j in range(HG):
                    h = HG * g + j
                    last = V.tensor_scalar(E[0:n, h, 0:n], pm[4 + g][0:n, n * j:n * j + n], bcum[0:n, m, h:h + 1],
                                           0.0, ALU.subtract, ALU.min)
                last.then_inc(mark("gdn_by_vector", t + f"D{g}"), 1)
            for g in range(2):
                dve.wait_ge(*when(t + f"E{g}"))
                ee = E[0:n, HG * g:HG * g + HG, 0:n]
                V.tensor_tensor(ee, ee, mid(TRI[m][0:n, 0:n], HG), ALU.mult) \
                    .then_inc(mark("gdn_by_vector", t + f"Em{g}"), 1)
            for g in range(2):
                dve.wait_ge(*when(t + f"KK{g}"))
                dve.wait_ge(*when(t + f"Em{g}"))
                dve.wait_ge(*when("beta"))
                for j in range(HG):
                    h = HG * g + j
                    last = V.scalar_tensor_tensor(LT[0:n, h, 0:n], pm[6 + g][0:n, n * j:n * j + n],
                                                  beta[0:n, m, h:h + 1], E[0:n, h, 0:n], ALU.mult, ALU.mult)
                last.then_inc(mark("gdn_by_vector", t + f"KK{g} read"), 1)
            for g in range(2):
                dve.wait_ge(*when(t + f"QK{g}"))
                V.tensor_tensor(AT[0:n, HG * g:HG * g + HG, 0:n],
                                     pm[4 + g][0:n, 0:HG * n].rearrange("p (h t) -> p h t", t=n),
                                     E[0:n, HG * g:HG * g + HG, 0:n], ALU.mult) \
                    .then_inc(mark("gdn_by_vector", t + f"AT{g}"), 1)

        def gdn_level(m, lv):
            o, n = TILES[m]
            t = f"gdn{m} "
            HG = 4
            levels = LEVELS if m < 2 else 2
            idm = mid(ident[0:n, 0:n], HG)
            if lv:
                if lv + 1 < levels:
                    block_matrix(m, lv + 1)
            for g in range(2):
                hs = slice(HG * g, HG * g + HG)
                view = lambda b: pm[b][0:n, 0:HG * n].rearrange("p (h t) -> p h t", t=n)
                if lv == 0:
                    if g == 0:
                        block_matrix(m, 0)
                    dve.wait_ge(*when(t + f"Lm0 {g}"))
                    V.tensor_tensor(X[0:n, hs, 0, 0:n], idm, Lm[0:n, hs, 0:n], ALU.subtract) \
                        .then_inc(mark("gdn_by_vector", t + f"XT0 {g}"), 1)
                    dve.wait_ge(*when(t + f"Y0 {g} ready"))
                    V.tensor_tensor(X[0:n, hs, 1, 0:n], idm, view(4 + g), ALU.subtract) \
                        .then_inc(mark("gdn_by_vector", t + f"Y0 {g}", t + f"X0 {g}"), 1)
                    if g:
                        block_matrix(m, 1)
                else:
                    dve.wait_ge(*when(t + f"ZT{lv} {g}"))
                    if lv < levels - 1:
                        dve.wait_ge(*when(t + f"Z{lv} {g}"))
                    V.tensor_tensor(X[0:n, hs, 0, 0:n], X[0:n, hs, 0, 0:n], view(6 + g), ALU.subtract) \
                        .then_inc(mark("gdn_by_vector", t + f"XT{lv} {g}"), 1)
                    if lv < levels - 1:
                        V.tensor_tensor(X[0:n, hs, 1, 0:n], X[0:n, hs, 1, 0:n], view(4 + g), ALU.subtract) \
                            .then_inc(mark("gdn_by_vector", t + f"X{lv} {g}"), 1)

        def gdn_values(m):
            o, n = TILES[m]
            t = f"gdn{m} "
            HG = 4
            levels = LEVELS if m < 2 else 2
            if m == 2:
                dve.wait_ge(*when("kM zero"))
                for h in range(HB):
                    last = V.tensor_copy(blocks(kM[:, h]), sampled_in(kB[:, h, o:o + n]))
                last.then_inc(mark("gdn_by_vector", t + "kM"), 1)
                dve.wait_ge(*when("qM zero"))
                for h in range(HB):
                    last = V.tensor_copy(blocks(qM[h // HG][:, h % HG]), sampled_in(qB[:, h, o:o + n]))
                last.then_inc(mark("gdn_by_vector", t + "qM"), 1)
            full = lambda b: pm[b][0:n, :].rearrange("p (h t) -> p h t", t=128)
            for g in range(2):
                hs = slice(HG * g, HG * g + HG)
                dve.wait_ge(*when(t + f"kT{g}"))
                dve.wait_ge(*when("exp b"))
                for x in range(2):
                    dve.wait_ge(*when(t + f"Lm{levels - 1} {x}"))
                V.tensor_tensor(ke[0:n, hs, :], full(4 + g), bc(elB[0:n, m, hs], 128), ALU.mult) \
                    .then_inc(mark("gdn_by_vector", t + f"ke{g}"), 1)
            if m == 2:
                dve.wait_ge(*when(t + "Ss"))
                V.tensor_copy(oSt, pm[6][:, 0:256]).then_inc(mark("gdn_by_vector", t + "kSs"), 1)
                V.tensor_copy(oSt2, pm[7][:, 0:256]).then_inc(mark("gdn_by_vector", t + "qSs"), 1)
            for g in range(2):
                hs = slice(HG * g, HG * g + HG)
                vtok = vB[0:n, m, 512 * g:512 * g + 512].rearrange("p (h v) -> p h v", v=128)
                if m == 0:
                    continue
                dve.wait_ge(*when(t + f"kS{g}"))
                V.tensor_tensor(R[0:n, hs, :], full(6 + g), bc(ebB[0:n, m, hs], 128), ALU.mult) \
                    .then_inc(mark("gdn_by_vector", t + f"ekS{g}"), 1)
                dve.wait_ge(*when(t + f"ekS{g}"))
                V.tensor_tensor(R[0:n, hs, :], vtok, R[0:n, hs, :], ALU.subtract) \
                    .then_inc(mark("gdn_by_vector", t + f"R{g}"), 1)
            for g in range(2):
                hs = slice(HG * g, HG * g + HG)
                dve.wait_ge(*when(t + f"y{g}"))
                V.tensor_tensor(R[0:n, hs, :], full(4 + g), bc(beta[0:n, m, hs], 128), ALU.mult) \
                    .then_inc(mark("gdn_by_vector", t + f"vn{g}"), 1)

        def gdn_out(m):
            o, n = TILES[m]
            t = f"gdn{m} "
            HG = 4
            full = lambda b: pm[b][0:n, :].rearrange("p (h t) -> p h t", t=128)
            for g in range(2):
                hs = slice(HG * g, HG * g + HG)
                if m:
                    dve.wait_ge(*when(t + f"qS{g}"))
                    V.tensor_tensor(E[0:n, hs, :], full(6 + g), bc(ebB[0:n, m, hs], 128), ALU.mult) \
                        .then_inc(mark("gdn_by_vector", t + f"qS{g} read"), 1)
            for g in range(2):
                hs = slice(HG * g, HG * g + HG)
                dve.wait_ge(*when(t + f"o{g} ready"))
                if m:
                    dve.wait_ge(*when(t + f"qS{g} read"))
                    V.tensor_tensor(E[0:n, hs, :], E[0:n, hs, :], full(4 + g), ALU.add) \
                        .then_inc(mark("gdn_by_vector", t + f"o{g}"), 1)
                else:
                    V.tensor_copy(E[0:n, hs, :], full(4 + g)).then_inc(mark("gdn_by_vector", t + f"o{g}"), 1)
            if m < 2:
                for g in range(2):
                    hs = slice(HG * g, HG * g + HG)
                    dve.wait_ge(*when(t + f"S{g} ready"))
                    if m == 0:
                        last = V.tensor_copy(SB[:, hs, :], full(6 + g))
                    else:
                        for j in range(HG):
                            h = HG * g + j
                            last = V.scalar_tensor_tensor(SB[:, h, :], SB[:, h, :], eSd[:, m, h:h + 1],
                                                          pm[6 + g][:, 128 * j:128 * j + 128], ALU.mult, ALU.add)
                    last.then_inc(mark("gdn_by_vector", t + f"state{g}"), 1)
            dve.wait_ge(*when(t + "squares"))
            V.tensor_reduce(ssum[0:n, :], sqo[0:n], AX, ALU.add).then_inc(mark("gdn_by_vector", t + "ssum"), 1)
            dve.wait_ge(*when(t + "rstd"))
            V.tensor_tensor(Y[0:n], E[0:n], bc(srs[0:n, :], 128), ALU.mult) \
                .then_inc(mark("gdn_by_vector", t + "oN"), 1)

        def gdn_turn(m):
            o, n = TILES[m]
            t = f"gdn{m} "
            HG = 4
            if m == 2:
                for s in range(NSEQ):
                    w = slot(("sgdn", s // 2)).rearrange("p k n -> p (k n)").rearrange("p (s h v) -> p s h v", h=HB, v=DVB)
                    for g in range(2):
                        dve.wait_ge(*when(f"gdn state product {s} {g}"))
                        for j in range(HG):
                            h = HG * g + j
                            st = w[:, s % 2, h, :]
                            last = V.scalar_tensor_tensor(st, st, eSs[:, s, h:h + 1],
                                                          pm[6 + g][:, 128 * j:128 * j + 128], ALU.mult, ALU.add)
                        last.then_inc(mark("gdn_by_vector", f"gdn state {s} {g}"), 1)
            for g in range(2):
                dve.wait_ge(*when(t + f"oT{g} ready"))
                V.tensor_copy(qB[:, 4 * g:4 * g + 4, o:o + n],
                                   pm[4 + g][:, 0:512].rearrange("p (a b) -> p a b", b=128)[:, :, 0:n]) \
                    .then_inc(mark("gdn_by_vector", t + f"oT{g}"), 1)

        def merge_gla():
            an = VEC["gla_norm"][0]
            for d in range(KD):
                dve.wait_ge(*when(f"act{GSA0 + d}"))
                V.scalar_tensor_tensor(GA[:, d, :], QKA[:, d, :], vecT[:, an + d % 2:an + d % 2 + 1], GA[:, d, :],
                                            ALU.mult, ALU.mult) \
                    .then_inc(mark("merge_by_vector", f"ma {d}"), 1)

        def merge():
            bn = VEC["gdn_norm"][0]
            dve.wait_ge(*when("gdn2 oT1"))
            dve.wait_ge(*when(f"act{NPROJ - 1}"))
            for d in range(KD):
                V.scalar_tensor_tensor(GB[:, d, :], qB[:, d, :], vecT[:, bn:bn + 1], GB[:, d, :],
                                            ALU.mult, ALU.mult) \
                    .then_inc(mark("merge_by_vector", f"mb {d}"), 1)

        def wout():
            dve.wait_ge(*when("read fold11"))
            for d in range(KD):
                dve.wait_ge(*when(f"wout{d} ready"))
                residual(d, rb(f"wout{d}")[:, 0:TOK], 16, f"read wout{d}", f"x2 {d}", "merge_by_vector")

        def residual(d, src, gate, read, new, kind):
            V.scalar_tensor_tensor(xT[:, d, 0:SEQ], src[:, 0:SEQ], modT[:, gate + d, 0:1], xT[:, d, 0:SEQ],
                                   ALU.mult, ALU.add)
            V.tensor_tensor(gs[:, d % 2, :].rearrange("p (s t) -> p s t", t=DT),
                                 src[:, SEQ:TOK].rearrange("p (s t) -> p s t", t=DT),
                                 bc(modT[:, gate + d, 1:NC9], DT), ALU.mult) \
                .then_inc(mark(kind, read), 1)
            dve.wait_ge(*when(read))
            V.tensor_tensor(xT[:, d, SEQ:TOK], xT[:, d, SEQ:TOK], gs[:, d % 2, :], ALU.add) \
                .then_inc(mark(kind, new), 1)

        def router():
            dve.wait_ge(*when("router ready"))
            dve.wait_ge(*when("router bias"))
            dve.wait_ge(*when("rt zero"))
            for i in range(4):
                dve.wait_ge(*when(f"stored {chunk_of[('sgdn', i)]}"))
            V.tensor_copy(rt[:, 0:2, :], rb("router")[:, 0:40].rearrange("p (a b) -> p a b", b=20))
            V.tensor_copy(rt[0:32, 2, :], rb("router")[0:32, 40:60]) \
                .then_inc(mark("router_by_vector", "read router"), 1)
            k = [0]

            def st(ins, *ev):
                k[0] += 1
                ins.then_inc(mark("router_by_vector", f"rstep{k[0]}", *ev), 1)
                dve.wait_ge(*when(f"rstep{k[0]}"))
            dve.wait_ge(*when("read router"))
            st(V.tensor_tensor(rt, rt, mid(rtb, 3), ALU.add))
            r = rs_
            iota = mid(const("iota")[:, 0:4], 3)
            one = lambda n: r[n][:, :, 0:1]
            spread = lambda n: r[n][:, :, 0:1].to_broadcast([P, 3, 4])

            def first_max(vals, mx, sel, i):
                st(V.tensor_reduce(one(mx), vals, AX, ALU.max))
                st(V.tensor_tensor(r["hit"], vals, spread(mx), ALU.is_equal))
                st(V.scalar_tensor_tensor(r["idx"], iota, -4.0, r["hit"], ALU.add, ALU.mult))
                st(V.tensor_reduce(one("i1"), r["idx"], AX, ALU.min))
                st(V.tensor_scalar(one("tmp"), one("i1"), 4.0, None, ALU.add))
                st(V.tensor_tensor(r[sel], iota, spread("tmp"), ALU.is_equal))

            first_max(rt[:, :, 0:4], "gmax", "gsel", 0)
            st(V.tensor_tensor(r["dd"], rt[:, :, 0:4], spread("gmax"), ALU.subtract), "gd")
            dve.wait_ge(*when("gexp"))
            st(V.tensor_reduce(one("gden"), r["dd"], AX, ALU.add))
            st(V.reciprocal(one("gw"), one("gden")))
            e4 = el16.rearrange("p m (g e) -> p m g e", e=4)
            l4 = rt[:, :, 4:20].rearrange("p m (g e) -> p m g e", e=4)
            for m in range(3):
                st(V.tensor_tensor(e4[:, m], l4[:, m], bc(r["gsel"][:, m, :], 4), ALU.mult))
                st(V.tensor_reduce(r["el"][:, m, :], e4[:, m].rearrange("p g e -> p e g"), AX, ALU.add))
            first_max(r["el"], "emax", "h1", 1)
            st(V.tensor_tensor(r["p1"], r["el"], spread("emax"), ALU.subtract), "ed")
            dve.wait_ge(*when("eexp"))
            st(V.scalar_tensor_tensor(r["p2"], r["h1"], -4.0, r["p1"], ALU.mult, ALU.add))
            first_max(r["p2"], "w2", "hh", 2)
            st(V.tensor_scalar(one("w1"), one("w2"), 1.0, None, ALU.add))
            st(V.reciprocal(one("w1"), one("w1")))
            st(V.tensor_tensor(r["within"], r["hh"], spread("w2"), ALU.mult))
            st(V.tensor_tensor(r["within"], r["within"], r["h1"], ALU.add))
            st(V.tensor_tensor(one("w1"), one("w1"), one("gw"), ALU.mult))
            st(V.tensor_tensor(r["within"], r["within"], spread("w1"), ALU.mult))
            c4 = comb[:, :, 0:NE].rearrange("p m (g e) -> p m g e", e=4)
            for m in range(3):
                st(V.tensor_tensor(c4[:, m], bc(r["gsel"][:, m, :], 4), mid(r["within"][:, m, :], 4), ALU.mult),
                   *(["comb"] if m == 2 else []))
            for m in range(3):
                st(V.tensor_tensor(r["tmp"][:, m, :], r["hh"][:, m, :], r["h1"][:, m, :], ALU.add))
                st(V.tensor_tensor(sel.rearrange("p m (g e) -> p m g e", e=4)[:, m], bc(r["gsel"][:, m, :], 4),
                                   mid(r["tmp"][:, m, :], 4), ALU.mult))
            st(V.tensor_copy(sel4.rearrange("p m (r e) -> p m r e", e=NE),
                             sel.unsqueeze(2).to_broadcast([P, 3, MORE, NE])), "sel4")
            q = MORE * NE
            dve.wait_ge(*when("rank ready"))
            b = rb("rank")
            for m, (o, n) in enumerate(TILES):
                st(V.tensor_tensor(rank[0:n, m, 0:NE], b[0:n, NE * m:NE * m + NE], sel[0:n, m, :], ALU.mult))
                st(V.tensor_scalar(rank[0:n, m, 0:NE], rank[0:n, m, 0:NE], -1.0, None, ALU.add))
            st(V.tensor_tensor(over[0:q, 0:1], b[0:q, 64:65], const("over_at")[0:q, :], ALU.is_gt), "read rank",
               "over flags")

        def dispatch(places, n):
            for s0, ns, iota, rank_of, comb_of in places:
                for m, (o, w) in enumerate(TILES):
                    dg, dc = [t[0:w, m].rearrange("p a b -> p (a b)")[:, s0:s0 + ns] for t in (Dg, Dc)]
                    V.tensor_scalar(dg, iota[0:w], rank_of(m, w), None, ALU.is_equal)
                    last = V.tensor_scalar(dc, iota[0:w], rank_of(m, w), comb_of(m, w), ALU.is_equal, ALU.mult)
            last.then_inc(n["dispatch"], 1)

        def dispatch_pair(first):
            def place(x):
                def column(table):
                    return lambda m, w: table[0:w, m, bass.ds(first + x, 1)]
                return SLOTS * x, SLOTS, const("iota")[:, 0:SLOTS], column(rank), column(comb)
            dispatch([place(0), place(1)], main_sems)

        def expert_block(i, n, next_dispatch):
            dve.wait_ge(n["gathered"], 2 * i + 1)
            V.tensor_copy(hg[:, 0:4, :], pm[0][:, 0:4 * PAIR].rearrange("p (k s) -> p k s", s=PAIR)) \
                .then_inc(n["gather_read0"], 1)
            s = sg2[0:PAIR]
            dve.wait_ge(n["softplus"], i + 1)
            V.scalar_tensor_tensor(s, pm[2][0:PAIR, :], 0.0, s, ALU.min, ALU.subtract).then_inc(n["log_sigmoid"], 1)
            dve.wait_ge(n["scatter_matrix"], i + 1)
            V.tensor_copy(DT_[0:PAIR, :], pm[4][0:PAIR, 0:TOK]).then_inc(n["scatter_matrix_read"], 1)
            dve.wait_ge(n["sigmoid"], i + 1)
            V.tensor_tensor(s, pm[2][0:PAIR, :], s, ALU.mult).then_inc(n["silu"], 1)
            next_dispatch()
            dve.wait_ge(n["silu"], i + 1)
            dve.wait_ge(n["up"], i + 1)
            V.tensor_tensor(hid[0:PAIR], pm[3][0:PAIR, :], s, ALU.mult).then_inc(n["hidden"], 1)
            dve.wait_ge(n["turned"], i + 1)
            V.tensor_copy(hidT, pm[5][:, 0:4 * PAIR].rearrange("p (k s) -> p k s", s=PAIR)) \
                .then_inc(n["turned_read"], 1)
            dve.wait_ge(n["down"], 2 * i + 1)
            V.tensor_copy(yt[0:PAIR, 0:512], pm[6][0:PAIR, :]).then_inc(n["down_read0"], 1)
            dve.wait_ge(n["added"], KD * i + 1)
            for d in range(KD):
                dve.wait_ge(n["scattered"], KD * i + d + 1)
                V.tensor_tensor(acc[:, d, :], acc[:, d, :], pm[4 + d % 4][:, 0:TOK], ALU.add).then_inc(n["added"], 1)

        def experts():
            count = [0]

            def step(ins, *events):
                count[0] += 1
                ins.then_inc(mark("router_by_vector", f"table step {count[0]}", *events), 1)
                dve.wait_ge(*when(f"table step {count[0]}"))

            dispatch_pair(0)
            q = MORE * NE
            dve.wait_ge(*when("over ready"))
            b = rb("over")
            step(V.tensor_scalar(over[0:q, 1:2], b[0:q, 0:1], -1.0, None, ALU.add))
            step(V.tensor_copy(tab[0:1, 0:1], b[0:1, 8:9]), "read over")
            step(V.tensor_scalar(oneh[0:q, :], const("iota")[0:q, 0:OVER], over[0:q, 1:2], over[0:q, 0:1],
                                 ALU.is_equal, ALU.mult), "one-hot")
            dve.wait_ge(*when("table ready"))
            b = rb("table")
            step(V.tensor_copy(tab[0:1, 1:1 + OVER], b[0:1, 0:OVER]))
            step(V.tensor_copy(expB, b[:, 0:OVER]))
            step(V.tensor_copy(rankO, mid(b[:, 16:16 + OVER], 3)), "read table", "tables")
            with dve.Fori(0, NE // 2) as i:
                expert_block(i, main_sems, lambda: dispatch_pair(2 * i + 2))
            dve.wait_ge(main_sems["added"], KD * (NE // 2) + 1)
            dve.wait_ge(main_sems["dispatch"], NE // 2 + 1)

            def one_over(j):
                V.tensor_tensor(hitE, const("iota")[:, 0:NE], expB[:, bass.ds(j, 1)].to_broadcast([P, NE]),
                                ALU.is_equal).then_inc(over_sems["picked"], 1)
                dve.wait_ge(over_sems["picked"], 6 * j + 1)
                V.tensor_tensor(el16, rank[:, :, 0:NE], mid(hitE, 3), ALU.mult).then_inc(over_sems["picked"], 1)
                dve.wait_ge(over_sems["picked"], 6 * j + 2)
                V.tensor_reduce(rankJ, el16, AX, ALU.add).then_inc(over_sems["picked"], 1)
                dve.wait_ge(over_sems["picked"], 6 * j + 3)
                V.tensor_tensor(rankJ, rankJ, rankO[:, :, bass.ds(j, 1)].rearrange("p m a -> p (m a)"),
                                ALU.subtract).then_inc(over_sems["picked"], 1)
                V.tensor_tensor(el16, comb[:, :, 0:NE], mid(hitE, 3), ALU.mult).then_inc(over_sems["picked"], 1)
                dve.wait_ge(over_sems["picked"], 6 * j + 5)
                V.tensor_reduce(combJ, el16, AX, ALU.add).then_inc(over_sems["picked"], 1)
                dve.wait_ge(over_sems["picked"], 6 * j + 6)
                dispatch([(0, PAIR, const("iota")[:, 0:PAIR], lambda m, w: rankJ[0:w, m:m + 1],
                           lambda m, w: combJ[0:w, m:m + 1])], over_sems)
                expert_block(j, over_sems, lambda: None)
                dve.wait_ge(over_sems["added"], KD * (j + 1) + 1)

            dve.wait_ge(over_sems["added"], 1)
            overflow(dve, one_over)

        def final():
            dve.wait_ge(*when("read fold23"))
            for d in range(KD):
                residual(d, acc[:, d, :], 40, f"moe {d}", f"x3 {d}", "final_by_vector")
            fo = VEC["final"][0]
            dve.wait_ge(*when("rstd3"))
            dve.wait_ge(*when("norm3 ready"))
            for d in range(KD):
                V.scalar_tensor_tensor(hT[:, d, :], xT[:, d, :], vecT[:, fo + d:fo + d + 1], rsB, ALU.mult,
                                            ALU.mult) \
                    .then_inc(mark("final_by_vector", f"yf {d}"), 1)
            for g in range(2):
                for m, (o, n) in enumerate(TILES):
                    if m != 1:
                        dve.wait_ge(*when(f"y{g}{m} ready"))
                        V.tensor_copy(yrow[0:n, m, 512 * g:512 * g + 512], rb(f"y{g}{m}")[0:n, :]) \
                            .then_inc(mark("final_by_vector", f"read y{g}{m}"), 1)

        run(locals())

    @block.scalar
    def _(act):
        A.preload_act_table_set("natural_log_exp_and_others")
        one = ones[:, 0:1]

        def lnexp(dst, src, n=P, kind="", event=None):
            A.activation(dst, src, ACT.Abs).then_inc(mark(kind, event + " abs"), 1)
            act.wait_ge(*when(event + " abs"))
            A.activation(dst, dst, ACT.Exp, scale=-1.0).then_inc(mark(kind, event + " exp"), 1)
            act.wait_ge(*when(event + " exp"))
            A.activation(dst, dst, ACT.Ln, bias=one[0:n]).then_inc(mark(kind, event), 1)

        def rstd(dst, src, scale, kind, event, n=P, bias=None, mid_event=None):
            ev = [mid_event] if mid_event else []
            A.activation(dst, src, ACT.Ln, bias=const("eps")[0:n], scale=scale) \
                .then_inc(mark(kind, event + " ln", *ev), 1)
            act.wait_ge(*when(event + " ln"))
            if bias is None:
                ins = A.activation(dst, dst, ACT.Exp, scale=-0.5)
            else:
                ins = A.activation(dst, dst, ACT.Exp, scale=-0.5, bias=bias)
            ins.then_inc(mark(kind, event), 1)

        def head():
            act.wait_ge(*when("consts"))
            act.wait_ge(*when("c rows"))
            lnexp(csx[0:NC9, 0, :], crow[0:NC9, :], NC9, "head_by_scalar", "c exp1")
            act.wait_ge(*when("c ls"))
            A.activation(csx[0:NC9, 1, :], csx[0:NC9, 1, :], ACT.Exp) \
                .then_inc(mark("head_by_scalar", "c sig"), 1)
            for d in range(KD):
                act.wait_ge(*when(f"read x{d}"))
                A.activation(hT[:, d, :], xT[:, d, :], ACT.Square) \
                    .then_inc(mark("head_by_scalar", f"square1 {d}"), 1)

        def ada(c):
            act.wait_ge(*when(f"ada{c} ready"))
            if c:
                act.wait_ge(*when(f"fold{c - 1} ready"))
            A.activation(adaq, pm[7 - 2 * (c % 2)][:, 0:CW], ACT.Copy) \
                .then_inc(mark("ada_by_scalar", f"read ada{c}"), 1)

        def norm_sums(i):
            if i == 2:
                for d in range(KD):
                    act.wait_ge(*when(f"x2 {d}"))
                    A.activation(hT[:, d, :], xT[:, d, :], ACT.Square) \
                        .then_inc(mark("norm_by_scalar", f"square2 {d}"), 1)
            act.wait_ge(*when(f"norm{i} ready"))
            if i == 2:
                act.wait_ge(*when("h1 7"))
            rstd(rsB, rb(f"norm{i}")[:, 0:TOK], 1.0 / D, "norm_by_scalar", f"rstd{i}", mid_event=f"read norm{i}")

        def norm(i):
            AA, base = (A1, A2)[i - 1], 24 * (i - 1)
            act.wait_ge(*when(f"A{i}"))
            for d in range(KD):
                A.activation(hT[:, d, 0:SEQ], hT[:, d, 0:SEQ], ACT.Identity, bias=modT[:, base + d, 0:1],
                                  scale=AA[:, d, 0:1]) \
                    .then_inc(mark("norm_by_scalar", f"hp{i} {d}"), 1)

        def small():
            act.wait_ge(*when("small parts ready"))
            A.activation(yb[:, 0, 0:TOK], rb("small parts")[:, 0:TOK], ACT.Copy) \
                .then_inc(mark("small_by_scalar", "read small parts"), 1)
            act.wait_ge(*when("a + dt"))
            t0 = sgm[:, 0, 0:24].rearrange("p (a b) -> p a b", b=8)
            t1 = sgm[:, 0, 24:48].rearrange("p (a b) -> p a b", b=8)
            A.activation(t0, ba[:, :, 0:8], ACT.Abs)
            A.activation(t1, ba[:, :, 8:16], ACT.Abs).then_inc(mark("small_by_scalar", "small abs"), 1)
            act.wait_ge(*when("small abs"))
            tt = sgm[:, 0, 0:48]
            A.activation(tt, tt, ACT.Exp, scale=-1.0).then_inc(mark("small_by_scalar", "small exp"), 1)
            act.wait_ge(*when("small exp"))
            A.activation(tt, tt, ACT.Ln, bias=one).then_inc(mark("small_by_scalar", "small ln"), 1)
            A.activation(adt[:, 0, :], adt[:, 0, :], ACT.Exp).then_inc(mark("small_by_scalar", "exp A"), 1)
            act.wait_ge(*when("softplus"))
            A.activation(beta, beta, ACT.Exp).then_inc(mark("small_by_scalar", "beta"), 1)

        def sums():
            act.wait_ge(*when("b rest"))
            A.activation(eSs, rb("bcum")[:, 64:128].rearrange("p (s h) -> p s h", h=HB), ACT.Exp) \
                .then_inc(mark("small_by_scalar", "read bcum"), 1)
            A.activation(ebB, bcum, ACT.Exp)
            A.activation(eSd, blast, ACT.Exp)
            A.activation(elB, gt, ACT.Exp).then_inc(mark("small_by_scalar", "exp b"), 1)

        def step(s):
            s5, s4, s3, s2, s0 = s - 5, s - 4, s - 3, s - 2, s
            if 0 <= s5 < NPROJ:
                kind, i, _ = PROJ[s5]
                if kind == "cv" and i < 16:
                    act.wait_ge(*when(f"ssq{s5} ready"))
                    rstd(rsb[:, s5 % 2, :], rb(f"ssq{s5}")[:, 0:TOK], 1.0, "proj_by_scalar", f"rs{s5}",
                         bias=const("lnq") if i < 8 else None, mid_event=f"read ssq{s5}")
            if 0 <= s4 < NPROJ:
                kind, i, _ = PROJ[s4]
                if kind == "cv" and i < 16:
                    act.wait_ge(*when(f"act{s4}"))
                    q = (qB if i < 8 else kB)[:, i % 8, :]
                    A.activation(sqb[:, s4 % 2, :], q, ACT.Square) \
                        .then_inc(mark("proj_by_scalar", f"sq{s4}"), 1)
            if 0 <= s3 < NPROJ:
                kind, i, _ = PROJ[s3]
                if kind in ("cv", "ga", "zb", "gsa", "gsb"):
                    n = YW if kind == "cv" else TOK
                    act.wait_ge(*when(f"ls{s3}"))
                    sg = sgm[:, s3 % 4, 0:n]
                    A.activation(sg, sg, ACT.Exp).then_inc(mark("proj_by_scalar", f"sig{s3}"), 1)
            if 0 <= s2 < NPROJ:
                kind, i, _ = PROJ[s2]
                if kind in ("cv", "ga", "zb", "gsa", "gsb"):
                    n = YW if kind == "cv" else TOK
                    act.wait_ge(*when(f"tap3 {s2}" if kind == "cv" else f"y{s2}"))
                    for event in sg_free(s2 - 4):
                        act.wait_ge(*when(event))
                    lnexp(sgm[:, s2 % 4, 0:n], yb[:, s2 % 4, 0:n], P, "proj_by_scalar", f"ln{s2}")
            if s0 < NPROJ:
                kind, i, _ = PROJ[s0]
                act.wait_ge(*when(f"proj{s0} ready"))
                b = rb(f"proj{s0}")
                if kind == "qa":
                    A.activation(QKA[:, i, :], b[:, 0:TOK], ACT.Copy, scale=DKA ** -0.5) \
                        .then_inc(mark("proj_by_scalar", f"read proj{s0}"), 1)
                elif kind == "ka":
                    A.activation(QKA[:, 4 + i, :], b[:, 0:TOK], ACT.Copy) \
                        .then_inc(mark("proj_by_scalar", f"read proj{s0}"), 1)
                elif kind == "cv":
                    x = xp[:, s0 % 2]
                    act.wait_ge(*when("xp zero"))
                    act.wait_ge(*when("read cb1"))
                    if i >= 2:
                        act.wait_ge(*when(f"cc{i - 2}"))
                    A.activation(x[:, 3:3 + SEQ], b[:, 0:SEQ], ACT.Copy)
                    blk = x[:, SAMP0:XPW].rearrange("p (s t) -> p s t", t=7)
                    A.activation(blk[:, :, 0:3], cbT[:, i, :].rearrange("p (s t) -> p s t", t=3), ACT.Copy)
                    A.activation(blk[:, :, 3:7], b[:, SEQ:TOK].rearrange("p (s t) -> p s t", t=DT), ACT.Copy) \
                        .then_inc(mark("proj_by_scalar", f"read proj{s0}", f"xp{s0}"), 1)
                else:
                    for event in y_free(s0 - 4):
                        act.wait_ge(*when(event))
                    A.activation(yb[:, s0 % 4, 0:TOK], b[:, 0:TOK], ACT.Copy) \
                        .then_inc(mark("proj_by_scalar", f"read proj{s0}", f"y{s0}"), 1)

        def gla_decays(m):
            o, n = TILES[m]
            t = f"gla{m} "
            act.wait_ge(*when(t + "logits"))
            lnexp(gA[0:n].rearrange("p a b -> p (a b)"), pm[4][0:n, :], n, "gla_by_scalar", t + "ln")

        def gla_sums(m):
            o, n = TILES[m]
            t = f"gla{m} "
            act.wait_ge(*when(t + "cum"))
            sc = 1.0 / TAU
            cum = pm[5][:, 0:HA * n].rearrange("p (h t) -> p h t", t=n)
            A.activation(Eb[:, :, 0:n], cum, ACT.Exp, scale=sc).then_inc(mark("gla_by_scalar", t + "eb"), 1)
            act.wait_ge(*when(t + "D"))
            A.activation(Em[:, :, 0:n], Ep[:, :, 0:n], ACT.Exp, scale=-sc)
            A.activation(El[:, :, 0:n], El[:, :, 0:n], ACT.Exp, scale=sc) \
                .then_inc(mark("gla_by_scalar", t + "em"), 1)
            act.wait_ge(*when(t + "em"))
            A.activation(Ep[:, :, 0:n], Ep[:, :, 0:n], ACT.Exp, scale=sc) \
                .then_inc(mark("gla_by_scalar", t + "exps"), 1)

        def gla_scores(m):
            o, n = TILES[m]
            t = f"gla{m} "
            act.wait_ge(*when(t + "ke transposed"))
            A.activation(keTa[0:n], pm[7][0:n, :].rearrange("p (h t) -> p h t", t=128), ACT.Copy) \
                .then_inc(mark("gla_by_scalar", t + "keT"), 1)

        def gla_out(m):
            o, n = TILES[m]
            t = f"gla{m} "
            if m == 0:
                for g in range(2):
                    act.wait_ge(*when(t + f"S{g} ready"))
                    A.activation(SA[:, 2 * g:2 * g + 2, :], pm[6 + g][:, :].rearrange("p (a b) -> p a b", b=256),
                                      ACT.Copy) \
                        .then_inc(mark("gla_by_scalar", t + f"S{g} read", *(["gla0 state"] if g else [])), 1)
            for g in range(2):
                act.wait_ge(*when(t + f"o{g} ready"))
                for hh in range(2):
                    h = 2 * g + hh
                    A.activation(oNa[0:n, 256 * h:256 * h + 256], pm[4 + g][0:n, 256 * hh:256 * hh + 256],
                                      ACT.Square, accum_out=ssum[0:n, h:h + 1]) \
                        .then_inc(mark("gla_by_scalar", *([t + "ss"] if h == HA - 1 else [])), 1)
            act.wait_ge(*when(t + "ss"))
            rstd(srs[0:n, 0:HA], ssum[0:n, 0:HA], 1.0 / DVA, "gla_by_scalar", t + "rstd", n=n)

        def gdn_scores(m):
            o, n = TILES[m]
            t = f"gdn{m} "
            HG = 4
            for g in range(2):
                act.wait_ge(*when(t + f"D{g}"))
                ee = E[0:n, HG * g:HG * g + HG, 0:n]
                A.activation(ee, ee, ACT.Exp).then_inc(mark("gdn_by_scalar", t + f"E{g}"), 1)

        def gdn_level(m, lv):
            o, n = TILES[m]
            t = f"gdn{m} "
            HG = 4
            if lv == 0:
                return
            for g in range(2):
                act.wait_ge(*when(t + f"Y{lv} {g} ready"))
                A.activation(Y[0:n, HG * g:HG * g + HG, 0:n],
                                  pm[4 + g][0:n, 0:HG * n].rearrange("p (h t) -> p h t", t=n), ACT.Copy) \
                    .then_inc(mark("gdn_by_scalar", t + f"Y{lv} {g}"), 1)

        def gdn_out(m):
            o, n = TILES[m]
            t = f"gdn{m} "
            HG = 4
            levels = LEVELS if m < 2 else 2
            act.wait_ge(*when(t + "o0"))
            act.wait_ge(*when(t + "o1"))
            A.activation(sqo[0:n], E[0:n], ACT.Square).then_inc(mark("gdn_by_scalar", t + "squares"), 1)
            act.wait_ge(*when(t + "ssum"))
            rstd(srs[0:n, :], ssum[0:n, :], 1.0 / DVB, "gdn_by_scalar", t + "rstd", n=n)

        def router():
            def token_major(m):
                n = TILES[m][1]
                for g in range(2):
                    act.wait_ge(*when(f"h2t{m}{g} ready"))
                    A.activation(h2t[0:n, m, 512 * g:512 * g + 512], rb(f"h2t{m}{g}")[0:n, :], ACT.Copy) \
                        .then_inc(mark("router_by_scalar", f"read h2t{m}{g}"), 1)

            act.wait_ge(*when("router parts ready"))
            for i in range(4):
                act.wait_ge(*when(f"stored {chunk_of[('sgdn', i)]}"))
            A.activation(rparts, rb("router parts")[:, 0:TOK], ACT.Copy) \
                .then_inc(mark("router_by_scalar", "read router parts"), 1)
            token_major(0)
            act.wait_ge(*when("gd"))
            A.activation(rs_["dd"], rs_["dd"], ACT.Exp).then_inc(mark("router_by_scalar", "gexp"), 1)
            token_major(1)
            act.wait_ge(*when("ed"))
            A.activation(rs_["p1"], rs_["p1"], ACT.Exp).then_inc(mark("router_by_scalar", "eexp"), 1)
            token_major(2)

        def expert_block(i, n):
            act.wait_ge(n["gathered"], 2 * i + 2)
            A.activation(hg[:, 4:8, :], pm[1][:, 0:4 * PAIR].rearrange("p (k s) -> p k s", s=PAIR), ACT.Copy) \
                .then_inc(n["gather_read1"], 1)
            s = sg2[0:PAIR]
            act.wait_ge(n["gate"], i + 1)
            A.activation(s, pm[2][0:PAIR, :], ACT.Abs).then_inc(n["softplus_step"], 1)
            act.wait_ge(n["softplus_step"], 2 * i + 1)
            A.activation(s, s, ACT.Exp, scale=-1.0).then_inc(n["softplus_step"], 1)
            act.wait_ge(n["softplus_step"], 2 * i + 2)
            A.activation(s, s, ACT.Ln, bias=one[0:PAIR]).then_inc(n["softplus"], 1)
            act.wait_ge(n["log_sigmoid"], i + 1)
            A.activation(s, s, ACT.Exp).then_inc(n["sigmoid"], 1)
            act.wait_ge(n["down"], 2 * i + 2)
            A.activation(yt[0:PAIR, 512:1024], pm[7][0:PAIR, :], ACT.Copy).then_inc(n["down_read1"], 1)

        def experts():
            with act.Fori(0, NE // 2) as i:
                expert_block(i, main_sems)
            act.wait_ge(*when("tables"))
            overflow(act, lambda j: expert_block(j, over_sems))

        def final():
            for d in range(KD):
                act.wait_ge(*when(f"x3 {d}"))
                A.activation(hT[:, d, :], xT[:, d, :], ACT.Square) \
                    .then_inc(mark("norm_by_scalar", f"square3 {d}"), 1)
            act.wait_ge(*when("norm3 ready"))
            act.wait_ge(*when("h2 7"))
            rstd(rsB, rb("norm3")[:, 0:TOK], 1.0 / D, "norm_by_scalar", "rstd3", mid_event="read norm3")
            for g in range(2):
                act.wait_ge(*when(f"y{g}1 ready"))
                A.activation(yrow[:, 1, 512 * g:512 * g + 512], rb(f"y{g}1")[:, :], ACT.Copy) \
                    .then_inc(mark("final_by_scalar", f"read y{g}1"), 1)

        run(locals())

    @block.gpsimd
    def _(pool):
        def head():
            pool.wait_ge(*when("x rows"))
            G.memset(ba, 0.0).then_inc(mark("cleared", "ba zero"), 1)
            G.memset(csT[:, KD * NC9:], 0.0).then_inc(mark("cleared", "c padding"), 1)
            G.memset(rtw[:, KD * 20:], 0.0).then_inc(mark("cleared", "router padding"), 1)
            G.memset(bcum, 0.0)
            G.memset(blast, 0.0).then_inc(mark("cleared", "bcum zero"), 1)
            G.memset(qbM, 0.0).then_inc(mark("cleared", "qbM zero"), 1)
            G.memset(xp, 0.0).then_inc(mark("cleared", "xp zero"), 1)
            G.memset(raT[0:32, :], 1.0).then_inc(mark("cleared", "raT ones"), 1)

        def step(s):
            s1 = s - 1
            if 0 <= s1 < NPROJ and PROJ[s1][0] == "cv":
                i = PROJ[s1][1]
                pool.wait_ge(*when(f"xp{s1}"))
                x = xp[:, s1 % 2]
                G.tensor_copy(ccT[:, i, 0:3], x[:, SEQ:SEQ + 3])
                G.tensor_copy(ccT[:, i, 3:27].rearrange("p (s t) -> p s t", t=3),
                                   x[:, SAMP0:XPW].rearrange("p (s t) -> p s t", t=7)[:, :, 4:7]) \
                    .then_inc(mark("conv_tails", f"cc{i}"), 1)

        def gla_out(m):
            if m == 2:
                for s in range(NSEQ):
                    pool.wait_ge(*when("gla2 keT"))
                    if s >= 2:
                        pool.wait_ge(*when(f"gla state product {s - 2} 1"))
                    G.tensor_scalar(kem1[0:32, s % 2, :], keTa[0:32].rearrange("p a b -> p (a b)"),
                                         const("seq")[0:32, s:s + 1], None, ALU.mult) \
                        .then_inc(mark("masked_keys", f"kem1 {s}"), 1)

        def gdn_scores(m):
            if m == 2:
                pool.wait_ge(*when("small outputs stored"))
                pool.wait_ge(*when("cvo5 ready"))
                pool.wait_ge(*when("tap3 39"))
                pool.wait_ge(*when("ba ready"))
                pool.wait_ge(*when("gdn1 qS1"))
                G.memset(kM, 0.0).then_inc(mark("cleared", "kM zero"), 1)
                G.memset(qM[0], 0.0)
                G.memset(qM[1], 0.0).then_inc(mark("cleared", "qM zero"), 1)

        def gdn_out(m):
            if m == 2:
                for s in range(NSEQ):
                    pool.wait_ge(*when("gdn2 ke0"))
                    pool.wait_ge(*when("gdn2 ke1"))
                    pool.wait_ge(*when("gdn2 y0"))
                    pool.wait_ge(*when("gdn2 y1"))
                    if s >= 2:
                        pool.wait_ge(*when(f"gdn state product {s - 2} 1"))
                    G.tensor_scalar(kem2[0:32, s % 2, :], ke[0:32].rearrange("p a b -> p (a b)"),
                                         const("seq")[0:32, s:s + 1], None, ALU.mult) \
                        .then_inc(mark("masked_keys", f"kem2 {s}"), 1)

        def merge():
            for d in range(KD):
                pool.wait_ge(*when(f"ma {d}"))
                pool.wait_ge(*when(f"mb {d}"))
                G.tensor_tensor(GA[:, d, :], GA[:, d, :], GB[:, d, :], ALU.add) \
                    .then_inc(mark("merged", f"merged {d}"), 1)

        def router():
            pool.wait_ge(*when("merged 7"))
            pool.wait_ge(*when("wout7 ready"))
            for i in range(4):
                pool.wait_ge(*when(f"stored {chunk_of[('sgdn', i)]}"))
            G.memset(rank, 0.0)
            G.memset(comb, 0.0)
            G.memset(rt, 0.0).then_inc(mark("cleared", "rt zero"), 1)
            G.memset(acc, 0.0).then_inc(main_sems["added"], 1)
            G.memset(combJ, 0.0).then_inc(over_sems["added"], 1)

        run(locals())

    @block.sync
    def _(sp):
        n = [0]

        def load(dst, src, event, kind=None):
            kind = kind or f"loaded_{event.replace(' ', '_')}"
            sp.dma_start(dst, src).then_inc(mark(kind, event, by=16), 16)

        load(cst, I["const"], "consts")
        load(crow[0:NC9, :], I["cc"], "c rows")
        for i, (k, (r, c)) in enumerate(VEC.items()):
            src = {"b_ada": I["b_ada"], "norm1": I["norm1_w"], "norm2": I["norm2_w"], "final": I["final_norm_w"],
                   "gla_norm": I["gla_norm_w"], "gdn_norm": I["gdn_norm_w"]}[k]
            sp.dma_start(vrow[r:r + c, :], src.rearrange("(n p) -> n p", p=P)) \
                .then_inc(mark("loaded_vectors", by=16), 16)
        sp.dma_start(cvrow[0:96, :], I["w_conv"].rearrange("t (n p) -> (t n) p", p=P)) \
            .then_inc(mark("loaded_vectors", "vec rows", by=16), 16)
        sp.dma_start(xr[:, 0:2, :], I["x_prompt"].rearrange("(m p) d -> p m d", p=P)) \
            .then_inc(mark("loaded_x", by=16), 16)
        sp.dma_start(xr[0:32, 2, :], I["x_sample"]).then_inc(mark("loaded_x", "x rows", by=16), 16)
        load(cbrow[0:24, :], I["state_conv"], "cb rows")
        sp.dma_start(wsm[:, :, 0:RANK], I["w_in"][:, 3072:3088].rearrange("(k p) n -> p k n", p=P)) \
            .then_inc(mark("loaded_small", by=16), 16)
        sp.dma_start(wsm[:, :, 16:32], I["w_in"][:, 7184:7200].rearrange("(k p) n -> p k n", p=P)) \
            .then_inc(mark("loaded_small", "small weights", by=16), 16)
        sp.dma_start(wa2[0:RANK, :], I["w_gla_a2"]).then_inc(mark("loaded_wa2", by=16), 16)
        sp.dma_start(wa2[RANK:RANK + 1, :], I["b_gla_a"].rearrange("(a n) -> a n", a=1)) \
            .then_inc(mark("loaded_wa2", "wa2", by=16), 16)
        sp.dma_start(adt[:, 0, :], I["gdn_A_log"].rearrange("(a n) -> a n", a=1).to_broadcast([P, HB])) \
            .then_inc(mark("loaded_adt", by=16), 16)
        sp.dma_start(adt[:, 1, :], I["gdn_dt_bias"].rearrange("(a n) -> a n", a=1).to_broadcast([P, HB])) \
            .then_inc(mark("loaded_adt", "adt", by=16), 16)
        sp.dma_start(rtw[:, 0:KD * 20].rearrange("p (k n) -> p k n", n=20)[:, :, 0:4], I["w_group_router"].rearrange("(k p) n -> p k n", p=P)) \
            .then_inc(mark("loaded_router", by=16), 16)
        sp.dma_start(rtw[:, 0:KD * 20].rearrange("p (k n) -> p k n", n=20)[:, :, 4:20], I["w_expert_router"].rearrange("(k p) n -> p k n", p=P)) \
            .then_inc(mark("loaded_router", "router weights", by=16), 16)
        sp.dma_start(rtb[:, 0:4], I["b_group_router"].rearrange("(a n) -> a n", a=1).to_broadcast([P, 4])) \
            .then_inc(mark("loaded_rtb", by=16), 16)
        sp.dma_start(rtb[:, 4:20], I["b_expert_router"].rearrange("(a n) -> a n", a=1).to_broadcast([P, 16])) \
            .then_inc(mark("loaded_rtb", "router bias", by=16), 16)
        outs = []
        def release(n):
            name = chunks[n][0]
            if name[0] not in ("sgla", "sgdn"):
                sp.wait_ge(*when(used(name)))
                return
            c = name[1]
            for s in (2 * c, 2 * c + 1):
                for g in range(2):
                    sp.wait_ge(*when(f"{name[0][1:]} state {s} {g}"))
            if name[0] == "sgla":
                dst, src = O["gla_s"][2 * c:2 * c + 2].rearrange("s h k v -> k (s h) v"), slot(name)
            else:
                dst = O["gdn_s"][2 * c:2 * c + 2].rearrange("s (h a) k v -> k (s h) a v", a=2)
                src = slot(name).rearrange("p k (a v) -> p k a v", a=2)
            sp.dma_start(dst, src).then_inc(mark(f"stored_slot{n % RING}", f"stored {n}", by=16), 16)
            sp.wait_ge(*when(f"stored {n}"))

        for n, (name, src) in enumerate(chunks):
            if n >= RING:
                release(n - RING)
            if name == ("sgdn", 0):
                for g in range(6):
                    sp.wait_ge(*when(f"read cvo{g}"))
                sp.dma_start(O["conv_p"], newconv[0:3, :]).then_inc(mark("stored", by=16), 16)
                sp.dma_start(O["conv_s"], newconv[3:27, :]).then_inc(mark("stored", by=16), 16)
                sp.dma_start(O["gla_p"].rearrange("h k v -> k h v"), SA).then_inc(mark("stored", by=16), 16)
                sp.wait_ge(*when("gdn1 state1"))
                sp.dma_start(O["gdn_p"].rearrange("h k v -> k h v"), SB) \
                    .then_inc(mark("stored", "small outputs stored", by=16), 16)
            d_ = slot(name)
            if name[0] == "sgdn":
                d_ = d_.rearrange("p k (a v) -> p k a v", a=2)
            sp.dma_start(d_, src).then_inc(mark(f"loaded_slot{n % RING}", loaded(name), by=16), 16)
        for n in range(len(chunks) - RING, len(chunks)):
            if chunks[n][0][0] == "sgdn":
                release(n)

        wts = [I[k].rearrange("g e a b -> (g e) a b") for k in ("w_exp_gate", "w_exp_up", "w_exp_down")]

        def load_expert(kind, experts, n, sems):
            sp.dma_start(EW[:, kind, 0:n, :].rearrange("p a (k n) -> p (a k) n", k=4 if kind == 2 else KD),
                         wts[kind][experts].rearrange("a (k p) n -> p (a k) n", p=P)).then_inc(sems[kind], 16)

        sp.wait_ge(*when("gdn2 oT1"))
        sp.wait_ge(*when("gdn2 oT1 ready"))
        sp.wait_ge(*when("small outputs stored"))
        sp.wait_ge(*when(f"act{NPROJ - 1}"))
        for kind in range(3):
            load_expert(kind, slice(0, 2), 2, expert_loaded)
        with sp.Fori(1, NE // 2) as i:
            pair = bass.ds(2 * i, 2)
            sp.wait_ge(main_sems["gate"], i)
            load_expert(0, pair, 2, expert_loaded)
            sp.wait_ge(main_sems["up"], i)
            load_expert(1, pair, 2, expert_loaded)
            sp.wait_ge(main_sems["down"], 2 * i)
            load_expert(2, pair, 2, expert_loaded)

        def over_load(j):
            sp.wait_ge(over_sems["dispatch"], j + 1)
            e = bass.ds(sp.value_load(tab[0:1, bass.ds(j + 1, 1)], min_val=0, max_val=NE - 1), 1)
            for kind in range(3):
                load_expert(kind, e, 1, over_loaded)

        sp.wait_ge(*when("tables"))
        sp.wait_ge(main_sems["down"], NE)
        overflow(sp, over_load)
        for g in range(2):
            for m in range(3):
                sp.wait_ge(*when(f"read y{g}{m}"))
            cs = slice(512 * g, 512 * g + 512)
            sp.dma_start(O["y_p"].rearrange("(m p) d -> p m d", p=P)[:, :, cs], yrow[:, 0:2, cs]) \
                .then_inc(mark("stored", by=16), 16)
            sp.dma_start(O["y_s"][:, cs], yrow[0:32, 2, cs]) \
                .then_inc(mark("stored", f"all stored{g}", by=16), 16)
        sp.wait_ge(*when("all stored1"))

    return S.marks


_SHAPES = {
    "y_p": (SEQ, D), "y_s": (NSEQ * DT, D), "gla_p": (HA, DKA, DVA), "gdn_p": (HB, DKB, DVB), "conv_p": (3, 3072),
    "gla_s": (NSEQ, HA, DKA, DVA), "gdn_s": (NSEQ, HB, DKB, DVB), "conv_s": (NSEQ * 3, 3072),
}
_NAMES = ("w_ada", "b_ada", "norm1_w", "w_in", "w_gla_a2", "b_gla_a", "gla_norm_w", "w_conv", "gdn_A_log",
          "gdn_dt_bias", "gdn_norm_w", "w_out", "norm2_w", "w_group_router", "b_group_router", "w_expert_router",
          "b_expert_router", "w_exp_gate", "w_exp_up", "w_exp_down")


def lay_out(inputs):
    a = {k: np.ascontiguousarray(np.asarray(inputs[k])[0]) for k in _NAMES}
    a["final_norm_w"] = np.asarray(inputs["final_norm_w"])
    a["x_prompt"] = np.asarray(inputs["x_prompt"]).reshape(SEQ, D)
    a["x_sample"] = np.asarray(inputs["x_sample"]).reshape(NSEQ * DT, D)
    a["cc"] = np.concatenate([np.asarray(inputs["c_prompt"]), np.asarray(inputs["c_sample"])], axis=0)
    a["state_gla"] = np.asarray(inputs["state_gla"])[0]
    a["state_gdn"] = np.asarray(inputs["state_gdn"])[0]
    a["state_conv"] = np.asarray(inputs["state_conv"]).reshape(NSEQ * 3, 3072)
    a["const"] = CONST
    return {k: np.ascontiguousarray(v) for k, v in a.items()}


def kernel(**inputs):
    import concourse.bacc as bacc
    from concourse.bass_utils import run_bass_kernel_spmd

    arrays = lay_out(inputs)
    counts = None
    for _ in range(2):
        nc = bacc.Bacc("TRN2", target_bir_lowering=False, num_devices=1)
        ins = {k: nc.dram_tensor("in_" + k, v.shape, F32, kind="ExternalInput").ap() for k, v in arrays.items()}
        outs = {k: nc.dram_tensor("out_" + k, s, F32, kind="ExternalOutput").ap() for k, s in _SHAPES.items()}
        counts = program(nc, ins, outs, counts)
    r = run_bass_kernel_spmd(nc, [{"in_" + k: v for k, v in arrays.items()}], core_ids=[0]).results[0]
    o = {k: r["out_" + k] for k in _SHAPES}
    return (o["y_p"].reshape(1, SEQ, D), o["y_s"].reshape(NSEQ, DT, D),
            o["gla_p"].reshape(1, 1, HA, DKA, DVA), o["gdn_p"].reshape(1, 1, HB, DKB, DVB),
            o["conv_p"].reshape(1, 1, 3, 3072), o["gla_s"].reshape(1, NSEQ, HA, DKA, DVA),
            o["gdn_s"].reshape(1, NSEQ, HB, DKB, DVB), o["conv_s"].reshape(1, NSEQ, 3, 3072))
```
